# Optimizing a Trainium2 kernel written in Bass

```python
import jax, jax.numpy as jnp
from jax import lax
import numpy as np

D_MODEL = 1024
BATCH = 1
SEQ = 256
DEPTH = 2
DEC_BATCH = 8
DEC_SEQ = 4
PAST_LEN = 2048
PAGE_SIZE = 128

N_RWKV_LAYERS = (DEPTH + 1) // 2
N_GLA_LAYERS = DEPTH // 2

RWKV_HEAD = 64
RWKV_H = D_MODEL // RWKV_HEAD
RWKV_DECAY_LORA = 64
RWKV_A_LORA = 64
RWKV_GATE_LORA = 128
RWKV_LNX_EPS = 64e-5

GLA_H = 4
GLA_DK = D_MODEL // 2 // GLA_H
GLA_DV = D_MODEL // GLA_H
GLA_ALPHA_LORA = 16
GLA_TAU = 16.0
GLA_CHUNK = 16
GLA_SPLITS = (GLA_H * GLA_DK, 2 * GLA_H * GLA_DK, 2 * GLA_H * GLA_DK + GLA_H * GLA_DV,
              2 * GLA_H * GLA_DK + GLA_H * GLA_DV + D_MODEL)
GLA_IN = GLA_SPLITS[-1] + GLA_ALPHA_LORA

PEER_HEADS = 8
PEER_NKEYS = 128
PEER_N = PEER_NKEYS * PEER_NKEYS
PEER_QDIM = 256
PEER_HALF = PEER_QDIM // 2
PEER_TOPK = 16
PEER_BLOCK = 256

NORM_EPS = 1e-6

kernel_name = 'rwkv7_gla_peer_adaln_hybrid_step'

def _rmsnorm(x, g):
    xf = x.astype(jnp.float32)
    y = xf * lax.rsqrt(jnp.mean(xf * xf, axis=-1, keepdims=True) + NORM_EPS)
    return (y * g.astype(jnp.float32)).astype(x.dtype)

def _rwkv7_scan(r, w, k, v, a, b, S0):
    f32 = jnp.float32
    xs = tuple(jnp.moveaxis(t.astype(f32), 1, 0) for t in (r, w, k, v, a, b))

    def step(S, inp):
        rt, wt, kt, vt, at, bt = inp
        sa = jnp.einsum('bhvk,bhk->bhv', S, at)
        S = S * wt[:, :, None, :] + sa[..., None] * bt[:, :, None, :] + vt[..., None] * kt[:, :, None, :]
        yt = jnp.einsum('bhvk,bhk->bhv', S, rt)
        return S, yt

    S, y = lax.scan(step, S0.astype(f32), xs)
    return jnp.moveaxis(y, 0, 1), S

def _rwkv7_mix(h, shift0, S0, mu, w_rkv, w0, w1, w2, a0, a1, a2, g1, g2,
               k_k, k_a, r_k, lnx_w, lnx_b, w_o):
    B, T, D = h.shape
    f32 = jnp.float32
    prev = jnp.concatenate([shift0[:, None, :].astype(h.dtype), h[:, :-1]], axis=1)
    xx = prev - h
    mix = h[None] + xx[None] * mu[:, None, None, :]
    r, k, v = jnp.einsum('cbtd,cde->cbte', mix[:3], w_rkv)
    xw, xa, xg = mix[3], mix[4], mix[5]
    wlog = -jax.nn.softplus(-(w0 + jnp.tanh(xw @ w1) @ w2).astype(f32)) - 0.5
    decay = jnp.exp(-jnp.exp(wlog))
    a = jax.nn.sigmoid((a0 + (xa @ a1) @ a2).astype(f32))
    g = jax.nn.sigmoid(xg @ g1) @ g2
    heads = lambda t: t.reshape(B, T, RWKV_H, RWKV_HEAD)
    kk = heads((k * k_k).astype(f32))
    kk = kk / jnp.maximum(jnp.sqrt(jnp.sum(kk * kk, axis=-1, keepdims=True)), 1e-12)
    kf = k.astype(f32) * (1.0 + (a - 1.0) * k_a.astype(f32))
    rh, kh, vh, ah = heads(r.astype(f32)), heads(kf), heads(v.astype(f32)), heads(a)
    y, S = _rwkv7_scan(rh, heads(decay), kh, vh, -kk, kk * ah, S0)
    mean = jnp.mean(y, axis=-1, keepdims=True)
    var = jnp.mean(jnp.square(y - mean), axis=-1, keepdims=True)
    y = ((y - mean) * lax.rsqrt(var + RWKV_LNX_EPS)).reshape(B, T, D)
    y = y * lnx_w.astype(f32) + lnx_b.astype(f32)
    bonus = jnp.sum(rh * kh * r_k.astype(f32), axis=-1, keepdims=True) * vh
    y = (y + bonus.reshape(B, T, D)).astype(h.dtype)
    out = (y * g) @ w_o
    return out, h[:, -1], S.astype(S0.dtype)

def _gla_chunked(q, k, v, log_alpha, S0):
    f32 = jnp.float32
    B, H, T, _ = q.shape
    C = GLA_CHUNK
    nc = -(-T // C)
    pad = nc * C - T

    def chunks(t):
        t = jnp.pad(t.astype(f32), ((0, 0), (0, 0), (0, pad), (0, 0)))
        return jnp.moveaxis(t.reshape(B, H, nc, C, t.shape[-1]), 2, 0)

    xs = (chunks(q), chunks(k), chunks(v), chunks(log_alpha))
    causal = jnp.tril(jnp.ones((C, C), dtype=bool))

    def step(S, inp):
        qc, kc, vc, lc = inp
        bcum = jnp.cumsum(lc, axis=2)
        diff = bcum[:, :, :, None, :] - bcum[:, :, None, :, :]
        dec = jnp.exp(jnp.where(causal[:, :, None], diff, -jnp.inf))
        A = jnp.einsum('bhid,bhjd,bhijd->bhij', qc, kc, dec)
        o = jnp.einsum('bhij,bhjv->bhiv', A, vc) + jnp.einsum('bhid,bhdv->bhiv', qc * jnp.exp(bcum), S)
        blast = bcum[:, :, -1:, :]
        S = jnp.exp(blast[:, :, 0, :])[..., None] * S + jnp.einsum('bhjd,bhjv->bhdv', kc * jnp.exp(blast - bcum), vc)
        return S, o

    S, o = lax.scan(step, S0.astype(f32), xs)
    o = jnp.moveaxis(o, 0, 2).reshape(B, H, nc * C, -1)[:, :, :T]
    return o, S

def _gla_mix(h, S0, w_in, wa2, ba, gnorm, w_o):
    B, T, D = h.shape
    p = h @ w_in
    q, k, v, r, al = jnp.split(p, GLA_SPLITS, axis=-1)
    log_alpha = jax.nn.log_sigmoid((al @ wa2 + ba).astype(jnp.float32)) / GLA_TAU
    hd = lambda t, d: jnp.moveaxis(t.reshape(B, T, GLA_H, d), 2, 1)
    o, S = _gla_chunked(hd(q, GLA_DK) * (GLA_DK ** -0.5), hd(k, GLA_DK), hd(v, GLA_DV),
                        hd(log_alpha, GLA_DK), S0)
    o = _rmsnorm(jnp.moveaxis(o, 1, 2), gnorm).reshape(B, T, GLA_H * GLA_DV)
    out = (o.astype(h.dtype) * jax.nn.silu(r)) @ w_o
    return out, S.astype(S0.dtype)

def _peer(h, wq, subkeys, u, v):
    B, T, D = h.shape
    n = B * T
    nb = -(-n // PEER_BLOCK)
    xb = jnp.pad(h.reshape(n, D), ((0, nb * PEER_BLOCK - n), (0, 0))).reshape(nb, PEER_BLOCK, D)
    f32 = jnp.float32

    def block(xt):
        q = (xt @ wq).reshape(PEER_BLOCK, PEER_HEADS, 2, PEER_HALF).astype(f32)
        s = jnp.einsum('thpk,hpnk->thpn', q, subkeys.astype(f32))
        s1, i1 = lax.top_k(s[:, :, 0], PEER_TOPK)
        s2, i2 = lax.top_k(s[:, :, 1], PEER_TOPK)
        cand = (s1[..., :, None] + s2[..., None, :]).reshape(PEER_BLOCK, PEER_HEADS, PEER_TOPK * PEER_TOPK)
        sc, pos = lax.top_k(cand, PEER_TOPK)
        expert = (jnp.take_along_axis(i1, pos // PEER_TOPK, axis=-1) * PEER_NKEYS
                  + jnp.take_along_axis(i2, pos % PEER_TOPK, axis=-1))
        gate = jax.nn.softmax(sc, axis=-1)
        ue = jnp.take(u, expert, axis=0)
        act = jax.nn.gelu(jnp.einsum('thed,td->the', ue, xt).astype(f32), approximate=False)
        ve = jnp.take(v, expert, axis=0)
        return jnp.einsum('the,thed->td', (gate * act).astype(xt.dtype), ve)

    y = lax.map(block, xb).reshape(nb * PEER_BLOCK, D)[:n]
    return y.reshape(B, T, D)

def _trunk(x, c, rwkv_S, rwkv_shift, gla_S, P):
    new_rS, new_rshift, new_gS = [], [], []
    for li in range(DEPTH):
        mod = jax.nn.silu(c) @ P['ada_w'][li] + P['ada_b'][li]
        sh1, sc1, gt1, sh2, sc2, gt2 = jnp.split(mod[:, None, :], 6, axis=-1)
        hm = _rmsnorm(x, P['norm1_g'][li]) * (1.0 + sc1) + sh1
        j = li // 2
        if li % 2 == 0:
            out, shf, S = _rwkv7_mix(hm, rwkv_shift[j], rwkv_S[j], P['rw_mu'][j], P['rw_w_rkv'][j],
                                     P['rw_w0'][j], P['rw_w1'][j], P['rw_w2'][j],
                                     P['rw_a0'][j], P['rw_a1'][j], P['rw_a2'][j],
                                     P['rw_g1'][j], P['rw_g2'][j], P['rw_kk'][j], P['rw_ka'][j],
                                     P['rw_rk'][j], P['rw_lnx_w'][j], P['rw_lnx_b'][j], P['rw_wo'][j])
            new_rS.append(S)
            new_rshift.append(shf)
        else:
            out, S = _gla_mix(hm, gla_S[j], P['gla_w_in'][j], P['gla_wa2'][j], P['gla_ba'][j],
                              P['gla_gnorm'][j], P['gla_wo'][j])
            new_gS.append(S)
        x = x + gt1 * out
        hc = _rmsnorm(x, P['norm2_g'][li]) * (1.0 + sc2) + sh2
        x = x + gt2 * _peer(hc, P['peer_wq'][li], P['peer_subkeys'][li], P['peer_u'][li], P['peer_v'][li])
    y = _rmsnorm(x, P['final_g'])
    return y, jnp.stack(new_rS), jnp.stack(new_rshift), jnp.stack(new_gS)

def setup_inputs(seed: int = 0) -> dict:
    key = jax.random.key(seed)
    ks = iter(jax.random.split(key, 48))
    nrm = lambda shape, s: jax.random.normal(next(ks), shape, jnp.float32) * s
    D = D_MODEL
    R, G = N_RWKV_LAYERS, N_GLA_LAYERS
    inp = {}
    inp['x_prompt'] = nrm((BATCH, SEQ, D), 1.0)
    inp['x_sample'] = nrm((DEC_BATCH, DEC_SEQ, D), 1.0)
    inp['state_rwkv_S'] = nrm((R, DEC_BATCH, RWKV_H, RWKV_HEAD, RWKV_HEAD), 0.5)
    inp['state_rwkv_shift'] = nrm((R, DEC_BATCH, D), 1.0)
    inp['state_gla_S'] = nrm((G, DEC_BATCH, GLA_H, GLA_DK, GLA_DV), 0.5)
    inp['c_prompt'] = nrm((BATCH, D), 1.0)
    inp['c_sample'] = nrm((DEC_BATCH, D), 1.0)
    inp['ada_w'] = nrm((DEPTH, D, 6 * D), 0.5 * D ** -0.5)
    inp['ada_b'] = nrm((DEPTH, 6 * D), 0.02)
    inp['norm1_g'] = 1.0 + nrm((DEPTH, D), 0.02)
    inp['norm2_g'] = 1.0 + nrm((DEPTH, D), 0.02)
    inp['final_g'] = 1.0 + nrm((D,), 0.02)
    inp['rw_mu'] = jax.random.uniform(next(ks), (R, 6, D), jnp.float32)
    inp['rw_w_rkv'] = nrm((R, 3, D, D), D ** -0.5)
    inp['rw_w0'] = jax.random.uniform(next(ks), (R, D), jnp.float32, -6.0, -1.0)
    inp['rw_w1'] = nrm((R, D, RWKV_DECAY_LORA), D ** -0.5)
    inp['rw_w2'] = nrm((R, RWKV_DECAY_LORA, D), 0.1 * RWKV_DECAY_LORA ** -0.5)
    inp['rw_a0'] = nrm((R, D), 0.1)
    inp['rw_a1'] = nrm((R, D, RWKV_A_LORA), D ** -0.5)
    inp['rw_a2'] = nrm((R, RWKV_A_LORA, D), 0.5 * RWKV_A_LORA ** -0.5)
    inp['rw_g1'] = nrm((R, D, RWKV_GATE_LORA), D ** -0.5)
    inp['rw_g2'] = nrm((R, RWKV_GATE_LORA, D), RWKV_GATE_LORA ** -0.5)
    inp['rw_kk'] = 0.85 + nrm((R, D), 0.02)
    inp['rw_ka'] = 1.0 + nrm((R, D), 0.02)
    inp['rw_rk'] = nrm((R, RWKV_H, RWKV_HEAD), 0.1)
    inp['rw_lnx_w'] = 1.0 + nrm((R, D), 0.02)
    inp['rw_lnx_b'] = nrm((R, D), 0.01)
    inp['rw_wo'] = nrm((R, D, D), D ** -0.5)
    inp['gla_w_in'] = nrm((G, D, GLA_IN), D ** -0.5)
    inp['gla_wa2'] = nrm((G, GLA_ALPHA_LORA, GLA_H * GLA_DK), GLA_ALPHA_LORA ** -0.5)
    inp['gla_ba'] = 2.0 + nrm((G, GLA_H * GLA_DK), 0.5)
    inp['gla_gnorm'] = 1.0 + nrm((G, GLA_DV), 0.02)
    inp['gla_wo'] = nrm((G, GLA_H * GLA_DV, D), (GLA_H * GLA_DV) ** -0.5)
    inp['peer_wq'] = nrm((DEPTH, D, PEER_HEADS * PEER_QDIM), D ** -0.5)
    inp['peer_subkeys'] = nrm((DEPTH, PEER_HEADS, 2, PEER_NKEYS, PEER_HALF), PEER_HALF ** -0.5)
    inp['peer_u'] = nrm((DEPTH, PEER_N, D), D ** -0.5)
    inp['peer_v'] = nrm((DEPTH, PEER_N, D), 0.25)
    return inp

def reference(x_prompt, x_sample, state_rwkv_S, state_rwkv_shift, state_gla_S, c_prompt, c_sample,
              ada_w, ada_b, norm1_g, norm2_g, final_g,
              rw_mu, rw_w_rkv, rw_w0, rw_w1, rw_w2, rw_a0, rw_a1, rw_a2, rw_g1, rw_g2,
              rw_kk, rw_ka, rw_rk, rw_lnx_w, rw_lnx_b, rw_wo,
              gla_w_in, gla_wa2, gla_ba, gla_gnorm, gla_wo,
              peer_wq, peer_subkeys, peer_u, peer_v):
    P = dict(ada_w=ada_w, ada_b=ada_b, norm1_g=norm1_g, norm2_g=norm2_g, final_g=final_g,
             rw_mu=rw_mu, rw_w_rkv=rw_w_rkv, rw_w0=rw_w0, rw_w1=rw_w1, rw_w2=rw_w2,
             rw_a0=rw_a0, rw_a1=rw_a1, rw_a2=rw_a2, rw_g1=rw_g1, rw_g2=rw_g2,
             rw_kk=rw_kk, rw_ka=rw_ka, rw_rk=rw_rk, rw_lnx_w=rw_lnx_w, rw_lnx_b=rw_lnx_b, rw_wo=rw_wo,
             gla_w_in=gla_w_in, gla_wa2=gla_wa2, gla_ba=gla_ba, gla_gnorm=gla_gnorm, gla_wo=gla_wo,
             peer_wq=peer_wq, peer_subkeys=peer_subkeys, peer_u=peer_u, peer_v=peer_v)
    B = x_prompt.shape[0]
    dt = x_prompt.dtype
    rS0 = jnp.zeros((N_RWKV_LAYERS, B, RWKV_H, RWKV_HEAD, RWKV_HEAD), dt)
    rsh0 = jnp.zeros((N_RWKV_LAYERS, B, D_MODEL), dt)
    gS0 = jnp.zeros((N_GLA_LAYERS, B, GLA_H, GLA_DK, GLA_DV), dt)
    y_prompt, rS_p, rsh_p, gS_p = _trunk(x_prompt, c_prompt, rS0, rsh0, gS0, P)
    y_sample, rS_s, rsh_s, gS_s = _trunk(x_sample, c_sample, state_rwkv_S, state_rwkv_shift, state_gla_S, P)
    return (y_prompt, y_sample, rS_p, rsh_p, gS_p, rS_s, rsh_s, gS_s)


_drawn_inputs = setup_inputs


def setup_inputs(seed=0):
    import zlib

    import numpy as np

    out = dict(_drawn_inputs(seed))
    spreads = {}
    factors = {'norm2_g': 6.139,
     'final_g': 7.794,
     'rw_w1': 5.985,
     'rw_w2': 6.128,
     'rw_lnx_w': 8.0,
     'rw_lnx_b': 8.0,
     'gla_gnorm': 22.322}
    for name, (base, spread) in spreads.items():
        noise = np.random.default_rng([zlib.crc32(name.encode()), seed]).standard_normal(out[name].shape)
        drawn = base * np.exp(spread * noise) if base else spread * noise
        out[name] = __import__('jax').numpy.asarray(drawn.astype(out[name].dtype))
    for name, factor in factors.items():
        out[name] = (out[name] * factor).astype(out[name].dtype)
    return out
```

```python
from contextlib import ExitStack

import concourse.bass as bass
from concourse import mybir

F32 = mybir.dt.float32
I32 = mybir.dt.int32
U32 = mybir.dt.uint32
ALU = mybir.AluOpType
ACT = mybir.ActivationFunctionType
AXX = mybir.AxisListType.X

P = 128
D = 1024
KD = D // P
NT = 3
TOK = NT * P
SAMPLE = 2
DEC_B, DEC_T = 8, 4
COPIES = P // (DEC_B * DEC_T)
RH, RK = 16, 64
HALF_H = RH // 2
PAIRS = HALF_H // 2
GH, GK, GV = 4, 128, 256
TAU = 16.0
PH, NKEYS, TOPK = 8, 128, 16
HP = 2 * PH
EPS = 1e-6
LNX_EPS = 64e-5
DECAY_C = 0.6065306597126334
LOWEST = -3.0e38
WBUF = 3
VBUF = 3
GRP, NGRP = 4, 4
RING = GRP * NGRP
SHORT = P // COPIES
SEGMENTS = (
    (P, (0, 0), None, False),
    (32, None, (0, 0), False),
    (P - 32, (1, 0), (0, 32), True),
    (32, (1, P - 32), None, False),
    (32, None, (1, 0), False),
    (SHORT, (SAMPLE, 0), (1, 32), True),
    (P - 32 - SHORT, None, (1, 32 + SHORT), False),
    (SHORT, None, (SAMPLE, 0), False),
)


def experts_of(t):
    return SHORT if t == SAMPLE else P


def groups_of(side, both):
    return range(2 * side, 2 * side + 2) if both else range(NGRP)


class Waits:

    def __init__(self, eng):
        self.eng, self.n = eng, {}

    def take(self, sem, k=1):
        self.n[sem.name] = self.n.get(sem.name, 0) + k
        self.eng.wait_ge(sem, self.n[sem.name])


def program(nc, a, outs):
    (y_p, y_s, S_p, sh_p, G_p, S_s, sh_s, G_s) = outs
    with ExitStack() as ctx:
        def sb(name, shape, dt=F32):
            return ctx.enter_context(nc.sbuf_tensor(name, shape, dt))

        def sem(name):
            return ctx.enter_context(nc.semaphore(name))

        mod_d = nc.dram_tensor("mod_d", (2, 6, 9, D), F32, kind="Internal").ap()
        rkv_d = nc.dram_tensor("rkv_d", (3, NT, P, D), F32, kind="Internal").ap()

        x = sb("x", [P, NT, D])
        hc = sb("hc", [P, NT, D])
        hT = sb("hT", [P, KD, TOK])
        wring = sb("wring", [P, WBUF, KD, 512])
        vring = sb("vring", [P, VBUF, D])
        arena = sb("arena", [P, 23680])
        ident = sb("ident", [P, P])
        zeros = sb("zeros", [P, P])
        le = sb("le", [P, P])
        le4 = sb("le4", [P, P])
        lt = sb("lt", [P, P])
        lt4 = sb("lt4", [P, P])
        cum_mid = sb("cum_mid", [P, P])
        low0 = sb("low0", [P, P])
        rep32 = sb("rep32", [P, P])
        lev = sb("lev", [P, 7, P])
        half_ind = sb("half_ind", [P, 2])
        seq_ind = sb("seq_ind", [P, DEC_B])
        iota16 = sb("iota16", [P, TOPK])
        cT = sb("cT", [P, KD * 9])
        muT = sb("muT", [P, 48])
        shiftT = sb("shiftT", [P, KD * DEC_B])
        rstd = sb("rstd", [P, 4])
        s16 = sb("s16", [P, 2, RH])
        bonus = sb("bonus", [P, RH])
        pcs = sb("pcs", [P, KD, DEC_B])
        stateT = sb("stateT", [P, KD, RK])
        st_in = sb("st_in", [P, PAIRS, RK])
        acts = sb("acts", [P, 2, P])
        act16 = sb("act16", [P, RING])
        idx_grp = sb("idx_grp", [P, RING], U32)

        def U(i, n=1):
            return arena[:, i * D:(i + n) * D]

        def W(off, n):
            return arena[:, off:off + n]

        def heads(ap, h, w):
            return ap.rearrange("p (h w) -> p h w", h=h)

        psv = ctx.enter_context(nc.psum_tensor("psv", [P, 2, D], F32))
        psa = ctx.enter_context(nc.psum_tensor("psa", [P, 2, D], F32))

        pool_consts = sem("pool_consts")
        consts_built = sem("consts_built")
        small_loaded = sem("small_loaded")
        x_loaded = sem("x_loaded")
        psum_for_vector = sem("psum_for_vector")
        psum_for_scalar = sem("psum_for_scalar")
        vector_drained = sem("vector_drained")
        scalar_drained = sem("scalar_drained")
        vector_step = sem("vector_step")
        scalar_step = sem("scalar_step")
        operand_written = sem("operand_written")
        vector_result = sem("vector_result")
        scalar_result = sem("scalar_result")
        weight_loaded = [sem(f"weight_loaded{i}") for i in range(WBUF)]
        weight_used = sem("weight_used")
        vec_loaded = [sem(f"vec_loaded{i}") for i in range(VBUF)]
        vec_used = sem("vec_used")
        mod_ready = sem("mod_ready")
        mod_stored = [sem(f"mod_stored{i}") for i in range(2)]
        norm_done = sem("norm_done")
        shift_stored = sem("shift_stored")
        mix_used = sem("mix_used")
        lora_loaded = sem("lora_loaded")
        spilled = [sem(f"spilled{i}") for i in range(3)]
        all_spilled = sem("all_spilled")
        cur_loaded = sem("cur_loaded")
        cur_used = sem("cur_used")
        s0_loaded = sem("s0_loaded")
        s0_used = sem("s0_used")
        masked_used = sem("masked_used")
        state_stored = [sem(f"state_stored{i}") for i in range(2)]
        gla_small_loaded = sem("gla_small_loaded")
        gla_state_loaded = [sem(f"gla_state_loaded{i}") for i in range(2)]
        gla_state_new = sem("gla_state_new")
        gla_state_stored = [sem(f"gla_state_stored{i}") for i in range(2)]
        gla_prompt_stored = sem("gla_prompt_stored")
        arena_free = sem("arena_free")
        keys_loaded = sem("keys_loaded")
        experts_chosen = sem("experts_chosen")
        idx_copied = sem("idx_copied")
        pool_passed = sem("pool_passed")
        rows_landed = [sem(f"rows_landed{i}") for i in range(NGRP)]
        rows_used = [sem(f"rows_used{i}") for i in range(NGRP)]
        acts_copied = sem("acts_copied")
        diag_ready = sem("diag_ready")
        y_ready = sem("y_ready")
        y_stored = sem("y_stored")
        gla_prompt_new = sem("gla_prompt_new")

        block = ctx.enter_context(nc.Block())

        xx, lora1 = W(0, 3 * D).rearrange("p (k t) -> p k t", k=KD), W(9 * D, 2 * D).rearrange("p (k t) -> p k t", k=KD)
        mixb = [W((3 + 3 * i) * D, 3 * D).rearrange("p (k t) -> p k t", k=KD) for i in range(2)]
        spill_buf = [W(11 * D + 512 * i, 512) for i in range(3)]
        cur = [U(16 + i) for i in range(3)]
        lora2 = U(19, 2).rearrange("p (i n) -> p i n", i=2)
        g2 = U(21)
        loraT = W(22 * D, 3 * TOK).rearrange("p (i t) -> p i t", i=3)
        modrow = [U(0), U(1)]
        crow, srow, murow = U(2), U(3), W(4 * D, P)
        qT = W(0, 4 * TOK).rearrange("p (h t) -> p h t", h=GH)
        kT = W(4 * TOK, 4 * TOK).rearrange("p (h t) -> p h t", h=GH)
        gv = [U(3 + t) for t in range(NT)]
        gr = [U(6 + t) for t in range(NT)]
        la, bT = W(9 * D, 512), W(9 * D + 512, 512)
        ex, df = W(10 * D, 512), W(10 * D + 512, 512)
        qe, ke = W(11 * D, 512), W(11 * D + 512, 512)
        at, atmp = W(12 * D, 512), W(12 * D + 512, 512)
        kd = W(13 * D, 512)
        go = U(14)
        gS = U(15)
        gS0 = [U(16, 2), U(18, 2)]
        qem, kdm = U(20), U(21)
        alT, wa2 = W(22 * D, TOK), W(22 * D + TOK, 512)
        ebt = W(13 * D + 512, GH * DEC_B)
        ring = U(0, 16).rearrange("p (s n) -> p s n", s=RING)
        skT = U(16, 2).rearrange("p (i n) -> p i n", i=HP)
        qb = [W(18 * D + TOK * i, TOK) for i in range(2)]
        sk = U(19, 2).rearrange("p (i k) -> p i k", i=HP)
        diag = U(19, 2).rearrange("p (s k) -> p s k", s=RING)
        top_s = W(21 * D, NT * 256).rearrange("p (t i e) -> p t i e", t=NT, i=HP)
        top_i = W(21 * D + NT * 256, NT * 256).bitcast(U32).rearrange("p (t i e) -> p t i e", t=NT, i=HP)
        peer_tmp = U(16)
        hflat = hT[:, :, :].rearrange("p k t -> p (k t)")
        cand = hflat[:, 0:2 * D]
        onehot = cand
        small = [U(18)[:, P * i:P * (i + 1)] for i in range(8)]
        scratch, sc, pf, e1, e2 = small[0:5]
        pos, pi = small[5].bitcast(U32), small[6].bitcast(U32)
        rest = hflat[:, 2 * D:2 * D + 256]
        iF = hflat[:, 2 * D + 256:2 * D + 512]
        gate = W(22 * D + 512, NT * P).rearrange("p (t e) -> p t e", t=NT)
        idx = W(17 * D, NT * P + 16).bitcast(U32)

        def diag_blocks(dst):
            return bass.AP(tensor=dst.tensor, offset=dst.offset,
                           ap=[list(dst.ap[0]), [P + DEC_T, DEC_B], [DEC_B * DEC_T, COPIES], [1, DEC_T]])

        def own_rows(src):
            return src.rearrange("p (c b i) -> p b c i", c=COPIES, b=DEC_B)

        @block.sync
        def _(sp):
            w = Waits(sp)
            n = [0]

            def weight(src):
                b = n[0] % WBUF
                if n[0] >= WBUF:
                    w.take(weight_used)
                cols = src.shape[1]
                sp.dma_start(wring[:, b, :, 0:cols], src.rearrange("(k p) n -> p k n", p=P)).then_inc(weight_loaded[b], 16)
                n[0] += 1

            sp.dma_start(crow[0:1, :], a["c_prompt"]).then_inc(small_loaded, 16)
            sp.dma_start(crow[1:9, :], a["c_sample"]).then_inc(small_loaded, 16)
            sp.dma_start(srow[0:8, :], a["state_rwkv_shift"][0]).then_inc(small_loaded, 16)
            sp.dma_start(murow[0:48, :], a["rw_mu"][0].rearrange("i (k p) -> (i k) p", p=P)).then_inc(small_loaded, 16)
            xs = a["x_sample"].rearrange("b t d -> (b t) d")
            for t in range(2):
                sp.dma_start(x[:, t, :], a["x_prompt"][0, t * P:(t + 1) * P, :]).then_inc(x_loaded, 16)
            for c in range(COPIES):
                sp.dma_start(x[32 * c:32 * c + 32, SAMPLE, :], xs).then_inc(x_loaded, 16)
            for li in range(2):
                for j in range(12):
                    weight(a["ada_w"][li][:, j * 512:(j + 1) * 512])
                if li == 0:
                    w.take(arena_free)
                    for src, lo in ((a["rw_w1"], 0), (a["rw_a1"], 64), (a["rw_g1"], 128)):
                        cols = src.shape[2]
                        sp.dma_start(lora1[:, :, lo:lo + cols], src[0].rearrange("(k p) n -> p k n", p=P)).then_inc(lora_loaded, 16)
                    for i, (m, b) in enumerate((("rw_w2", "rw_w0"), ("rw_a2", "rw_a0"))):
                        sp.dma_start(lora2[0:64, i, :], a[m][0]).then_inc(lora_loaded, 16)
                        sp.dma_start(lora2[64:65, i, :], a[b]).then_inc(lora_loaded, 16)
                    sp.dma_start(g2, a["rw_g2"][0]).then_inc(lora_loaded, 16)
                    w.take(norm_done)
                    sp.dma_start(sh_p[0], hc[P - 1:P, 1, :]).then_inc(shift_stored, 16)
                    sp.dma_start(sh_s[0], hc[DEC_T - 1:DEC_B * DEC_T:DEC_T, SAMPLE, :]).then_inc(shift_stored, 16)
                    for i in (0, 1, 2):
                        for j in range(2):
                            weight(a["rw_w_rkv"][0, i][:, j * 512:(j + 1) * 512])
                    w.take(all_spilled)
                    for t in range(NT):
                        if t:
                            w.take(cur_used)
                        for i in range(3):
                            sp.dma_start(cur[i], rkv_d[i, t]).then_inc(cur_loaded, 16)
                        if t == 0:
                            for j in range(2):
                                weight(a["rw_wo"][0][:, j * 512:(j + 1) * 512])
                        if t == SAMPLE:
                            w.take(shift_stored, 32)
                            for hh in range(2):
                                for q in range(2):
                                    if hh or q:
                                        w.take(s0_used)
                                    for b in range(4):
                                        sp.dma_start(
                                            hc[0:RK, 0:2, :].rearrange("v u (c n) -> v (u c) n", c=2)[:, b, :].rearrange("v (h k) -> v h k", k=RK),
                                            a["state_rwkv_S"][0, 4 * q + b, hh * HALF_H:(hh + 1) * HALF_H].rearrange("h v k -> v h k"),
                                        ).then_inc(s0_loaded, 16)
                else:
                    w.take(arena_free)
                    w.take(norm_done)
                    sp.dma_start(wa2[0:16, :], a["gla_wa2"][0]).then_inc(gla_small_loaded, 16)
                    sp.dma_start(wa2[16:17, :], a["gla_ba"]).then_inc(gla_small_loaded, 16)
                    for j in range(6):
                        weight(a["gla_w_in"][0][:, j * 512:(j + 1) * 512])
                    weight(a["gla_w_in"][0][:, 3072:3088])
                    for j in range(2):
                        weight(a["gla_wo"][0][:, j * 512:(j + 1) * 512])
                    def gla_state(b):
                        return gS0[b].rearrange("p (b v) -> p b v", b=DEC_B)

                    for h in range(GH + 2):
                        if h == 2:
                            w.take(gla_prompt_new)
                            sp.dma_start(G_p[0, 0].rearrange("h k v -> k h v"), gS.rearrange("p (h v) -> p h v", h=GH)).then_inc(gla_prompt_stored, 16)
                        if h >= 2:
                            w.take(gla_state_new)
                            sp.dma_start(G_s[0, :, h - 2].rearrange("b k v -> k b v"), gla_state(h % 2)).then_inc(gla_state_stored[h % 2], 16)
                        if h < GH:
                            if h >= 2:
                                w.take(gla_state_stored[h % 2], 16)
                            sp.dma_start(gla_state(h % 2), a["state_gla_S"][0, :, h].rearrange("b k v -> k b v")).then_inc(gla_state_loaded[h % 2], 16)
                w.take(arena_free)
                sp.dma_start(sk[:, :, :], a["peer_subkeys"][li].rearrange("h s n k -> n (h s) k")).then_inc(keys_loaded, 16)
                for j in range(4):
                    weight(a["peer_wq"][li][:, j * 512:(j + 1) * 512])
            w.take(y_ready)
            sp.dma_start(y_p[0].rearrange("(t p) d -> p t d", p=P), hc[:, 0:2, :]).then_inc(y_stored, 16)
            sp.dma_start(y_s.rearrange("b t d -> (b t) d"), hc[0:32, SAMPLE, :]).then_inc(y_stored, 16)
            sp.wait_ge(y_stored, 32)
            sp.wait_ge(shift_stored, 32)
            sp.wait_ge(gla_prompt_stored, 16)
            sp.wait_ge(gla_state_stored[0], 32)
            sp.wait_ge(gla_state_stored[1], 32)

        @block.gpsimd
        def _(pool):
            w = Waits(pool)
            nv = [0]
            rounds = [0] * NGRP
            ncopy = [0]

            def vec(src, sample=False):
                b = nv[0] % VBUF
                if nv[0] >= VBUF:
                    w.take(vec_used)
                nv[0] += 1
                if sample:
                    for c in range(COPIES):
                        pool.dma_start(vring[32 * c:32 * c + 32, b, :],
                                       src[1:9, :].unsqueeze(1).to_broadcast([DEC_B, DEC_T, D])).then_inc(vec_loaded[b], 16)
                else:
                    nn = src.shape[1]
                    pool.dma_start(vring[:, b, 0:nn], src.to_broadcast([P, nn])).then_inc(vec_loaded[b], 16)

            def row(name, i=0):
                return a[name][i:i + 1, :]

            pool.memset(zeros[:], 0.0).then_inc(pool_consts, 1)
            pool.memset(ident[:], 0.0).then_inc(pool_consts, 1)
            pool.wait_ge(pool_consts, 2)
            pool.affine_select(out=ident[:], in_=ident[:], compare_op=ALU.not_equal, fill=1.0, base=0,
                               pattern=[[-1, P]], channel_multiplier=1).then_inc(pool_consts, 1)
            pool.iota(U(5)[:, 0:P].bitcast(I32), [[1, P]], base=0, channel_multiplier=0).then_inc(pool_consts, 1)
            pool.iota(U(5)[:, P:2 * P].bitcast(I32), [[0, P]], base=0, channel_multiplier=1).then_inc(pool_consts, 1)

            def norm_vecs(name, li, k):
                vec(row(name, li))
                for s in (False, True):
                    vec(mod_d[li, k + 1] if s else mod_d[li, k + 1, 0:1], s)
                    vec(mod_d[li, k] if s else mod_d[li, k, 0:1], s)

            u_rows = a["peer_u"].rearrange("l n d -> (l n) d")
            v_rows = a["peer_v"].rearrange("l n d -> (l n) d")

            def gather(n, u, v):
                both = bool(u and v)
                sides = [(side, tab, *which) for side, tab, which in ((0, u_rows, u), (1, v_rows, v)) if which]
                turns = sorted((k, side, g, tab, t, first) for side, tab, t, first in sides
                               for k, g in enumerate(groups_of(side, both)))
                per = len(turns) // len(sides) * GRP
                with pool.Fori(0, n // per) as i:
                    for m, (k, side, g, tab, t, first) in enumerate(turns):
                        pool.wait_ge(rows_used[g], i * GRP + (rounds[g] * GRP + 1))
                        pool.sem_inc(pool_passed, 1)
                        pool.tensor_copy(idx_grp[:, g * GRP:(g + 1) * GRP],
                                         idx[:, bass.ds(i * per + (t * P + first + k * GRP), GRP)]).then_inc(idx_copied, 1)
                        pool.wait_ge(idx_copied, i * NGRP + (ncopy[0] + m + 1))
                        pool.sem_inc(pool_passed, 1)
                        for s in range(g * GRP, (g + 1) * GRP):
                            pool.indirect_dma_start(ring[:, s, :], None, tab,
                                                    bass.IndirectOffsetOnAxis(idx_grp[:, s:s + 1], 0)).then_inc(rows_landed[g], 16)
                for g in range(NGRP):
                    rounds[g] += n // per
                ncopy[0] += NGRP * (n // per)

            for li in range(2):
                for k in range(6):
                    vec(a["ada_b"][li:li + 1, k * D:(k + 1) * D])
                for i in range(2):
                    w.take(mod_stored[i], 3 * 16)
                norm_vecs("norm1_g", li, 0)
                for t in range(NT):
                    if li == 0:
                        for name in ("rw_kk", "rw_ka", "rw_rk", "rw_lnx_w", "rw_lnx_b"):
                            vec(a["rw_rk"].rearrange("r h k -> r (h k)") if name == "rw_rk" else row(name))
                    else:
                        vec(row("gla_gnorm"))
                vec(mod_d[li, 2, 0:1])
                vec(mod_d[li, 2], True)
                norm_vecs("norm2_g", li, 3)
                vec(mod_d[li, 5, 0:1])
                w.take(experts_chosen)
                for n, u, v, choice in SEGMENTS:
                    if choice:
                        w.take(experts_chosen)
                    gather(n, u, v)
                vec(mod_d[li, 5], True)
            vec(a["final_g"].rearrange("(o n) -> o n", o=1))

        @block.scalar
        def _(act):
            w = Waits(act)
            steps = {}
            nf = [0]
            nsp = [0]
            rounds = [0] * NGRP
            nst = [0, 0]

            def done(ins, s=None):
                s = s or scalar_step
                steps[s.name] = steps.get(s.name, 0) + 1
                ins.then_inc(s, 1)
                act.wait_ge(s, steps[s.name])

            def fill():
                w.take(psum_for_scalar)
                nf[0] += 1
                return psa[:, (nf[0] - 1) % 2, :]

            def copy_out(dst, cols, rows=P, func=ACT.Copy, scale=1.0):
                ps = fill()
                src = ps[0:rows, 0:cols]
                if len(dst.shape) == 3:
                    src = src.rearrange("p (x y) -> p x y", y=dst.shape[2])
                done(act.activation(dst, src, func, scale=scale), scalar_drained)

            def root(dst, src):
                w.take(vector_result)
                done(act.activation(dst, src, ACT.Sqrt))
                act.sem_inc(scalar_result, 1)

            w.take(small_loaded, 64)
            done(act.activation(crow[0:9, :], crow[0:9, :], ACT.Silu))
            act.sem_inc(operand_written, 1)
            copy_out(cT[:, :], KD * 9)
            copy_out(shiftT[:, :], KD * DEC_B)
            copy_out(muT[:, :], 48)
            act.sem_inc(arena_free, 1)

            def to_hT(t):
                copy_out(hT[:, :, t * P:(t + 1) * P], D)

            for li in range(2):
                for k in range(6):
                    w.take(mod_ready)
                    act.dma_start(mod_d[li, k], modrow[k % 2][0:9, :]).then_inc(mod_stored[k % 2], 16)
                root(rstd[:, 0:3], rstd[:, 0:3])
                for t in range(NT):
                    to_hT(t)
                if li == 0:
                    act.sem_inc(scalar_result, 1)

                    def spill(i):
                        for j in range(2):
                            for t in range(NT):
                                b = nsp[0] % 3
                                if nsp[0] >= 3:
                                    act.wait_ge(spilled[b], 16 * (nsp[0] // 3))
                                copy_out(spill_buf[b], 512)
                                act.dma_start(rkv_d[i, t][:, j * 512:(j + 1) * 512], spill_buf[b]).then_inc(spilled[b], 16)
                                nsp[0] += 1

                    spill(0)
                    copy_out(loraT[0:64, 0, :], TOK, 64, ACT.Tanh)
                    spill(1)
                    spill(2)
                    copy_out(loraT[0:64, 1, :], TOK, 64)
                    copy_out(loraT[:, 2, :], TOK, P, ACT.Sigmoid)
                    for b in range(3):
                        act.wait_ge(spilled[b], 16 * 6)
                    act.sem_inc(all_spilled, 1)
                    act.sem_inc(scalar_result, 1)
                    for t in range(NT):
                        sample = t == SAMPLE
                        copy_out(U(0), D, func=ACT.Sigmoid)
                        copy_out(U(1), D, func=ACT.Sigmoid)
                        ps = fill()
                        done(act.activation(U(5), ps, ACT.Exp, scale=-DECAY_C))
                        done(act.activation(U(6), ps, ACT.Exp, scale=DECAY_C), scalar_drained)
                        nn = DEC_B if sample else 2
                        copy_out(pcs[:, :, 0:nn], KD * nn, func=ACT.Exp, scale=-DECAY_C)
                        done(act.activation(U(7), U(0), ACT.Exp, scale=DECAY_C))
                        act.sem_inc(scalar_result, 1)
                        root(s16[:, 0, :], s16[:, 0, :])
                        w.take(vector_result)
                        for hh in range(2):
                            ps = fill()
                            for i in range(2):
                                z = U(5 + i).rearrange("p (q e t) -> p q e t", q=PAIRS, e=2)
                                for e in range(2):
                                    r0 = 64 * e
                                    ins = act.activation(z[r0:r0 + 64, :, e, :],
                                                         ps[r0:r0 + 64, i * 512:(i + 1) * 512].rearrange("p (q t) -> p q t", q=PAIRS), ACT.Copy)
                                    done(ins, scalar_drained if i and e else None)
                            copy_out(U(7), D)
                            for k in ([1] if sample else range(1, 7)):
                                copy_out(U(3), D)
                            if sample:
                                for q in range(2):
                                    copy_out(U(14, 2).rearrange("p (q n) -> p q n", q=2)[:, q, :], D)
                                    act.sem_inc(s0_used, 1)
                                act.sem_inc(scalar_result, 1)
                            copy_out(U(0)[:, 0:512], 512)
                            copy_out(U(0)[:, 512:1024], 512)
                            act.sem_inc(scalar_result, 1)
                            copy_out(cur[1][:, hh * 512:(hh + 1) * 512], 512)
                            if sample:
                                for q in range(4):
                                    i = q % 2
                                    if nst[i]:
                                        act.wait_ge(state_stored[i], nst[i])
                                    copy_out(U(8 + i)[0:RK, :], D, RK)
                                    for b in range(2):
                                        act.dma_start(S_s[0, 2 * q + b, hh * HALF_H:(hh + 1) * HALF_H].rearrange("h v k -> v h k"),
                                                      U(8 + i)[0:RK, b * 512:(b + 1) * 512].rearrange("v (h k) -> v h k", k=RK)).then_inc(state_stored[i], 16)
                                        nst[i] += 16
                            elif t == 1:
                                copy_out(U(8)[0:RK, 0:512], 512, RK)
                                act.dma_start(S_p[0, 0, hh * HALF_H:(hh + 1) * HALF_H].rearrange("h v k -> v h k"),
                                              U(8)[0:RK, 0:512].rearrange("v (h k) -> v h k", k=RK)).then_inc(state_stored[0], 16)
                                nst[0] += 16
                            for i in range(2):
                                if nst[i]:
                                    act.wait_ge(state_stored[i], nst[i])
                            act.sem_inc(scalar_result, 1)
                        root(s16[:, 1, :], s16[:, 1, :])
                        to_hT(t)
                        act.sem_inc(cur_used, 1)
                        act.sem_inc(scalar_result, 1)
                else:
                    for h in range(GH):
                        copy_out(qT[:, h, :], TOK, scale=GK ** -0.5)
                    for h in range(GH):
                        copy_out(kT[:, h, :], TOK)
                    for j in range(2):
                        for t in range(NT):
                            copy_out(gv[t][:, j * 512:(j + 1) * 512], 512)
                    for j in range(2):
                        for t in range(NT):
                            copy_out(gr[t][:, j * 512:(j + 1) * 512], 512, func=ACT.Silu)
                    w.take(vector_result)
                    copy_out(alT[0:16, :], TOK, 16)
                    act.sem_inc(scalar_result, 1)
                    for t in range(NT):
                        sample = t == SAMPLE
                        w.take(vector_result)
                        done(act.activation(ex, ex, ACT.Exp, scale=-1.0))
                        act.sem_inc(scalar_result, 1)
                        w.take(vector_result)
                        done(act.activation(ex, ex, ACT.Ln))
                        act.sem_inc(scalar_result, 1)
                        copy_out(bT, 512, scale=1.0 / TAU)
                        act.sem_inc(scalar_result, 1)
                        for k in (range(2) if sample else range(7)):
                            m = 1 << k
                            w.take(vector_result)
                            d3 = df.rearrange("p (b m) -> p b m", m=2 * m)
                            e3 = ex.rearrange("p (b m) -> p b m", m=2 * m)
                            done(act.activation(e3[:, :, m:2 * m], d3[:, :, m:2 * m], ACT.Exp))
                            done(act.activation(e3[:, :, 0:m], d3[:, :, 0:m], ACT.Exp, scale=-1.0))
                            act.sem_inc(scalar_result, 1)
                        w.take(vector_result)
                        done(act.activation(ex, bT, ACT.Exp))
                        done(act.activation(df, df, ACT.Exp))
                        nb = DEC_B if sample else 1
                        src = bT.rearrange("p (h s i) -> p h s i", h=GH, i=DEC_T)[:, :, 0:DEC_B, DEC_T - 1] if sample else \
                            bT.rearrange("p (h s) -> p h s", h=GH)[:, :, P - 1:P]
                        done(act.activation(ebt.rearrange("p (h b) -> p h b", h=GH)[:, :, 0:nb], src, ACT.Exp))
                        act.sem_inc(scalar_result, 1)
                        copy_out(kd, 512)
                        act.sem_inc(scalar_result, 1)
                        root(rstd[:, 0:4], rstd[:, 0:4])
                        to_hT(t)
                        act.sem_inc(scalar_result, 1)
                root(rstd[:, 0:3], rstd[:, 0:3])
                for t in range(NT):
                    to_hT(t)
                for i in range(2):
                    copy_out(skT[:, 8 * i:8 * i + 8, :], D)
                for hp in range(HP):
                    copy_out(qb[hp % 2], TOK)
                def diagonals(n, t, first, both):
                    groups = groups_of(1, both)
                    per = len(groups) * GRP
                    with act.Fori(0, n // per) as i:
                        for k, g in enumerate(groups):
                            act.wait_ge(rows_used[g], i * GRP + (rounds[g] * GRP + 1))
                            for s in range(GRP):
                                act.activation(diag[:, g * GRP + s, :], rep32[:, :] if t == SAMPLE else ident[:, :], ACT.Copy,
                                               scale=acts[:, t % 2, bass.ds(i * per + (first + k * GRP + s), 1)]).then_inc(diag_ready, 1)

                for n, u, v, choice in SEGMENTS:
                    both = bool(u and v)
                    if v:
                        diagonals(n, *v, both)
                    for g in range(NGRP):
                        rounds[g] += n // (len(groups_of(0, both)) * GRP)
                    if u and u[1] + n == experts_of(u[0]):
                        t, slots = u[0], experts_of(u[0])
                        w.take(vector_result)
                        done(act.activation(gate[:, t, 0:slots], gate[:, t, 0:slots], ACT.Exp))
                        done(act.activation(acts[:, t % 2, 0:slots], acts[:, t % 2, 0:slots], ACT.Gelu))
                        act.sem_inc(scalar_result, 1)
                        w.take(vector_result)
            root(rstd[:, 0:3], rstd[:, 0:3])

        @block.vector
        def _(dve):
            w = Waits(dve)
            steps = {}
            nf = [0]
            nv = [0]
            vd = [0] * VBUF
            rounds = [0] * NGRP
            ncopied = [0]
            am_made = [0]

            def done(ins, s=None):
                s = s or vector_step
                steps[s.name] = steps.get(s.name, 0) + 1
                ins.then_inc(s, 1)
                dve.wait_ge(s, steps[s.name])

            def tt(out, i0, i1, op, s=None):
                done(dve.tensor_tensor(out, i0, i1, op), s)

            def ts(out, i0, a1, a2, o0, o1=None, s=None):
                done(dve.tensor_scalar(out, i0, a1, a2, o0, o1) if o1 is not None else dve.tensor_scalar(out, i0, a1, None, o0), s)

            def stt(out, i0, sc, i1, o0, o1, s=None):
                done(dve.scalar_tensor_tensor(out=out, in0=i0, scalar=sc, in1=i1, op0=o0, op1=o1), s)

            def fill():
                w.take(psum_for_vector)
                nf[0] += 1
                return psv[:, (nf[0] - 1) % 2, :]

            def vec(k=1):
                b = nv[0] % VBUF
                vd[b] += 16 * k
                dve.wait_ge(vec_loaded[b], vd[b])
                nv[0] += 1
                return vring[:, b, :]

            MUL, ADD, SUB = ALU.mult, ALU.add, ALU.subtract

            w.take(pool_consts, 5)
            ci, ri = U(5)[:, 0:P].bitcast(I32), U(5)[:, P:2 * P].bitcast(I32)
            c2, r2 = U(6)[:, 0:P].bitcast(I32), U(6)[:, P:2 * P].bitcast(I32)
            cf, rf = U(7)[:, 0:P], U(7)[:, P:2 * P]
            eq = U(8).rearrange("p (k n) -> p k n", k=8)
            done(dve.tensor_copy(cf, ci))
            done(dve.tensor_copy(rf, ri))
            tt(le[:], rf, cf, ALU.is_le)
            tt(lt[:], rf, cf, ALU.is_lt)
            for k in range(7):
                ts(c2, ci, k, None, ALU.arith_shift_right)
                ts(r2, ri, k, None, ALU.arith_shift_right)
                tt(eq[:, k, :], c2, r2, ALU.is_equal)
                if k == 2:
                    tt(seq_ind[:], ci[:, 0:DEC_B], r2[:, 0:DEC_B], ALU.is_equal)
            done(dve.memset(eq[:, 7, :], 1.0))
            for k in range(7):
                tt(lev[:, k, :], eq[:, k + 1, :], eq[:, k, :], SUB)
            tt(le4[:], le[:], eq[:, 2, :], MUL)
            tt(lt4[:], lt[:], eq[:, 2, :], MUL)
            tt(low0[:], rf, cf, ALU.is_gt)
            tt(low0[:], low0[:], lev[:, 0, :], MUL)
            ts(half_ind[:, 0:1], rf[:, 0:1], 63.5, None, ALU.is_le)
            ts(half_ind[:, 1:2], rf[:, 0:1], 63.5, None, ALU.is_gt)
            tt(cum_mid[:], le[:], half_ind[:, 0:1].to_broadcast([P, P]), SUB)
            ts(c2, ci, 31, None, ALU.bitwise_and)
            ts(r2, ri, 31, None, ALU.bitwise_and)
            tt(rep32[:], c2, r2, ALU.is_equal)
            done(dve.tensor_copy(iota16[:], cf[:, 0:TOPK]))
            done(dve.memset(stateT[:], 0.0))
            for g in range(NGRP):
                dve.sem_inc(rows_used[g], 1)
            dve.sem_inc(consts_built, 1)

            def norm():
                for t in range(NT):
                    done(dve.tensor_tensor_reduce(hc[:, t, :], x[:, t, :], x[:, t, :], 1.0, 0.0, MUL, ADD, rstd[:, t:t + 1]))
                ts(rstd[:, 0:3], rstd[:, 0:3], 1.0 / D, EPS, MUL, ADD)
                dve.sem_inc(vector_result, 1)
                w.take(scalar_result)
                done(dve.reciprocal(rstd[:, 0:3], rstd[:, 0:3]))
                g = vec()
                for t in range(NT):
                    stt(hc[:, t, :], x[:, t, :], rstd[:, t:t + 1], g, MUL, MUL)
                dve.sem_inc(vec_used, 1)

            def adaln():
                norm()
                for tiles, k in (((0, 1), 1), ((2,), 4)):
                    sc = vec(k)
                    for t in tiles:
                        stt(hc[:, t, :], sc, 1.0, hc[:, t, :], ADD, MUL)
                    dve.sem_inc(vec_used, 1)
                    sh = vec(k)
                    for t in tiles:
                        tt(hc[:, t, :], hc[:, t, :], sh, ADD)
                    dve.sem_inc(vec_used, 1)
                dve.sem_inc(operand_written, 1)

            def gated_add(tmp):
                for t in range(NT):
                    if t != 1:
                        g = vec(4 if t == SAMPLE else 1)
                    ps = fill()
                    tt(tmp, ps, g, MUL, vector_drained)
                    tt(x[:, t, :], x[:, t, :], tmp, ADD)
                    if t:
                        dve.sem_inc(vec_used, 1)

            def top16(vals, idxs, src, scratch):
                done(dve.max(vals[:, 0:8], src))
                done(dve.max_index(idxs[:, 0:8], vals[:, 0:8], src))
                done(dve.match_replace(scratch, vals[:, 0:8], src, LOWEST))
                done(dve.max(vals[:, 8:16], scratch))
                done(dve.max_index(idxs[:, 8:16], vals[:, 8:16], scratch))

            def bc(ap, n):
                return ap.unsqueeze(2).to_broadcast([P, ap.shape[1], n])

            for li in range(2):
                for k in range(6):
                    ps = fill()
                    b = vec()
                    if k >= 2:
                        dve.wait_ge(mod_stored[k % 2], 16 * (3 * li + k // 2))
                    tt(modrow[k % 2][0:9, :], ps[0:9, :], b[0:9, :], ADD, vector_drained)
                    dve.sem_inc(mod_ready, 1)
                    dve.sem_inc(vec_used, 1)
                if li == 0:
                    w.take(x_loaded, 6 * 16)
                if li:
                    for i in range(2):
                        dve.wait_ge(mod_stored[i], 6 * 16)
                    dve.sem_inc(arena_free, 1)
                adaln()
                dve.sem_inc(norm_done, 1)
                if li == 0:
                    for i in range(2):
                        dve.wait_ge(mod_stored[i], 3 * 16)
                    w.take(scalar_result)
                    n = 2 * P
                    tt(xx[:, :, 1:n], hT[:, :, 0:n - 1], hT[:, :, 1:n], SUB)
                    ts(xx[:, :, 0:1], hT[:, :, 0:1], -1.0, None, MUL)
                    xs4 = xx[:, :, n:].rearrange("p k (s i) -> p k s i", i=DEC_T)
                    hs4 = hT[:, :, n:].rearrange("p k (s i) -> p k s i", i=DEC_T)
                    for k in range(KD):
                        tt(xs4[:, k, :, 1:DEC_T], hs4[:, k, :, 0:DEC_T - 1], hs4[:, k, :, 1:DEC_T], SUB)
                    sT = shiftT[:, :].rearrange("p (k b) -> p k b", k=KD)
                    for c in range(COPIES):
                        tt(xs4[:, :, c * DEC_B:(c + 1) * DEC_B, 0], sT, hs4[:, :, c * DEC_B:(c + 1) * DEC_B, 0], SUB)
                    done(dve.memset(loraT[64:65, 0:2, :], 1.0))
                    for n, i in enumerate((0, 3, 1, 2, 4, 5)):
                        if n >= 2:
                            w.take(mix_used)
                        for k in range(KD):
                            stt(mixb[n % 2][:, k, :], xx[:, k, :], muT[:, i * KD + k:i * KD + k + 1], hT[:, k, :], MUL, ADD)
                        dve.sem_inc(operand_written, 1)
                    w.take(scalar_result)
                    for t in range(NT):
                        sample = t == SAMPLE
                        r, k_, v = cur
                        w.take(cur_loaded, 48)
                        g = vec()
                        tt(U(2), k_, g, MUL)
                        dve.sem_inc(vec_used, 1)
                        tt(U(3), U(2), U(2), MUL)
                        done(dve.tensor_reduce(s16[:, 0, :], heads(U(3), RH, RK), AXX, ADD))
                        w.take(scalar_result)
                        dve.sem_inc(vector_result, 1)
                        w.take(scalar_result)
                        ts(s16[:, 0, :], s16[:, 0, :], 1e-12, None, ALU.max)
                        done(dve.reciprocal(s16[:, 0, :], s16[:, 0, :]))
                        tt(heads(U(2), RH, RK), heads(U(2), RH, RK), bc(s16[:, 0, :], RK), MUL)
                        g = vec()
                        stt(U(3), U(1), -1.0, g, ADD, MUL)
                        dve.sem_inc(vec_used, 1)
                        stt(U(4), U(3), 1.0, k_, ADD, MUL)
                        g = vec()
                        tt(U(3), U(4), r, MUL)
                        tt(U(3), U(3), g, MUL)
                        dve.sem_inc(vec_used, 1)
                        done(dve.tensor_reduce(bonus[:], heads(U(3), RH, RK), AXX, ADD))
                        tt(U(1), U(1), U(2), MUL)
                        tt(U(1), U(1), U(6), MUL)
                        stt(U(2), U(2), -1.0, U(7), MUL, MUL)
                        tt(U(2), U(2), U(5), MUL)
                        tt(r, r, U(5), MUL)
                        tt(U(4), U(4), U(6), MUL)
                        done(dve.memset(U(5), 0.0))
                        done(dve.memset(U(6), 0.0))
                        dve.sem_inc(vector_result, 1)
                        dve.sem_inc(operand_written, 1)
                        strict, incl = (lt4, le4) if sample else (lt, le)

                        def m8(m):
                            return m.unsqueeze(1).to_broadcast([P, HALF_H, P])

                        for hh in range(2):
                            h8 = lambda i: heads(U(i), HALF_H, P)
                            tt(h8(8), heads(fill(), HALF_H, P), m8(strict[:]), MUL, vector_drained)
                            tt(h8(12), heads(fill(), HALF_H, P), m8(low0[:]), MUL, vector_drained)
                            tt(h8(9), heads(fill(), HALF_H, P), m8(strict[:]), MUL, vector_drained)
                            tt(h8(10), heads(fill(), HALF_H, P), m8(incl[:]), MUL, vector_drained)
                            tt(h8(11), heads(fill(), HALF_H, P), m8(incl[:]), MUL, vector_drained)
                            tt(h8(12), h8(12), m8(ident[:]), ADD)
                            tt(h8(13), h8(8), m8(lev[:, 0, :]), MUL)
                            tt(h8(13), h8(13), m8(ident[:]), ADD)
                            levels = [1] if sample else range(1, 7)
                            for k in levels:
                                tt(h8(14), h8(8), m8(lev[:, k, :]), MUL)
                                dve.sem_inc(operand_written, 1)
                                if k != levels[-1]:
                                    tt(U(12), U(12), fill(), ADD, vector_drained)
                                tt(U(13), U(13), fill(), ADD, vector_drained)
                            if sample:
                                w.take(scalar_result)
                                done(dve.memset(U(12), 0.0))
                                done(dve.memset(U(3), 0.0))
                                for src in (5, 6):
                                    for h in range(HALF_H):
                                        if h + 8 * (src - 5) >= 2:
                                            w.take(masked_used)
                                        done(dve.tensor_copy(diag_blocks(U((12, 3)[h % 2])), own_rows(U(src)[:, h * P:(h + 1) * P])))
                                        dve.sem_inc(operand_written, 1)
                                w.take(masked_used, 2)
                                w.take(scalar_result)
                                s0 = U(14, 2).rearrange("p (b q v) -> p b q v", b=DEC_B, q=PAIRS)
                                sind = seq_ind[:].unsqueeze(1).unsqueeze(3).to_broadcast([P, 1, DEC_B, RK])
                                for q in range(PAIRS):
                                    for src, dst in ((U(0)[:, 512 + 128 * q:640 + 128 * q], U(12)),
                                                     (v[:, hh * 512 + 128 * q:hh * 512 + 128 * q + 128], U(3))):
                                        for e in range(2):
                                            done(dve.tensor_tensor(dst[:, e * 512:(e + 1) * 512].rearrange("p (b v) -> p b v", b=DEC_B),
                                                                   src[:, e * RK:(e + 1) * RK].unsqueeze(1).to_broadcast([P, DEC_B, RK]),
                                                                   seq_ind[:].unsqueeze(2).to_broadcast([P, DEC_B, RK]), MUL))
                                    dve.sem_inc(operand_written, 1)
                                    ps = fill()
                                    for e in range(2):
                                        rr = slice(64 * e, 64 * e + 64)
                                        tt(s0[rr, :, q, :], s0[rr, :, q, :], ps[rr, e * 512:(e + 1) * 512].rearrange("p (b v) -> p b v", b=DEC_B),
                                           ADD, vector_drained if e else None)
                                    tt(s0[:, :, q, :], s0[:, :, q, :], bc(pcs[:, hh * PAIRS + q, :], RK), MUL)
                                dve.sem_inc(operand_written, 1)
                            else:
                                sl = slice(hh * PAIRS, (hh + 1) * PAIRS)
                                tt(st_in[:], stateT[:, sl, :], pcs[:, sl, 0:1].to_broadcast([P, PAIRS, RK]), MUL)
                                dve.sem_inc(operand_written, 1)
                                w.take(scalar_result)
                                ps = fill().rearrange("p (q e v) -> p q e v", q=PAIRS * 2, e=2)[:, 0:PAIRS]
                                for e in range(2):
                                    rr = slice(64 * e, 64 * e + 64)
                                    tt(st_in[rr], st_in[rr], ps[rr, :, e, :], ADD, vector_drained if e else None)
                                tt(stateT[:, sl, :], st_in[:], pcs[:, sl, 1:2].to_broadcast([P, PAIRS, RK]), MUL)
                                if t == 1:
                                    dve.sem_inc(operand_written, 1)
                            w.take(scalar_result)
                        y = k_
                        mean, var = s16[:, 0, :], s16[:, 1, :]
                        done(dve.tensor_reduce(mean, heads(y, RH, RK), AXX, ADD))
                        ts(mean, mean, 1.0 / RK, None, MUL)
                        tt(heads(y, RH, RK), heads(y, RH, RK), bc(mean, RK), SUB)
                        tt(U(3), y, y, MUL)
                        done(dve.tensor_reduce(var, heads(U(3), RH, RK), AXX, ADD))
                        ts(var, var, 1.0 / RK, LNX_EPS, MUL, ADD)
                        dve.sem_inc(vector_result, 1)
                        w.take(scalar_result)
                        done(dve.reciprocal(var, var))
                        tt(heads(y, RH, RK), heads(y, RH, RK), bc(var, RK), MUL)
                        g = vec()
                        tt(y, y, g, MUL)
                        dve.sem_inc(vec_used, 1)
                        g = vec()
                        tt(y, y, g, ADD)
                        dve.sem_inc(vec_used, 1)
                        tt(heads(U(3), RH, RK), heads(v, RH, RK), bc(bonus[:], RK), MUL)
                        tt(y, y, U(3), ADD)
                        tt(y, y, fill(), MUL, vector_drained)
                        dve.sem_inc(operand_written, 1)
                        w.take(scalar_result)
                else:
                    done(dve.memset(alT[0:17, :], 1.0))
                    dve.sem_inc(vector_result, 1)
                    w.take(scalar_result)
                    done(dve.memset(gS, 0.0))
                    for t in range(NT):
                        sample = t == SAMPLE
                        ps = fill()
                        ts(la, ps[:, 0:512], 0.0, None, ALU.min)
                        stt(ex, la, -2.0, ps[:, 0:512], MUL, ADD, vector_drained)
                        dve.sem_inc(vector_result, 1)
                        w.take(scalar_result)
                        ts(ex, ex, 1.0, None, ADD)
                        dve.sem_inc(vector_result, 1)
                        w.take(scalar_result)
                        tt(la, la, ex, SUB)
                        dve.sem_inc(operand_written, 1)
                        w.take(scalar_result)
                        q3, k3 = qT[:, :, t * P:(t + 1) * P], kT[:, :, t * P:(t + 1) * P]
                        h4 = lambda ap: heads(ap, GH, P)
                        m4 = lambda m: m.unsqueeze(1).to_broadcast([P, GH, P])
                        tt(h4(at), h4(fill()[:, 0:512]), m4(ident[:]), MUL, vector_drained)
                        for k in (range(2) if sample else range(7)):
                            m = 1 << k
                            b3 = bT.rearrange("p (b m) -> p b m", m=2 * m)
                            tt(df.rearrange("p (b m) -> p b m", m=2 * m), b3,
                               b3[:, :, m - 1:m].to_broadcast([P, 512 // (2 * m), 2 * m]), SUB)
                            dve.sem_inc(vector_result, 1)
                            w.take(scalar_result)
                            tt(h4(qe), q3, h4(ex), MUL)
                            tt(h4(ke), k3, h4(ex), MUL)
                            dve.sem_inc(operand_written, 1)
                            tt(h4(atmp), h4(fill()[:, 0:512]), m4(lev[:, k, :]), MUL, vector_drained)
                            tt(at, at, atmp, ADD)
                        tt(h4(at), h4(at), m4((le4 if sample else le)[:]), MUL)
                        if sample:
                            b4 = bT.rearrange("p (b m) -> p b m", m=DEC_T)
                            tt(df.rearrange("p (b m) -> p b m", m=DEC_T), b4[:, :, 3:4].to_broadcast([P, P, DEC_T]), b4, SUB)
                        else:
                            tt(h4(df), h4(bT)[:, :, P - 1:P].to_broadcast([P, GH, P]), h4(bT), SUB)
                        dve.sem_inc(vector_result, 1)
                        w.take(scalar_result)
                        tt(h4(qe), q3, h4(ex), MUL)
                        tt(h4(ke), k3, h4(df), MUL)
                        dve.sem_inc(operand_written, 1)
                        w.take(scalar_result)
                        if sample:
                            done(dve.memset(qem, 0.0))
                            for h in range(GH):
                                done(dve.tensor_copy(diag_blocks(qem), own_rows(qe[:, h * P:(h + 1) * P])))
                                tt(kdm.rearrange("p (b n) -> p b n", b=DEC_B), kd[:, h * P:(h + 1) * P].unsqueeze(1).to_broadcast([P, DEC_B, P]),
                                   bc(seq_ind[:], P), MUL)
                                dve.sem_inc(operand_written, 1)
                                s0 = gS0[h % 2].rearrange("p (b v) -> p b v", b=DEC_B)
                                w.take(gla_state_loaded[h % 2], 16)
                                done(dve.tensor_copy(go[:, h * GV:(h + 1) * GV], fill()[:, 0:GV]), vector_drained)
                                tt(s0, s0, ebt.rearrange("p (h b) -> p h b", h=GH)[:, h, :].unsqueeze(2).to_broadcast([P, DEC_B, GV]), MUL)
                                for q in range(2):
                                    tt(gS0[h % 2][:, q * D:(q + 1) * D], gS0[h % 2][:, q * D:(q + 1) * D], fill(), ADD, vector_drained)
                                dve.sem_inc(gla_state_new, 1)
                        else:
                            done(dve.tensor_copy(go, fill()), vector_drained)
                            g3 = heads(gS, GH, GV)
                            tt(g3, g3, ebt.rearrange("p (h b) -> p h b", h=GH)[:, :, 0:1].to_broadcast([P, GH, GV]), MUL)
                            tt(gS, gS, fill(), ADD, vector_drained)
                            if t == 1:
                                dve.sem_inc(gla_prompt_new, 1)
                        tt(U(10), go, go, MUL)
                        done(dve.tensor_reduce(rstd[:, 0:4], heads(U(10), GH, GV), AXX, ADD))
                        ts(rstd[:, 0:4], rstd[:, 0:4], 1.0 / GV, EPS, MUL, ADD)
                        dve.sem_inc(vector_result, 1)
                        w.take(scalar_result)
                        done(dve.reciprocal(rstd[:, 0:4], rstd[:, 0:4]))
                        tt(heads(go, GH, GV), heads(go, GH, GV), bc(rstd[:, 0:4], GV), MUL)
                        g = vec()
                        tt(heads(go, GH, GV), heads(go, GH, GV), g[:, 0:GV].unsqueeze(1).to_broadcast([P, GH, GV]), MUL)
                        dve.sem_inc(vec_used, 1)
                        tt(go, go, gr[t], MUL)
                        dve.sem_inc(operand_written, 1)
                        w.take(scalar_result)
                    dve.wait_ge(gla_prompt_stored, 16)
                    dve.wait_ge(gla_state_stored[0], 32)
                    dve.wait_ge(gla_state_stored[1], 32)
                gated_add(U(0))
                dve.sem_inc(arena_free, 1)
                adaln()
                for hp in range(HP):
                    ps = fill()
                    for t in range(NT):
                        top16(top_s[:, t, hp, :], top_i[:, t, hp, :], ps[:, t * P:(t + 1) * P], U(20)[:, 512:512 + P])
                    dve.sem_inc(vector_drained, 1)
                steps[vector_drained.name] += HP
                def choose(t):
                    s4 = top_s[:, t].rearrange("p (h s) e -> p h s e", s=2)
                    tt(cand.rearrange("p (h i j) -> p h i j", h=PH, i=TOPK),
                       s4[:, :, 0, :].unsqueeze(3).to_broadcast([P, PH, TOPK, TOPK]),
                       s4[:, :, 1, :].unsqueeze(2).to_broadcast([P, PH, TOPK, TOPK]), ADD)
                    for h in range(PH):
                        top16(sc[:, h * TOPK:(h + 1) * TOPK], pos[:, h * TOPK:(h + 1) * TOPK], cand[:, h * 256:(h + 1) * 256], rest)
                    done(dve.tensor_copy(iF, top_i[:, t].rearrange("p i e -> p (i e)")))
                    i4 = iF.rearrange("p (h s e) -> p h s e", h=PH, s=2)
                    for side, e_out in ((0, e1), (1, e2)):
                        if side == 0:
                            ts(pi, pos, 4, None, ALU.logical_shift_right)
                        else:
                            ts(pi, pos, 15, None, ALU.bitwise_and)
                        done(dve.tensor_copy(pf, pi))
                        o3 = onehot.rearrange("p (n c) -> p n c", c=TOPK)
                        tt(o3, iota16[:].unsqueeze(1).to_broadcast([P, P, TOPK]), bc(pf, TOPK), ALU.is_equal)
                        o4 = onehot.rearrange("p (h e c) -> p h e c", h=PH, e=TOPK)
                        tt(o4, o4, i4[:, :, side, :].unsqueeze(2).to_broadcast([P, PH, TOPK, TOPK]), MUL)
                        done(dve.tensor_reduce(e_out, o3, AXX, ADD))
                    stt(e1, e1, float(NKEYS), e2, MUL, ADD)
                    if li:
                        ts(e1, e1, float(li * NKEYS * NKEYS), None, ADD)
                    s3 = sc.rearrange("p (h e) -> p h e", h=PH)
                    below = e2 if t == SAMPLE else gate[:, t, :]
                    tt(below.rearrange("p (h e) -> p h e", h=PH), s3, s3[:, :, 0:1].to_broadcast([P, PH, TOPK]), SUB)
                    if t == SAMPLE:
                        for c in range(COPIES):
                            rr = slice(32 * c, 32 * c + 32)
                            done(dve.tensor_copy(gate[rr, t, 0:32], e2[rr, rr]))
                            done(dve.tensor_copy(idx[rr, t * P:t * P + 32], e1[rr, rr]))
                    else:
                        done(dve.tensor_copy(idx[:, t * P:(t + 1) * P], e1))
                    dve.sem_inc(experts_chosen, 1)

                def products(n, t, first, both):
                    groups = groups_of(0, both)
                    per = len(groups) * GRP
                    with dve.Fori(0, n // per) as i:
                        for k, g in enumerate(groups):
                            dve.wait_ge(rows_landed[g], i * (16 * GRP) + (rounds[g] + 1) * 16 * GRP)
                            for s in range(GRP):
                                row = ring[:, g * GRP + s, :]
                                dve.tensor_tensor_reduce(row, row, hc[:, t, :], 1.0, 0.0, MUL, ADD,
                                                         act16[:, k * GRP + s:k * GRP + s + 1]).then_inc(rows_used[g], 1)
                        for g in groups:
                            dve.wait_ge(rows_used[g], i * GRP + (rounds[g] + 1) * GRP + 1)
                        dve.tensor_copy(acts[:, t % 2, bass.ds(i * per + first, per)], act16[:, 0:per]).then_inc(acts_copied, 1)
                        dve.wait_ge(acts_copied, i + (ncopied[0] + 1))
                    ncopied[0] += n // per

                def weigh(t):
                    slots = experts_of(t)
                    nh = slots // TOPK
                    dve.sem_inc(vector_result, 1)
                    w.take(scalar_result)
                    g3 = gate[:, t, 0:slots].rearrange("p (h e) -> p h e", h=nh)
                    done(dve.tensor_reduce(s16[:, 0, 0:nh], g3, AXX, ADD))
                    done(dve.reciprocal(s16[:, 0, 0:nh], s16[:, 0, 0:nh]))
                    tt(g3, g3, bc(s16[:, 0, 0:nh], TOPK), MUL)
                    tt(acts[:, t % 2, 0:slots], acts[:, t % 2, 0:slots], gate[:, t, 0:slots], MUL)
                    dve.sem_inc(vector_result, 1)

                def add_experts(t, gain):
                    tt(peer_tmp, fill(), gain, MUL, vector_drained)
                    tt(x[:, t, :], x[:, t, :], peer_tmp, ADD)

                gain = vec()
                choose(0)
                for n, u, v, choice in SEGMENTS:
                    if choice:
                        choose(u[0])
                    both = bool(u and v)
                    if u:
                        products(n, *u, both)
                    for g in range(NGRP):
                        rounds[g] += n // (len(groups_of(0, both)) * GRP)
                    if u:
                        if u[1] + n == experts_of(u[0]):
                            weigh(u[0])
                            if u[0] == 1:
                                add_experts(0, gain)
                add_experts(1, gain)
                dve.sem_inc(vec_used, 1)
                add_experts(SAMPLE, vec(4))
                dve.sem_inc(vec_used, 1)
            norm()
            dve.sem_inc(y_ready, 1)

        @block.tensor
        def _(pe):
            w = Waits(pe)
            nfv, nfa, nw = [0], [0], [0]
            rounds = [0] * NGRP
            ndiag = [0]

            def for_vector():
                if nfv[0] >= 2:
                    pe.wait_ge(vector_drained, nfv[0] - 1)
                nfv[0] += 1
                return psv[:, (nfv[0] - 1) % 2, :]

            def for_scalar():
                if nfa[0] >= 2:
                    pe.wait_ge(scalar_drained, nfa[0] - 1)
                nfa[0] += 1
                return psa[:, (nfa[0] - 1) % 2, :]

            def scalar_copies():
                pe.wait_ge(scalar_drained, nfa[0])

            def vector_copies():
                pe.wait_ge(vector_drained, nfv[0])

            def weight():
                b = nw[0] % WBUF
                pe.wait_ge(weight_loaded[b], 16 * (nw[0] // WBUF + 1))
                nw[0] += 1
                return wring[:, b]

            def mm(out, lhsT, rhs, start=True, stop=True):
                return nc.tensor.matmul(out, lhsT, rhs, start=start, stop=stop)

            def rows_product(ps, t, wt, cols=512, at_=0):
                for k in range(KD):
                    last = mm(ps[:, at_:at_ + cols], hT[:, k, t * P:(t + 1) * P], wt[:, k, 0:cols], k == 0, k == KD - 1)
                return last

            def turn(src, ps, n=8):
                for k in range(n):
                    last = nc.tensor.transpose(ps[:, k * P:(k + 1) * P], src[:, k * P:(k + 1) * P], ident[:])
                return last

            def h_turned():
                w.take(operand_written)
                for t in range(NT):
                    turn(hc[:, t, :], for_scalar()).then_inc(psum_for_scalar, 1)

            def project_out():
                scalar_copies()
                wts = [weight(), weight()]
                for t in range(NT):
                    ps = for_vector()
                    for j in range(2):
                        last = rows_product(ps, t, wts[j], 512, j * 512)
                    last.then_inc(psum_for_vector, 1)
                pe.wait_ge(psum_for_vector, nfv[0])
                for j in range(2):
                    pe.sem_inc(weight_used, 1)

            pe.wait_ge(consts_built, 1)
            w.take(operand_written)
            ps = for_scalar()
            for k in range(KD):
                last = nc.tensor.transpose(ps[:, k * 9:(k + 1) * 9], crow[0:9, k * P:(k + 1) * P], ident[0:9, 0:9])
            last.then_inc(psum_for_scalar, 1)
            ps = for_scalar()
            for k in range(KD):
                last = nc.tensor.transpose(ps[:, k * DEC_B:(k + 1) * DEC_B], srow[0:DEC_B, k * P:(k + 1) * P], ident[0:8, 0:8])
            last.then_inc(psum_for_scalar, 1)
            nc.tensor.transpose(for_scalar()[:, 0:48], murow[0:48, :], ident[0:48, 0:48]).then_inc(psum_for_scalar, 1)
            scalar_copies()

            for li in range(2):
                for k in range(6):
                    ps = for_vector()
                    for j in range(2):
                        wt = weight()
                        for kk in range(KD):
                            last = mm(ps[0:9, j * 512:(j + 1) * 512], cT[:, kk * 9:(kk + 1) * 9], wt[:, kk, :], kk == 0, kk == KD - 1)
                        last.then_inc(weight_used if j == 0 else psum_for_vector, 1)
                    pe.wait_ge(psum_for_vector, nfv[0])
                    pe.sem_inc(weight_used, 1)
                h_turned()
                if li == 0:
                    pe.wait_ge(lora_loaded, 16 * 8)
                    for n, i in enumerate((0, 3, 1, 2, 4, 5)):
                        w.take(operand_written)
                        mx = mixb[n % 2]
                        if i < 3:
                            for j in range(2):
                                wt = weight()
                                for t in range(NT):
                                    ps = for_scalar()
                                    for k in range(KD):
                                        last = mm(ps[:, 0:512], mx[:, k, t * P:(t + 1) * P], wt[:, k, :], k == 0, k == KD - 1)
                                    last.then_inc(psum_for_scalar, 1)
                                pe.wait_ge(psum_for_scalar, nfa[0])
                                pe.sem_inc(weight_used, 1)
                        else:
                            lo, m = ((0, 64), (64, 64), (128, P))[i - 3]
                            ps = for_scalar()
                            for k in range(KD):
                                last = mm(ps[0:m, 0:TOK], lora1[:, k, lo:lo + m], mx[:, k, :], k == 0, k == KD - 1)
                            last.then_inc(psum_for_scalar, 1)
                            pe.wait_ge(psum_for_scalar, nfa[0])
                        if n < 4:
                            pe.sem_inc(mix_used, 1)
                    scalar_copies()
                    for t in range(NT):
                        sample = t == SAMPLE
                        if t:
                            scalar_copies()
                        for i in range(2):
                            ps = for_scalar()
                            for j in range(2):
                                last = mm(ps[:, j * 512:(j + 1) * 512], loraT[0:65, i, t * P:(t + 1) * P], lora2[0:65, i, j * 512:(j + 1) * 512])
                            last.then_inc(psum_for_scalar, 1)
                        scalar_copies()
                        ps = for_scalar()
                        for j in range(2):
                            last = mm(ps[:, j * 512:(j + 1) * 512], (le4 if sample else cum_mid)[:], U(0)[:, j * 512:(j + 1) * 512])
                        last.then_inc(psum_for_scalar, 1)
                        ps = for_scalar()
                        ind, nn = (seq_ind, DEC_B) if sample else (half_ind, 2)
                        for k in range(KD):
                            last = mm(ps[:, k * nn:(k + 1) * nn], U(0)[:, k * P:(k + 1) * P], ind[:])
                        last.then_inc(psum_for_scalar, 1)
                        w.take(operand_written)
                        r, y, v = cur
                        for hh in range(2):
                            o = hh * 512
                            ps = for_scalar()
                            turn(U(2)[:, o:o + 512], ps[:, 0:512], 4)
                            turn(r[:, o:o + 512], ps[:, 512:1024], 4).then_inc(psum_for_scalar, 1)
                            ps = for_scalar()
                            turn(U(1)[:, o:o + 512], ps[:, 0:512], 4)
                            turn(U(4)[:, o:o + 512], ps[:, 512:1024], 4).then_inc(psum_for_scalar, 1)
                            scalar_copies()

                            def hd(u, h):
                                return U(u)[:, h * P:(h + 1) * P]

                            def bT_(h):
                                return U(7)[:, (h // 2) * P:(h // 2 + 1) * P]

                            def kT_(h):
                                return U(7)[:, 512 + (h // 2) * P:512 + (h // 2 + 1) * P]

                            for lhs, rhs in ((bT_, lambda h: hd(5, h)), (lambda h: hd(5, h), bT_), (kT_, lambda h: hd(5, h)),
                                             (bT_, lambda h: hd(6, h)), (kT_, lambda h: hd(6, h))):
                                ps = for_vector()
                                for h in range(HALF_H):
                                    last = mm(ps[:, h * P:(h + 1) * P], lhs(h), rhs(h))
                                last.then_inc(psum_for_vector, 1)
                            levels = [1] if sample else range(1, 7)
                            for k in levels:
                                w.take(operand_written)
                                vector_copies()
                                ps = for_scalar()
                                for h in range(HALF_H):
                                    last = mm(ps[:, h * P:(h + 1) * P], hd(14, h), hd(12, h))
                                last.then_inc(psum_for_scalar, 1)
                                scalar_copies()
                                for lu, ru in ([(13, 3)] if k != levels[-1] else []) + [(3, 13)]:
                                    ps = for_vector()
                                    for h in range(HALF_H):
                                        last = mm(ps[:, h * P:(h + 1) * P], hd(lu, h), hd(ru, h))
                                    last.then_inc(psum_for_vector, 1)
                            vector_copies()
                            if sample:
                                for q in range(2):
                                    w.take(s0_loaded, 64)
                                    ps = for_scalar()
                                    for b in range(4):
                                        src = hc[0:RK, b // 2, (b % 2) * 512:(b % 2) * 512 + 512]
                                        for pr in range(PAIRS):
                                            last = nc.tensor.transpose(ps[:, b * 256 + pr * RK:b * 256 + (pr + 1) * RK],
                                                                       src[:, pr * P:(pr + 1) * P], ident[0:RK, 0:RK])
                                    last.then_inc(psum_for_scalar, 1)
                                scalar_copies()
                            s0 = U(14, 2).rearrange("p (b q v) -> p b q v", b=DEC_B, q=PAIRS)

                            def from_state(out, h, z, start, stop):
                                if sample:
                                    w.take(operand_written)
                                    am = U((12, 3)[h % 2])
                                    for b in range(DEC_B):
                                        last = mm(out, am[:, b * P:(b + 1) * P], s0[:, b, h // 2, :], start and b == 0, stop and b == 7)
                                    return last.then_inc(masked_used, 1)
                                return mm(out, hd(z, h), st_in[:, h // 2, :], start, stop)

                            if not sample:
                                w.take(operand_written)
                            ps = for_scalar()
                            for h in range(HALF_H):
                                out = ps[:, h * RK:(h + 1) * RK]
                                from_state(out, h, 5, True, False)
                                last = mm(out, hd(9, h), v[:, o + h * RK:o + (h + 1) * RK], False, True)
                            last.then_inc(psum_for_scalar, 1)
                            scalar_copies()
                            ps = for_scalar()
                            for h in range(HALF_H):
                                last = mm(ps[:, h * RK:(h + 1) * RK], hd(13, h), U(0)[:, h * RK:(h + 1) * RK])
                            last.then_inc(psum_for_scalar, 1)
                            scalar_copies()
                            sa = U(0)[:, 512:1024]
                            ps = for_scalar()
                            for h in range(HALF_H):
                                out = ps[:, h * RK:(h + 1) * RK]
                                from_state(out, h, 6, True, False)
                                mm(out, hd(10, h), sa[:, h * RK:(h + 1) * RK], False, False)
                                last = mm(out, hd(11, h), v[:, o + h * RK:o + (h + 1) * RK], False, True)
                            last.then_inc(psum_for_scalar, 1)
                            if sample:
                                for q in range(PAIRS):
                                    w.take(operand_written)
                                    ps = for_vector()
                                    ch = slice(o + q * P, o + (q + 1) * P)
                                    for e in range(2):
                                        out = ps[:, e * 512:(e + 1) * 512]
                                        mm(out, U(1)[:, ch], U(12)[:, e * 512:(e + 1) * 512], True, False)
                                        last = mm(out, U(4)[:, ch], U(3)[:, e * 512:(e + 1) * 512], False, True)
                                    last.then_inc(psum_for_vector, 1)
                                w.take(operand_written)
                                for q in range(4):
                                    ps = for_scalar()
                                    for b in range(2):
                                        for pr in range(PAIRS):
                                            last = nc.tensor.transpose(ps[0:RK, b * 512 + pr * P:b * 512 + (pr + 1) * P],
                                                                       s0[:, 2 * q + b, pr, :], ident[:])
                                    last.then_inc(psum_for_scalar, 1)
                            else:
                                ps = for_vector()
                                for h in range(HALF_H):
                                    out = ps[:, h * RK:(h + 1) * RK]
                                    ch = slice(o + (h // 2) * P, o + (h // 2 + 1) * P)
                                    mm(out, U(1)[:, ch], sa[:, h * RK:(h + 1) * RK], True, False)
                                    last = mm(out, U(4)[:, ch], v[:, o + h * RK:o + (h + 1) * RK], False, True)
                                last.then_inc(psum_for_vector, 1)
                                if t == 1:
                                    w.take(operand_written)
                                    ps = for_scalar()
                                    for pr in range(PAIRS):
                                        last = nc.tensor.transpose(ps[0:RK, pr * P:(pr + 1) * P], stateT[:, hh * PAIRS + pr, :], ident[:])
                                    last.then_inc(psum_for_scalar, 1)
                        ps = for_vector()
                        for j in range(2):
                            last = mm(ps[:, j * 512:(j + 1) * 512], loraT[:, 2, t * P:(t + 1) * P], g2[:, j * 512:(j + 1) * 512])
                        last.then_inc(psum_for_vector, 1)
                        w.take(operand_written)
                        turn(y, for_scalar()).then_inc(psum_for_scalar, 1)
                else:
                    scalar_copies()
                    for blk in range(2):
                        wt = weight()
                        for h in range(GH):
                            ps = for_scalar()
                            for k in range(KD):
                                last = mm(ps[:, 0:TOK], wt[:, k, h * P:(h + 1) * P], hT[:, k, :], k == 0, k == KD - 1)
                            last.then_inc(psum_for_scalar, 1)
                        pe.wait_ge(psum_for_scalar, nfa[0])
                        pe.sem_inc(weight_used, 1)
                    for blk in range(4):
                        wt = weight()
                        for t in range(NT):
                            rows_product(for_scalar(), t, wt).then_inc(psum_for_scalar, 1)
                        pe.wait_ge(psum_for_scalar, nfa[0])
                        pe.sem_inc(weight_used, 1)
                    wt = weight()
                    ps = for_scalar()
                    for k in range(KD):
                        last = mm(ps[0:16, 0:TOK], wt[:, k, 0:16], hT[:, k, :], k == 0, k == KD - 1)
                    last.then_inc(psum_for_scalar, 1)
                    pe.wait_ge(psum_for_scalar, nfa[0])
                    pe.sem_inc(weight_used, 1)
                    w.take(gla_small_loaded, 32)
                    for t in range(NT):
                        sample = t == SAMPLE
                        tok = slice(t * P, (t + 1) * P)
                        scalar_copies()
                        mm(for_vector()[:, 0:512], alT[0:17, tok], wa2[0:17, :]).then_inc(psum_for_vector, 1)
                        w.take(operand_written)
                        ps = for_scalar()
                        for h in range(GH):
                            last = mm(ps[:, h * P:(h + 1) * P], la[:, h * P:(h + 1) * P], (le4 if sample else le)[:])
                        last.then_inc(psum_for_scalar, 1)
                        ps = for_vector()
                        for h in range(GH):
                            last = mm(ps[:, h * P:(h + 1) * P], kT[:, h, tok], qT[:, h, tok])
                        last.then_inc(psum_for_vector, 1)
                        for k in (range(2) if sample else range(7)):
                            w.take(operand_written)
                            ps = for_vector()
                            for h in range(GH):
                                last = mm(ps[:, h * P:(h + 1) * P], ke[:, h * P:(h + 1) * P], qe[:, h * P:(h + 1) * P])
                            last.then_inc(psum_for_vector, 1)
                        w.take(operand_written)
                        turn(ke, for_scalar(), 4).then_inc(psum_for_scalar, 1)
                        scalar_copies()
                        if sample:
                            for h in range(GH):
                                w.take(operand_written)
                                pe.wait_ge(gla_state_loaded[h % 2], 16 * (h // 2 + 1))
                                s0 = gS0[h % 2].rearrange("p (b v) -> p b v", b=DEC_B)
                                vv = gv[t][:, h * GV:(h + 1) * GV]
                                out = for_vector()[:, 0:GV]
                                mm(out, at[:, h * P:(h + 1) * P], vv, True, False)
                                for b in range(DEC_B):
                                    last = mm(out, qem[:, b * P:(b + 1) * P], s0[:, b, :], False, b == DEC_B - 1)
                                last.then_inc(psum_for_vector, 1)
                                for q in range(2):
                                    ps = for_vector()
                                    for b in range(4):
                                        bb = 4 * q + b
                                        last = mm(ps[:, b * GV:(b + 1) * GV], kdm[:, bb * P:(bb + 1) * P], vv)
                                    last.then_inc(psum_for_vector, 1)
                        else:
                            ps = for_vector()
                            for h in range(GH):
                                out = ps[:, h * GV:(h + 1) * GV]
                                vv = gv[t][:, h * GV:(h + 1) * GV]
                                mm(out, at[:, h * P:(h + 1) * P], vv, True, False)
                                last = mm(out, qe[:, h * P:(h + 1) * P], gS[:, h * GV:(h + 1) * GV], False, True)
                            last.then_inc(psum_for_vector, 1)
                            ps = for_vector()
                            for h in range(GH):
                                last = mm(ps[:, h * GV:(h + 1) * GV], kd[:, h * P:(h + 1) * P], gv[t][:, h * GV:(h + 1) * GV])
                            last.then_inc(psum_for_vector, 1)
                        w.take(operand_written)
                        turn(go, for_scalar()).then_inc(psum_for_scalar, 1)
                project_out()
                h_turned()
                w.take(keys_loaded, 16)
                for i in range(2):
                    ps = for_scalar()
                    for k in range(8):
                        last = nc.tensor.transpose(ps[:, k * P:(k + 1) * P], sk[:, 8 * i + k, :], ident[:])
                    last.then_inc(psum_for_scalar, 1)
                scalar_copies()
                wt = None
                for hp in range(HP + 1):
                    if hp < HP:
                        if hp % 4 == 0:
                            wt = weight()
                        ps = for_scalar()
                        for k in range(KD):
                            last = mm(ps[:, 0:TOK], wt[:, k, (hp % 4) * P:(hp % 4 + 1) * P], hT[:, k, :], k == 0, k == KD - 1)
                        last.then_inc(psum_for_scalar, 1)
                    if hp:
                        pe.wait_ge(scalar_drained, nfa[0] - (1 if hp < HP else 0))
                        ps = for_vector()
                        for t in range(NT):
                            last = mm(ps[:, t * P:(t + 1) * P], qb[(hp - 1) % 2][:, t * P:(t + 1) * P], skT[:, hp - 1, :])
                        last.then_inc(psum_for_vector, 1)
                    if hp < HP and hp % 4 == 3:
                        pe.wait_ge(psum_for_scalar, nfa[0])
                        pe.sem_inc(weight_used, 1)
                for n, u, v, choice in SEGMENTS:
                    both = bool(u and v)
                    per = len(groups_of(1, both)) * GRP
                    if v:
                        t, first = v
                        if first == 0:
                            ps = for_vector()
                            for j in range(2):
                                mm(ps[:, j * 512:(j + 1) * 512], zeros[:], hc[:, t, j * 512:(j + 1) * 512], True, False)
                        with pe.Fori(0, n // per) as i:
                            for k, g in enumerate(groups_of(1, both)):
                                pe.wait_ge(diag_ready, i * per + (ndiag[0] + (k + 1) * GRP))
                                pe.wait_ge(rows_landed[g], i * (16 * GRP) + (rounds[g] + 1) * 16 * GRP)
                                for s in range(g * GRP, (g + 1) * GRP):
                                    for j in range(2):
                                        last = mm(ps[:, j * 512:(j + 1) * 512], diag[:, s, :], ring[:, s, j * 512:(j + 1) * 512], False, False)
                                last.then_inc(rows_used[g], GRP)
                        ndiag[0] += n
                        if first + n == experts_of(t):
                            for j in range(2):
                                last = mm(ps[:, j * 512:(j + 1) * 512], zeros[:], hc[:, t, j * 512:(j + 1) * 512], False, True)
                            last.then_inc(psum_for_vector, 1)
                    for g in range(NGRP):
                        rounds[g] += n // per


_INS = ["x_prompt", "x_sample", "state_rwkv_S", "state_rwkv_shift", "state_gla_S", "c_prompt", "c_sample",
        "ada_w", "ada_b", "norm1_g", "norm2_g", "final_g",
        "rw_mu", "rw_w_rkv", "rw_w0", "rw_w1", "rw_w2", "rw_a0", "rw_a1", "rw_a2", "rw_g1", "rw_g2",
        "rw_kk", "rw_ka", "rw_rk", "rw_lnx_w", "rw_lnx_b", "rw_wo",
        "gla_w_in", "gla_wa2", "gla_ba", "gla_gnorm", "gla_wo",
        "peer_wq", "peer_subkeys", "peer_u", "peer_v"]
_OUTS = [(1, 256, 1024), (8, 4, 1024), (1, 1, 16, 64, 64), (1, 1, 1024), (1, 1, 4, 128, 256),
         (1, 8, 16, 64, 64), (1, 8, 1024), (1, 8, 4, 128, 256)]


def kernel(**inputs):
    import numpy as np
    import concourse.bacc as bacc
    from concourse.bass_utils import run_bass_kernel_spmd

    nc = bacc.Bacc("TRN2", target_bir_lowering=False, num_devices=1)
    arrays, aps = {}, {}
    for name in _INS:
        v = np.ascontiguousarray(inputs[name])
        arrays["in_" + name] = v
        aps[name] = nc.dram_tensor("in_" + name, v.shape, mybir.dt.from_np(v.dtype), kind="ExternalInput").ap()
    outs = [nc.dram_tensor(f"out_{i}", s, F32, kind="ExternalOutput").ap() for i, s in enumerate(_OUTS)]
    program(nc, aps, outs)
    r = run_bass_kernel_spmd(nc, [arrays], core_ids=[0])
    return tuple(r.results[0][f"out_{i}"] for i in range(len(_OUTS)))
```

```python
from contextlib import ExitStack

import concourse.bass as bass
from concourse import mybir

F32 = mybir.dt.float32
I32 = mybir.dt.int32
U32 = mybir.dt.uint32
ALU = mybir.AluOpType
ACT = mybir.ActivationFunctionType
AXX = mybir.AxisListType.X

P = 128
D = 1024
KD = D // P
NT = 3
TOK = NT * P
SAMPLE = 2
DEC_B, DEC_T = 8, 4
COPIES = P // (DEC_B * DEC_T)
RH, RK = 16, 64
HALF_H = RH // 2
PAIRS = HALF_H // 2
GH, GK, GV = 4, 128, 256
TAU = 16.0
PH, NKEYS, TOPK = 8, 128, 16
HP = 2 * PH
EPS = 1e-6
LNX_EPS = 64e-5
DECAY_C = 0.6065306597126334
LOWEST = -3.0e38
WBUF = 2
VBUF = 3
GRP, NGRP = 4, 4
RING = GRP * NGRP
SHORT = P // COPIES
SEGMENTS = (
    (P // 4, (0, 0), None, False),
    (P // 4, (0, P // 4), None, False),
    (P // 4, (0, P // 2), None, False),
    (P // 4, (0, 3 * P // 4), None, False),
    (32, None, (0, 0), False),
    (P - 32, (1, 0), (0, 32), True),
    (32, (1, P - 32), None, False),
    (32, None, (1, 0), False),
    (SHORT, (SAMPLE, 0), (1, 32), True),
    (P - 32 - SHORT, None, (1, 32 + SHORT), False),
    (SHORT, None, (SAMPLE, 0), False),
)

SCORE_BLOCKS = (2, 3, 0, 1)


def experts_of(t):
    return SHORT if t == SAMPLE else P


def groups_of(side, both):
    return range(2 * side, 2 * side + 2) if both else range(NGRP)


class Waits:

    def __init__(self, eng):
        self.eng, self.n = eng, {}

    def take(self, sem, k=1):
        self.n[sem.name] = self.n.get(sem.name, 0) + k
        self.eng.wait_ge(sem, self.n[sem.name])


def program(nc, a, outs):
    (y_p, y_s, S_p, sh_p, G_p, S_s, sh_s, G_s) = outs
    with ExitStack() as ctx:
        def sb(name, shape, dt=F32):
            return ctx.enter_context(nc.sbuf_tensor(name, shape, dt))

        def sem(name):
            return ctx.enter_context(nc.semaphore(name))

        mod_d = nc.dram_tensor("mod_d", (2, 6, 9, D), F32, kind="Internal").ap()
        rkv_d = nc.dram_tensor("rkv_d", (3, NT, P, D), F32, kind="Internal").ap()

        x = sb("x", [P, NT, D])
        hc = sb("hc", [P, NT, D])
        hT = sb("hT", [P, KD, TOK])
        wring = sb("wring", [P, WBUF, KD, 512])
        wx = sb("wx", [P, 4, D])
        vring = sb("vring", [P, VBUF, D])
        arena = sb("arena", [P, 23680])
        ident = sb("ident", [P, P])
        zeros = sb("zeros", [P, P])
        le = sb("le", [P, P])
        le4 = sb("le4", [P, P])
        lt = sb("lt", [P, P])
        lt4 = sb("lt4", [P, P])
        cum_mid = sb("cum_mid", [P, P])
        low0 = sb("low0", [P, P])
        rep32 = sb("rep32", [P, P])
        lev = sb("lev", [P, 7, P])
        half_ind = sb("half_ind", [P, 2])
        seq_ind = sb("seq_ind", [P, DEC_B])
        own_seq = sb("own_seq", [P, DEC_B])
        iota16 = sb("iota16", [P, TOPK])
        cT = sb("cT", [P, KD * 9])
        muT = sb("muT", [P, 48])
        shiftT = sb("shiftT", [P, KD * DEC_B])
        rstd = sb("rstd", [P, 4])
        s16 = sb("s16", [P, 2, RH])
        bonus = sb("bonus", [P, RH])
        pcs = sb("pcs", [P, KD, DEC_B])
        stateT = sb("stateT", [P, KD, RK])
        st_in = sb("st_in", [P, KD, RK])
        acts = sb("acts", [P, 2, P])
        act16 = sb("act16", [P, RING])
        idx_grp = sb("idx_grp", [P, RING], U32)

        def U(i, n=1):
            return arena[:, i * D:(i + n) * D]

        def W(off, n):
            return arena[:, off:off + n]

        def heads(ap, h, w):
            return ap.rearrange("p (h w) -> p h w", h=h)

        psv = ctx.enter_context(nc.psum_tensor("psv", [P, 2, D], F32))
        psa = ctx.enter_context(nc.psum_tensor("psa", [P, 2, D], F32))

        pool_consts = sem("pool_consts")
        consts_built = sem("consts_built")
        small_loaded = sem("small_loaded")
        x_loaded = sem("x_loaded")
        psum_for_vector = sem("psum_for_vector")
        psum_for_scalar = sem("psum_for_scalar")
        vector_drained = sem("vector_drained")
        scalar_drained = sem("scalar_drained")
        vector_step = sem("vector_step")
        scalar_step = sem("scalar_step")
        operand_written = sem("operand_written")
        vector_result = sem("vector_result")
        scalar_result = sem("scalar_result")
        weight_loaded = [sem(f"weight_loaded{i}") for i in range(WBUF)]
        weight_used = sem("weight_used")
        vec_loaded = [sem(f"vec_loaded{i}") for i in range(VBUF)]
        vec_used = sem("vec_used")
        mod_ready = sem("mod_ready")
        mod_stored = [sem(f"mod_stored{i}") for i in range(2)]
        next_mod_ready = sem("next_mod_ready")
        next_mod_stored = sem("next_mod_stored")
        norm_done = sem("norm_done")
        shift_stored = sem("shift_stored")
        mix_used = sem("mix_used")
        lora_loaded = sem("lora_loaded")
        spilled = [sem(f"spilled{i}") for i in range(3)]
        all_spilled = sem("all_spilled")
        cur_loaded = sem("cur_loaded")
        cur_used = sem("cur_used")
        s0_loaded = sem("s0_loaded")
        s0_used = sem("s0_used")
        state_stored = [sem(f"state_stored{i}") for i in range(2)]
        gla_small_loaded = sem("gla_small_loaded")
        gla_state_loaded = [sem(f"gla_state_loaded{i}") for i in range(2)]
        gla_state_new = sem("gla_state_new")
        gla_state_stored = [sem(f"gla_state_stored{i}") for i in range(2)]
        gla_prompt_stored = sem("gla_prompt_stored")
        arena_free = sem("arena_free")
        keys_loaded = sem("keys_loaded")
        experts_chosen = sem("experts_chosen")
        idx_copied = sem("idx_copied")
        pool_passed = sem("pool_passed")
        rows_landed = [sem(f"rows_landed{i}") for i in range(NGRP)]
        rows_used = [sem(f"rows_used{i}") for i in range(NGRP)]
        acts_copied = sem("acts_copied")
        diag_ready = sem("diag_ready")
        y_ready = sem("y_ready")
        y_stored = sem("y_stored")
        gla_prompt_new = sem("gla_prompt_new")

        block = ctx.enter_context(nc.Block())

        xx, lora1 = W(0, 3 * D).rearrange("p (k t) -> p k t", k=KD), W(9 * D, 2 * D).rearrange("p (k t) -> p k t", k=KD)
        mixb = [W((3 + 3 * i) * D, 3 * D).rearrange("p (k t) -> p k t", k=KD) for i in range(2)]
        spill_buf = [W(11 * D + 512 * i, 512) for i in range(3)]
        cur = [U(16 + i) for i in range(3)]
        lora2 = U(19, 2).rearrange("p (i n) -> p i n", i=2)
        g2 = U(21)
        loraT = W(22 * D, 3 * TOK).rearrange("p (i t) -> p i t", i=3)
        halves = [dict(atz=U(5), rtz=U(6), turned=U(7), nt=U(8), ak=U(9), rb=U(10), rk=U(11),
                       t=U(12), tt=U(13), lt=U(14), z=U(3), rhs=U(0)),
                  dict(atz=wx[:, 0, :], rtz=wx[:, 1, :], turned=U(16), nt=wx[:, 2, :], ak=wx[:, 3, :], rb=hc[:, 0, :], rk=hc[:, 1, :],
                       t=hc[:, 2, :], tt=U(15), lt=U(7), z=U(2), rhs=U(16))]
        modrow = [U(0), U(1)]
        crow, srow, murow = U(2), U(3), W(4 * D, P)
        qT = W(0, 4 * TOK).rearrange("p (h t) -> p h t", h=GH)
        kT = W(4 * TOK, 4 * TOK).rearrange("p (h t) -> p h t", h=GH)
        gv = [U(3 + t) for t in range(NT)]
        gr = [U(6 + t) for t in range(NT)]
        la, bT = W(9 * D, 512), W(9 * D + 512, 512)
        ex, df = W(10 * D, 512), W(10 * D + 512, 512)
        qe, ke = W(11 * D, 512), W(11 * D + 512, 512)
        at, atmp = W(12 * D, 512), W(12 * D + 512, 512)
        kd = W(13 * D, 512)
        go = U(14)
        gS = U(15)
        gS0 = [U(16, 2), U(18, 2)]
        qem, kdm = U(20), U(21)
        alT, wa2 = W(22 * D, TOK), W(22 * D + TOK, 512)
        ebt = W(13 * D + 512, GH * DEC_B)
        ring = U(0, 16).rearrange("p (s n) -> p s n", s=RING)
        skT = U(16, 2).rearrange("p (i n) -> p i n", i=HP)
        qa = [U(0)[:, 0:512], U(0)[:, 512:1024]]
        qb = [wx[:, 3, 0:256], wx[:, 3, 256:512]]
        sk = U(19, 2).rearrange("p (i k) -> p i k", i=HP)
        diag = U(19, 2).rearrange("p (s k) -> p s k", s=RING)
        top_s = W(21 * D, NT * 256).rearrange("p (t i e) -> p t i e", t=NT, i=HP)
        top_i = W(21 * D + NT * 256, NT * 256).bitcast(U32).rearrange("p (t i e) -> p t i e", t=NT, i=HP)
        peer_tmp = U(16)
        cand = wx[:, 0:2, :].rearrange("p u n -> p (u n)")
        onehot = cand
        small = [U(18)[:, P * i:P * (i + 1)] for i in range(8)]
        scratch, sc, pf, e1, e2 = small[0:5]
        pos, pi = small[5].bitcast(U32), small[6].bitcast(U32)
        rest, iF = wx[:, 2, 0:256], wx[:, 2, 256:512]
        gate = W(22 * D + 512, NT * P).rearrange("p (t e) -> p t e", t=NT)
        idx = wx[:, 3, 512:512 + NT * P + 16].bitcast(U32)

        def diag_blocks(dst):
            return bass.AP(tensor=dst.tensor, offset=dst.offset,
                           ap=[list(dst.ap[0]), [P + DEC_T, DEC_B], [DEC_B * DEC_T, COPIES], [1, DEC_T]])

        def blocks(ap, m, odd):
            return ap.rearrange("p (b two m) -> p b two m", two=2, m=m)[:, :, odd, :]

        def compact(ap, m):
            return ap.rearrange("p (b m) -> p b m", m=m)

        def own_rows(src):
            return src.rearrange("p (c b i) -> p b c i", c=COPIES, b=DEC_B)

        @block.sync
        def _(sp):
            w = Waits(sp)
            n = [0]

            def weight(src):
                b = n[0] % WBUF
                if n[0] >= WBUF:
                    w.take(weight_used)
                cols = src.shape[1]
                sp.dma_start(wring[:, b, :, 0:cols], src.rearrange("(k p) n -> p k n", p=P)).then_inc(weight_loaded[b], 16)
                n[0] += 1

            sp.dma_start(crow[0:1, :], a["c_prompt"]).then_inc(small_loaded, 16)
            sp.dma_start(crow[1:9, :], a["c_sample"]).then_inc(small_loaded, 16)
            sp.dma_start(srow[0:8, :], a["state_rwkv_shift"][0]).then_inc(small_loaded, 16)
            sp.dma_start(murow[0:48, :], a["rw_mu"][0].rearrange("i (k p) -> (i k) p", p=P)).then_inc(small_loaded, 16)
            xs = a["x_sample"].rearrange("b t d -> (b t) d")
            for t in range(2):
                sp.dma_start(x[:, t, :], a["x_prompt"][0, t * P:(t + 1) * P, :]).then_inc(x_loaded, 16)
            for c in range(COPIES):
                sp.dma_start(x[32 * c:32 * c + 32, SAMPLE, :], xs).then_inc(x_loaded, 16)
            def ada(li, blocks):
                for j in blocks:
                    weight(a["ada_w"][li][:, j * 512:(j + 1) * 512])

            ada(0, range(12))
            for li in range(2):
                if li == 0:
                    w.take(arena_free)
                    for src, lo in ((a["rw_w1"], 0), (a["rw_a1"], 64), (a["rw_g1"], 128)):
                        cols = src.shape[2]
                        sp.dma_start(lora1[:, :, lo:lo + cols], src[0].rearrange("(k p) n -> p k n", p=P)).then_inc(lora_loaded, 16)
                    for i, (m, b) in enumerate((("rw_w2", "rw_w0"), ("rw_a2", "rw_a0"))):
                        sp.dma_start(lora2[0:64, i, :], a[m][0]).then_inc(lora_loaded, 16)
                        sp.dma_start(lora2[64:65, i, :], a[b]).then_inc(lora_loaded, 16)
                    sp.dma_start(g2, a["rw_g2"][0]).then_inc(lora_loaded, 16)
                    w.take(norm_done)
                    sp.dma_start(sh_p[0], hc[P - 1:P, 1, :]).then_inc(shift_stored, 16)
                    sp.dma_start(sh_s[0], hc[DEC_T - 1:DEC_B * DEC_T:DEC_T, SAMPLE, :]).then_inc(shift_stored, 16)
                    for i in (0, 1, 2):
                        for j in range(2):
                            weight(a["rw_w_rkv"][0, i][:, j * 512:(j + 1) * 512])
                    ada(1, (0, 1))
                    w.take(all_spilled)
                    for t in range(NT):
                        if t:
                            w.take(cur_used)
                        for i in range(3):
                            sp.dma_start(cur[i], rkv_d[i, t]).then_inc(cur_loaded, 16)
                        if t < SAMPLE:
                            ada(1, range(4 * t + 2, 4 * t + 6))
                        if t == SAMPLE:
                            w.take(shift_stored, 32)
                            for hh in range(2):
                                for q in range(2):
                                    if hh or q:
                                        w.take(s0_used)
                                    for b in range(4):
                                        sp.dma_start(
                                            hc[0:RK, 0:2, :].rearrange("v u (c n) -> v (u c) n", c=2)[:, b, :].rearrange("v (h k) -> v h k", k=RK),
                                            a["state_rwkv_S"][0, 4 * q + b, hh * HALF_H:(hh + 1) * HALF_H].rearrange("h v k -> v h k"),
                                        ).then_inc(s0_loaded, 16)
                                    if hh == 0 and q == 0:
                                        ada(1, (10, 11))
                                        for j in range(2):
                                            weight(a["rw_wo"][0][:, j * 512:(j + 1) * 512])
                else:
                    for j in range(6):
                        if j == 2:
                            w.take(norm_done)
                            sp.dma_start(wa2[0:16, :], a["gla_wa2"][0]).then_inc(gla_small_loaded, 16)
                            sp.dma_start(wa2[16:17, :], a["gla_ba"]).then_inc(gla_small_loaded, 16)
                        weight(a["gla_w_in"][0][:, j * 512:(j + 1) * 512])
                    weight(a["gla_w_in"][0][:, 3072:3088])
                    for j in range(2):
                        weight(a["gla_wo"][0][:, j * 512:(j + 1) * 512])
                    def gla_state(b):
                        return gS0[b].rearrange("p (b v) -> p b v", b=DEC_B)

                    for h in range(GH + 2):
                        if h == 2:
                            w.take(gla_prompt_new)
                            sp.dma_start(G_p[0, 0].rearrange("h k v -> k h v"), gS.rearrange("p (h v) -> p h v", h=GH)).then_inc(gla_prompt_stored, 16)
                        if h >= 2:
                            w.take(gla_state_new)
                            sp.dma_start(G_s[0, :, h - 2].rearrange("b k v -> k b v"), gla_state(h % 2)).then_inc(gla_state_stored[h % 2], 16)
                        if h < GH:
                            if h >= 2:
                                w.take(gla_state_stored[h % 2], 16)
                            sp.dma_start(gla_state(h % 2), a["state_gla_S"][0, :, h].rearrange("b k v -> k b v")).then_inc(gla_state_loaded[h % 2], 16)
                w.take(arena_free)
                sp.dma_start(sk[:, :, :], a["peer_subkeys"][li].rearrange("h s n k -> n (h s) k")).then_inc(keys_loaded, 16)
                for j in (*range(4), *SCORE_BLOCKS[2:]):
                    weight(a["peer_wq"][li][:, j * 512:(j + 1) * 512])
            w.take(y_ready)
            sp.dma_start(y_p[0].rearrange("(t p) d -> p t d", p=P), hc[:, 0:2, :]).then_inc(y_stored, 16)
            sp.dma_start(y_s.rearrange("b t d -> (b t) d"), hc[0:32, SAMPLE, :]).then_inc(y_stored, 16)
            sp.wait_ge(y_stored, 32)
            sp.wait_ge(shift_stored, 32)
            sp.wait_ge(gla_prompt_stored, 16)
            sp.wait_ge(gla_state_stored[0], 32)
            sp.wait_ge(gla_state_stored[1], 32)

        @block.gpsimd
        def _(pool):
            w = Waits(pool)
            nv = [0]
            rounds = [0] * NGRP
            ncopy = [0]

            def vec(src, sample=False):
                b = nv[0] % VBUF
                if nv[0] >= VBUF:
                    w.take(vec_used)
                nv[0] += 1
                if sample:
                    for c in range(COPIES):
                        pool.dma_start(vring[32 * c:32 * c + 32, b, :],
                                       src[1:9, :].unsqueeze(1).to_broadcast([DEC_B, DEC_T, D])).then_inc(vec_loaded[b], 16)
                else:
                    nn = src.shape[1]
                    pool.dma_start(vring[:, b, 0:nn], src.to_broadcast([P, nn])).then_inc(vec_loaded[b], 16)

            def row(name, i=0):
                return a[name][i:i + 1, :]

            pool.memset(zeros[:], 0.0).then_inc(pool_consts, 1)
            pool.memset(ident[:], 0.0).then_inc(pool_consts, 1)
            pool.wait_ge(pool_consts, 2)
            pool.affine_select(out=ident[:], in_=ident[:], compare_op=ALU.not_equal, fill=1.0, base=0,
                               pattern=[[-1, P]], channel_multiplier=1).then_inc(pool_consts, 1)
            pool.iota(U(5)[:, 0:P].bitcast(I32), [[1, P]], base=0, channel_multiplier=0).then_inc(pool_consts, 1)
            pool.iota(U(5)[:, P:2 * P].bitcast(I32), [[0, P]], base=0, channel_multiplier=1).then_inc(pool_consts, 1)

            def norm_vecs(name, li, k):
                vec(row(name, li))
                for s in (False, True):
                    vec(mod_d[li, k + 1] if s else mod_d[li, k + 1, 0:1], s)
                    vec(mod_d[li, k] if s else mod_d[li, k, 0:1], s)

            u_rows = a["peer_u"].rearrange("l n d -> (l n) d")
            v_rows = a["peer_v"].rearrange("l n d -> (l n) d")

            def gather(n, u, v):
                both = bool(u and v)
                sides = [(side, tab, *which) for side, tab, which in ((0, u_rows, u), (1, v_rows, v)) if which]
                turns = sorted((k, side, g, tab, t, first) for side, tab, t, first in sides
                               for k, g in enumerate(groups_of(side, both)))
                per = len(turns) // len(sides) * GRP
                with pool.Fori(0, n // per) as i:
                    for m, (k, side, g, tab, t, first) in enumerate(turns):
                        pool.wait_ge(rows_used[g], i * GRP + (rounds[g] * GRP + 1))
                        pool.sem_inc(pool_passed, 1)
                        pool.tensor_copy(idx_grp[:, g * GRP:(g + 1) * GRP],
                                         idx[:, bass.ds(i * per + (t * P + first + k * GRP), GRP)]).then_inc(idx_copied, 1)
                        pool.wait_ge(idx_copied, i * NGRP + (ncopy[0] + m + 1))
                        pool.sem_inc(pool_passed, 1)
                        for s in range(g * GRP, (g + 1) * GRP):
                            pool.indirect_dma_start(ring[:, s, :], None, tab,
                                                    bass.IndirectOffsetOnAxis(idx_grp[:, s:s + 1], 0)).then_inc(rows_landed[g], 16)
                for g in range(NGRP):
                    rounds[g] += n // per
                ncopy[0] += NGRP * (n // per)

            for k in range(6):
                vec(a["ada_b"][0:1, k * D:(k + 1) * D])
            for li in range(2):
                if li == 0:
                    for i in range(2):
                        w.take(mod_stored[i], 3 * 16)
                else:
                    w.take(next_mod_stored, 6 * 16)
                norm_vecs("norm1_g", li, 0)
                for t in range(NT):
                    if li == 0:
                        for name in ("rw_kk", "rw_ka", "rw_rk", "rw_lnx_w", "rw_lnx_b"):
                            if name == "rw_lnx_w":
                                for k in (2 * t, 2 * t + 1):
                                    vec(a["ada_b"][1:2, k * D:(k + 1) * D])
                            vec(a["rw_rk"].rearrange("r h k -> r (h k)") if name == "rw_rk" else row(name))
                    else:
                        vec(row("gla_gnorm"))
                vec(mod_d[li, 2, 0:1])
                vec(mod_d[li, 2], True)
                norm_vecs("norm2_g", li, 3)
                vec(mod_d[li, 5, 0:1])
                w.take(experts_chosen)
                for n, u, v, choice in SEGMENTS:
                    if choice:
                        w.take(experts_chosen)
                    gather(n, u, v)
                vec(mod_d[li, 5], True)
            vec(a["final_g"].rearrange("(o n) -> o n", o=1))

        @block.scalar
        def _(act):
            w = Waits(act)
            steps = {}
            nf = [0]
            nsp = [0]
            rounds = [0] * NGRP
            nst = [0, 0]
            first_bias = 6 + 5 + 3

            def done(ins, s=None):
                s = s or scalar_step
                steps[s.name] = steps.get(s.name, 0) + 1
                ins.then_inc(s, 1)
                act.wait_ge(s, steps[s.name])

            def fill():
                w.take(psum_for_scalar)
                nf[0] += 1
                return psa[:, (nf[0] - 1) % 2, :]

            def copy_out(dst, cols, rows=P, func=ACT.Copy, scale=1.0):
                ps = fill()
                src = ps[0:rows, 0:cols]
                if len(dst.shape) == 3:
                    src = src.rearrange("p (x y) -> p x y", y=dst.shape[2])
                done(act.activation(dst, src, func, scale=scale), scalar_drained)

            def root(dst, src):
                w.take(vector_result)
                done(act.activation(dst, src, ACT.Sqrt))
                act.sem_inc(scalar_result, 1)

            w.take(small_loaded, 64)
            done(act.activation(crow[0:9, :], crow[0:9, :], ACT.Silu))
            act.sem_inc(operand_written, 1)
            copy_out(cT[:, :], KD * 9)
            copy_out(shiftT[:, :], KD * DEC_B)
            copy_out(muT[:, :], 48)
            act.sem_inc(arena_free, 1)

            def to_hT(t):
                copy_out(hT[:, :, t * P:(t + 1) * P], D)

            for k in range(6):
                w.take(mod_ready)
                act.dma_start(mod_d[0, k], modrow[k % 2][0:9, :]).then_inc(mod_stored[k % 2], 16)
            for li in range(2):
                root(rstd[:, 0:3], rstd[:, 0:3])
                for t in range(NT):
                    to_hT(t)
                if li == 0:
                    act.sem_inc(scalar_result, 1)

                    def spill(i):
                        for j in range(2):
                            for t in range(NT):
                                b = nsp[0] % 3
                                if nsp[0] >= 3:
                                    act.wait_ge(spilled[b], 16 * (nsp[0] // 3))
                                copy_out(spill_buf[b], 512)
                                act.dma_start(rkv_d[i, t][:, j * 512:(j + 1) * 512], spill_buf[b]).then_inc(spilled[b], 16)
                                nsp[0] += 1

                    spill(0)
                    copy_out(loraT[0:64, 0, :], TOK, 64, ACT.Tanh)
                    spill(1)
                    spill(2)
                    copy_out(loraT[0:64, 1, :], TOK, 64)
                    copy_out(loraT[:, 2, :], TOK, P, ACT.Sigmoid)
                    for b in range(3):
                        act.wait_ge(spilled[b], 16 * 6)
                    act.sem_inc(all_spilled, 1)
                    act.sem_inc(scalar_result, 1)
                    for t in range(NT):
                        sample = t == SAMPLE
                        copy_out(U(0), D, func=ACT.Sigmoid)
                        copy_out(U(1), D, func=ACT.Sigmoid)
                        ps = fill()
                        done(act.activation(U(5), ps, ACT.Exp, scale=-DECAY_C))
                        done(act.activation(U(6), ps, ACT.Exp, scale=DECAY_C), scalar_drained)
                        nn = DEC_B if sample else 2
                        copy_out(pcs[:, :, 0:nn], KD * nn, func=ACT.Exp, scale=-DECAY_C)
                        done(act.activation(U(7), U(0), ACT.Exp, scale=DECAY_C))
                        act.sem_inc(scalar_result, 1)
                        root(s16[:, 0, :], s16[:, 0, :])
                        w.take(vector_result)
                        def turned(b):
                            ps = fill()
                            for i, name in enumerate(("atz", "rtz")):
                                z = b[name].rearrange("p (q e t) -> p q e t", q=PAIRS, e=2)
                                for e in range(2):
                                    r0 = 64 * e
                                    ins = act.activation(z[r0:r0 + 64, :, e, :],
                                                         ps[r0:r0 + 64, i * 512:(i + 1) * 512].rearrange("p (q t) -> p q t", q=PAIRS), ACT.Copy)
                                    done(ins, scalar_drained if i and e else None)
                            copy_out(b["turned"], D)

                        def store_next_mod():
                            for k in (2 * t, 2 * t + 1):
                                w.take(next_mod_ready)
                                act.dma_start(mod_d[1, k], vring[0:9, (first_bias + 7 * t + k % 2) % VBUF, :]).then_inc(next_mod_stored, 16)

                        if not sample:
                            for b in halves:
                                turned(b)
                            store_next_mod()
                            for b in halves:
                                copy_out(b["rhs"][:, 0:512], 512)
                            for k in range(1, 7):
                                for b in halves:
                                    copy_out(b["z"], D)
                            for b in halves:
                                copy_out(b["rhs"][:, 512:1024], 512)
                            for hh in range(2):
                                copy_out(cur[1][:, hh * 512:(hh + 1) * 512], 512)
                            if t == 1:
                                copy_out(U(8)[0:RK, :], D, RK)
                                act.dma_start(S_p[0, 0].rearrange("h v k -> v h k"),
                                              U(8)[0:RK, :].rearrange("v (h k) -> v h k", k=RK)).then_inc(state_stored[0], 16)
                                nst[0] += 16
                                act.wait_ge(state_stored[0], nst[0])
                            act.sem_inc(scalar_result, 1)
                        for hh in (range(2) if sample else ()):
                            turned(halves[0])
                            if hh == 0:
                                store_next_mod()
                            copy_out(U(3), D)
                            for q in range(2):
                                copy_out(U(14, 2).rearrange("p (q n) -> p q n", q=2)[:, q, :], D)
                                act.sem_inc(s0_used, 1)
                            act.sem_inc(scalar_result, 1)
                            copy_out(U(0)[:, 512:1024], 512)
                            act.sem_inc(scalar_result, 1)
                            for q in range(4):
                                i = q % 2
                                if nst[i]:
                                    act.wait_ge(state_stored[i], nst[i])
                                copy_out(U(8 + i)[0:RK, :], D, RK)
                                for b in range(2):
                                    act.dma_start(S_s[0, 2 * q + b, hh * HALF_H:(hh + 1) * HALF_H].rearrange("h v k -> v h k"),
                                                  U(8 + i)[0:RK, b * 512:(b + 1) * 512].rearrange("v (h k) -> v h k", k=RK)).then_inc(state_stored[i], 16)
                                    nst[i] += 16
                            for i in range(2):
                                if nst[i]:
                                    act.wait_ge(state_stored[i], nst[i])
                            act.sem_inc(scalar_result, 1)
                        root(s16[:, 1, :], s16[:, 1, :])
                        to_hT(t)
                        act.sem_inc(cur_used, 1)
                        act.sem_inc(scalar_result, 1)
                else:
                    for h in range(GH):
                        copy_out(qT[:, h, :], TOK, scale=GK ** -0.5)
                    for h in range(GH):
                        copy_out(kT[:, h, :], TOK)
                    for j in range(2):
                        for t in range(NT):
                            copy_out(gv[t][:, j * 512:(j + 1) * 512], 512)
                    for j in range(2):
                        for t in range(NT):
                            copy_out(gr[t][:, j * 512:(j + 1) * 512], 512, func=ACT.Silu)
                    w.take(vector_result)
                    copy_out(alT[0:16, :], TOK, 16)
                    act.sem_inc(scalar_result, 1)
                    for t in range(NT):
                        sample = t == SAMPLE
                        w.take(vector_result)
                        done(act.activation(ex, ex, ACT.Exp, scale=-1.0))
                        act.sem_inc(scalar_result, 1)
                        w.take(vector_result)
                        done(act.activation(ex, ex, ACT.Ln))
                        act.sem_inc(scalar_result, 1)
                        copy_out(bT, 512, scale=1.0 / TAU)
                        act.sem_inc(scalar_result, 1)
                        for k in (range(2) if sample else range(7)):
                            m = 1 << k
                            w.take(vector_result)
                            d3 = df.rearrange("p (b m) -> p b m", m=2 * m)
                            e3 = ex.rearrange("p (b m) -> p b m", m=2 * m)
                            done(act.activation(e3[:, :, m:2 * m], d3[:, :, m:2 * m], ACT.Exp))
                            done(act.activation(e3[:, :, 0:m], d3[:, :, 0:m], ACT.Exp, scale=-1.0))
                            act.sem_inc(scalar_result, 1)
                        w.take(vector_result)
                        done(act.activation(ex, bT, ACT.Exp))
                        done(act.activation(df, df, ACT.Exp))
                        nb = DEC_B if sample else 1
                        src = bT.rearrange("p (h s i) -> p h s i", h=GH, i=DEC_T)[:, :, 0:DEC_B, DEC_T - 1] if sample else \
                            bT.rearrange("p (h s) -> p h s", h=GH)[:, :, P - 1:P]
                        done(act.activation(ebt.rearrange("p (h b) -> p h b", h=GH)[:, :, 0:nb], src, ACT.Exp))
                        act.sem_inc(scalar_result, 1)
                        copy_out(kd, 512)
                        act.sem_inc(scalar_result, 1)
                        root(rstd[:, 0:4], rstd[:, 0:4])
                        to_hT(t)
                        act.sem_inc(scalar_result, 1)
                root(rstd[:, 0:3], rstd[:, 0:3])
                for t in range(NT):
                    to_hT(t)
                for i in range(2):
                    copy_out(skT[:, 8 * i:8 * i + 8, :], D)
                for blk in range(4):
                    copy_out(qa[blk % 2], 512)
                for hp in range(HP):
                    copy_out(qb[hp % 2], 2 * P)
                def diagonals(n, t, first, both):
                    groups = groups_of(1, both)
                    per = len(groups) * GRP
                    with act.Fori(0, n // per) as i:
                        for k, g in enumerate(groups):
                            act.wait_ge(rows_used[g], i * GRP + (rounds[g] * GRP + 1))
                            for s in range(GRP):
                                act.activation(diag[:, g * GRP + s, :], rep32[:, :] if t == SAMPLE else ident[:, :], ACT.Copy,
                                               scale=acts[:, t % 2, bass.ds(i * per + (first + k * GRP + s), 1)]).then_inc(diag_ready, 1)

                for n, u, v, choice in SEGMENTS:
                    both = bool(u and v)
                    if v:
                        diagonals(n, *v, both)
                    for g in range(NGRP):
                        rounds[g] += n // (len(groups_of(0, both)) * GRP)
                    if u and u[1] + n == experts_of(u[0]):
                        t, slots = u[0], experts_of(u[0])
                        w.take(vector_result)
                        done(act.activation(gate[:, t, 0:slots], gate[:, t, 0:slots], ACT.Exp))
                        done(act.activation(acts[:, t % 2, 0:slots], acts[:, t % 2, 0:slots], ACT.Gelu))
                        act.sem_inc(scalar_result, 1)
                        w.take(vector_result)
            root(rstd[:, 0:3], rstd[:, 0:3])

        @block.vector
        def _(dve):
            w = Waits(dve)
            steps = {}
            nf = [0]
            nv = [0]
            vd = [0] * VBUF
            rounds = [0] * NGRP
            ncopied = [0]
            am_made = [0]

            def done(ins, s=None):
                s = s or vector_step
                steps[s.name] = steps.get(s.name, 0) + 1
                ins.then_inc(s, 1)
                dve.wait_ge(s, steps[s.name])

            def tt(out, i0, i1, op, s=None):
                done(dve.tensor_tensor(out, i0, i1, op), s)

            def ts(out, i0, a1, a2, o0, o1=None, s=None):
                done(dve.tensor_scalar(out, i0, a1, a2, o0, o1) if o1 is not None else dve.tensor_scalar(out, i0, a1, None, o0), s)

            def stt(out, i0, sc, i1, o0, o1, s=None):
                done(dve.scalar_tensor_tensor(out=out, in0=i0, scalar=sc, in1=i1, op0=o0, op1=o1), s)

            def fill():
                w.take(psum_for_vector)
                nf[0] += 1
                return psv[:, (nf[0] - 1) % 2, :]

            def vec(k=1):
                b = nv[0] % VBUF
                vd[b] += 16 * k
                dve.wait_ge(vec_loaded[b], vd[b])
                nv[0] += 1
                return vring[:, b, :]

            MUL, ADD, SUB = ALU.mult, ALU.add, ALU.subtract

            w.take(pool_consts, 5)
            ci, ri = U(5)[:, 0:P].bitcast(I32), U(5)[:, P:2 * P].bitcast(I32)
            c2, r2 = U(6)[:, 0:P].bitcast(I32), U(6)[:, P:2 * P].bitcast(I32)
            cf, rf = U(7)[:, 0:P], U(7)[:, P:2 * P]
            eq = U(8).rearrange("p (k n) -> p k n", k=8)
            done(dve.tensor_copy(cf, ci))
            done(dve.tensor_copy(rf, ri))
            tt(le[:], rf, cf, ALU.is_le)
            tt(lt[:], rf, cf, ALU.is_lt)
            for k in range(7):
                ts(c2, ci, k, None, ALU.arith_shift_right)
                ts(r2, ri, k, None, ALU.arith_shift_right)
                tt(eq[:, k, :], c2, r2, ALU.is_equal)
                if k == 2:
                    tt(seq_ind[:], ci[:, 0:DEC_B], r2[:, 0:DEC_B], ALU.is_equal)
            done(dve.memset(eq[:, 7, :], 1.0))
            for k in range(7):
                tt(lev[:, k, :], eq[:, k + 1, :], eq[:, k, :], SUB)
            tt(le4[:], le[:], eq[:, 2, :], MUL)
            tt(lt4[:], lt[:], eq[:, 2, :], MUL)
            tt(low0[:], rf, cf, ALU.is_gt)
            tt(low0[:], low0[:], lev[:, 0, :], MUL)
            ts(half_ind[:, 0:1], rf[:, 0:1], 63.5, None, ALU.is_le)
            ts(half_ind[:, 1:2], rf[:, 0:1], 63.5, None, ALU.is_gt)
            tt(cum_mid[:], le[:], half_ind[:, 0:1].to_broadcast([P, P]), SUB)
            ts(c2, ci, 31, None, ALU.bitwise_and)
            ts(r2, ri, 31, None, ALU.bitwise_and)
            tt(rep32[:], c2, r2, ALU.is_equal)
            done(dve.tensor_reduce(own_seq[:], rep32[:, 0:DEC_B * DEC_T].rearrange("p (b i) -> p b i", i=DEC_T), AXX, ADD))
            done(dve.tensor_copy(iota16[:], cf[:, 0:TOPK]))
            done(dve.memset(stateT[:], 0.0))
            for g in range(NGRP):
                dve.sem_inc(rows_used[g], 1)
            dve.sem_inc(consts_built, 1)

            def norm():
                for t in range(NT):
                    done(dve.tensor_tensor_reduce(hc[:, t, :], x[:, t, :], x[:, t, :], 1.0, 0.0, MUL, ADD, rstd[:, t:t + 1]))
                ts(rstd[:, 0:3], rstd[:, 0:3], 1.0 / D, EPS, MUL, ADD)
                dve.sem_inc(vector_result, 1)
                w.take(scalar_result)
                done(dve.reciprocal(rstd[:, 0:3], rstd[:, 0:3]))
                g = vec()
                for t in range(NT):
                    stt(hc[:, t, :], x[:, t, :], rstd[:, t:t + 1], g, MUL, MUL)
                dve.sem_inc(vec_used, 1)

            def adaln():
                norm()
                for tiles, k in (((0, 1), 1), ((2,), 4)):
                    sc = vec(k)
                    for t in tiles:
                        stt(hc[:, t, :], sc, 1.0, hc[:, t, :], ADD, MUL)
                    dve.sem_inc(vec_used, 1)
                    sh = vec(k)
                    for t in tiles:
                        tt(hc[:, t, :], hc[:, t, :], sh, ADD)
                    dve.sem_inc(vec_used, 1)
                dve.sem_inc(operand_written, 1)

            def gated_add(tmp):
                for t in range(NT):
                    if t != 1:
                        g = vec(4 if t == SAMPLE else 1)
                    ps = fill()
                    tt(tmp, ps, g, MUL, vector_drained)
                    tt(x[:, t, :], x[:, t, :], tmp, ADD)
                    if t:
                        dve.sem_inc(vec_used, 1)

            def top16(vals, idxs, src, scratch):
                done(dve.max(vals[:, 0:8], src))
                done(dve.max_index(idxs[:, 0:8], vals[:, 0:8], src))
                done(dve.match_replace(scratch, vals[:, 0:8], src, LOWEST))
                done(dve.max(vals[:, 8:16], scratch))
                done(dve.max_index(idxs[:, 8:16], vals[:, 8:16], scratch))

            def bc(ap, n):
                return ap.unsqueeze(2).to_broadcast([P, ap.shape[1], n])

            for k in range(6):
                ps = fill()
                b = vec()
                if k >= 2:
                    dve.wait_ge(mod_stored[k % 2], 16 * (k // 2))
                tt(modrow[k % 2][0:9, :], ps[0:9, :], b[0:9, :], ADD, vector_drained)
                dve.sem_inc(mod_ready, 1)
                dve.sem_inc(vec_used, 1)
            w.take(x_loaded, 6 * 16)
            for li in range(2):
                adaln()
                dve.sem_inc(norm_done, 1)
                if li == 0:
                    for i in range(2):
                        dve.wait_ge(mod_stored[i], 3 * 16)
                    w.take(scalar_result)
                    n = 2 * P
                    tt(xx[:, :, 1:n], hT[:, :, 0:n - 1], hT[:, :, 1:n], SUB)
                    ts(xx[:, :, 0:1], hT[:, :, 0:1], -1.0, None, MUL)
                    xs4 = xx[:, :, n:].rearrange("p k (s i) -> p k s i", i=DEC_T)
                    hs4 = hT[:, :, n:].rearrange("p k (s i) -> p k s i", i=DEC_T)
                    for k in range(KD):
                        tt(xs4[:, k, :, 1:DEC_T], hs4[:, k, :, 0:DEC_T - 1], hs4[:, k, :, 1:DEC_T], SUB)
                    sT = shiftT[:, :].rearrange("p (k b) -> p k b", k=KD)
                    for c in range(COPIES):
                        tt(xs4[:, :, c * DEC_B:(c + 1) * DEC_B, 0], sT, hs4[:, :, c * DEC_B:(c + 1) * DEC_B, 0], SUB)
                    done(dve.memset(loraT[64:65, 0:2, :], 1.0))
                    for n, i in enumerate((0, 3, 1, 2, 4, 5)):
                        if n >= 2:
                            w.take(mix_used)
                        for k in range(KD):
                            stt(mixb[n % 2][:, k, :], xx[:, k, :], muT[:, i * KD + k:i * KD + k + 1], hT[:, k, :], MUL, ADD)
                        dve.sem_inc(operand_written, 1)
                    w.take(scalar_result)
                    w.take(shift_stored, 32)
                    for name in ("atz", "rtz"):
                        done(dve.memset(halves[1][name], 0.0))
                    for t in range(NT):
                        sample = t == SAMPLE
                        r, k_, v = cur
                        w.take(cur_loaded, 48)
                        g = vec()
                        tt(U(2), k_, g, MUL)
                        dve.sem_inc(vec_used, 1)
                        tt(U(3), U(2), U(2), MUL)
                        done(dve.tensor_reduce(s16[:, 0, :], heads(U(3), RH, RK), AXX, ADD))
                        w.take(scalar_result)
                        dve.sem_inc(vector_result, 1)
                        w.take(scalar_result)
                        ts(s16[:, 0, :], s16[:, 0, :], 1e-12, None, ALU.max)
                        done(dve.reciprocal(s16[:, 0, :], s16[:, 0, :]))
                        tt(heads(U(2), RH, RK), heads(U(2), RH, RK), bc(s16[:, 0, :], RK), MUL)
                        g = vec()
                        stt(U(3), U(1), -1.0, g, ADD, MUL)
                        dve.sem_inc(vec_used, 1)
                        stt(U(4), U(3), 1.0, k_, ADD, MUL)
                        g = vec()
                        tt(U(3), U(4), r, MUL)
                        tt(U(3), U(3), g, MUL)
                        dve.sem_inc(vec_used, 1)
                        done(dve.tensor_reduce(bonus[:], heads(U(3), RH, RK), AXX, ADD))
                        tt(U(1), U(1), U(2), MUL)
                        tt(U(1), U(1), U(6), MUL)
                        stt(U(2), U(2), -1.0, U(7), MUL, MUL)
                        tt(U(2), U(2), U(5), MUL)
                        tt(r, r, U(5), MUL)
                        tt(U(4), U(4), U(6), MUL)
                        done(dve.memset(U(5), 0.0))
                        done(dve.memset(U(6), 0.0))
                        dve.sem_inc(vector_result, 1)
                        dve.sem_inc(operand_written, 1)
                        for k in range(2):
                            b = vec()
                            tt(b[0:9, :], fill()[0:9, :], b[0:9, :], ADD, vector_drained)
                            dve.sem_inc(next_mod_ready, 1)
                        strict, incl = (lt4, le4) if sample else (lt, le)

                        def m8(m):
                            return m.unsqueeze(1).to_broadcast([P, HALF_H, P])

                        h8 = lambda ap: heads(ap, HALF_H, P)

                        def attention(b):
                            tt(h8(b["nt"]), h8(fill()), m8(strict[:]), MUL, vector_drained)
                            tt(h8(b["t"]), h8(fill()), m8(low0[:]), MUL, vector_drained)
                            tt(h8(b["ak"]), h8(fill()), m8(strict[:]), MUL, vector_drained)
                            tt(h8(b["rb"]), h8(fill()), m8(incl[:]), MUL, vector_drained)
                            tt(h8(b["rk"]), h8(fill()), m8(incl[:]), MUL, vector_drained)
                            tt(h8(b["t"]), h8(b["t"]), m8(ident[:]), ADD)
                            tt(h8(b["tt"]), h8(b["nt"]), m8(lev[:, 0, :]), MUL)
                            tt(h8(b["tt"]), h8(b["tt"]), m8(ident[:]), ADD)

                        def level_part(b, k):
                            tt(h8(b["lt"]), h8(b["nt"]), m8(lev[:, k, :]), MUL)

                        if not sample:
                            tt(st_in[:], stateT[:], pcs[:, :, 0:1].to_broadcast([P, KD, RK]), MUL)
                            for b in halves:
                                attention(b)
                                level_part(b, 1)
                                dve.sem_inc(operand_written, 1)
                            for k in range(1, 7):
                                m = 1 << k
                                for b in halves:
                                    if k < 6:
                                        t_even = blocks(b["t"], m, 0)
                                        tt(t_even, t_even, compact(fill()[:, 0:512], m), ADD, vector_drained)
                                        level_part(b, k + 1)
                                    tt_odd = blocks(b["tt"], m, 1)
                                    tt(tt_odd, tt_odd, compact(fill()[:, 0:512], m), ADD, vector_drained)
                                    if k < 6:
                                        dve.sem_inc(operand_written, 1)
                            for hh in range(2):
                                sl = slice(hh * PAIRS, (hh + 1) * PAIRS)
                                ps = fill().rearrange("p (q e v) -> p q e v", q=PAIRS * 2, e=2)[:, 0:PAIRS]
                                for e in range(2):
                                    rr = slice(64 * e, 64 * e + 64)
                                    tt(st_in[rr, sl], st_in[rr, sl], ps[rr, :, e, :], ADD, vector_drained if e else None)
                            tt(stateT[:], st_in[:], pcs[:, :, 1:2].to_broadcast([P, KD, RK]), MUL)
                            if t == 1:
                                dve.sem_inc(operand_written, 1)
                            w.take(scalar_result)
                        for hh in (range(2) if sample else ()):
                            b = halves[0]
                            attention(b)
                            level_part(b, 1)
                            dve.sem_inc(operand_written, 1)
                            tt(b["tt"], b["tt"], fill(), ADD, vector_drained)
                            w.take(scalar_result)
                            kept = U(3)
                            for part in range(2):
                                for g2_ in range(PAIRS):
                                    prod = U(12).rearrange("p (e b v) -> p e b v", e=2, b=DEC_B)
                                    tt(prod, fill().rearrange("p (e b v) -> p e b v", e=2, b=DEC_B),
                                       own_seq[:].unsqueeze(1).unsqueeze(3).to_broadcast([P, 2, DEC_B, RK]), MUL, vector_drained)
                                    to = part * 512 + g2_ * P
                                    done(dve.tensor_reduce(heads(kept[:, to:to + P], 2, RK), prod.rearrange("p e b v -> p e v b"), AXX, ADD))
                                if part == 0:
                                    tt(b["rhs"][:, 0:512], kept[:, 0:512], fill()[:, 0:512], ADD, vector_drained)
                                    dve.sem_inc(operand_written, 1)
                            w.take(scalar_result)
                            s0 = U(14, 2).rearrange("p (b q v) -> p b q v", b=DEC_B, q=PAIRS)

                            def spread(q):
                                for src, dst in ((b["rhs"][:, 512 + P * q:512 + P * (q + 1)], wx[:, 2 * (q % 2), :]),
                                                 (v[:, hh * 512 + P * q:hh * 512 + P * (q + 1)], wx[:, 2 * (q % 2) + 1, :])):
                                    tt(dst.rearrange("p (e b v) -> p e b v", e=2, b=DEC_B),
                                       heads(src, 2, RK).unsqueeze(2).to_broadcast([P, 2, DEC_B, RK]),
                                       seq_ind[:].unsqueeze(1).unsqueeze(3).to_broadcast([P, 2, DEC_B, RK]), MUL)
                                dve.sem_inc(operand_written, 1)

                            spread(0)
                            spread(1)
                            tt(k_[:, hh * 512:(hh + 1) * 512], kept[:, 512:1024], fill()[:, 0:512], ADD, vector_drained)
                            for q in range(PAIRS):
                                ps = fill()
                                for e in range(2):
                                    rr = slice(64 * e, 64 * e + 64)
                                    tt(s0[rr, :, q, :], s0[rr, :, q, :], ps[rr, e * 512:(e + 1) * 512].rearrange("p (b v) -> p b v", b=DEC_B),
                                       ADD, vector_drained if e else None)
                                tt(s0[:, :, q, :], s0[:, :, q, :], bc(pcs[:, hh * PAIRS + q, :], RK), MUL)
                                if q + 2 < PAIRS:
                                    spread(q + 2)
                            dve.sem_inc(operand_written, 1)
                            w.take(scalar_result)
                        w.take(next_mod_stored, 32)
                        dve.sem_inc(vec_used, 2)
                        y = k_
                        mean, var = s16[:, 0, :], s16[:, 1, :]
                        done(dve.tensor_reduce(mean, heads(y, RH, RK), AXX, ADD))
                        ts(mean, mean, 1.0 / RK, None, MUL)
                        tt(heads(y, RH, RK), heads(y, RH, RK), bc(mean, RK), SUB)
                        tt(U(3), y, y, MUL)
                        done(dve.tensor_reduce(var, heads(U(3), RH, RK), AXX, ADD))
                        ts(var, var, 1.0 / RK, LNX_EPS, MUL, ADD)
                        dve.sem_inc(vector_result, 1)
                        w.take(scalar_result)
                        done(dve.reciprocal(var, var))
                        tt(heads(y, RH, RK), heads(y, RH, RK), bc(var, RK), MUL)
                        g = vec()
                        tt(y, y, g, MUL)
                        dve.sem_inc(vec_used, 1)
                        g = vec()
                        tt(y, y, g, ADD)
                        dve.sem_inc(vec_used, 1)
                        tt(heads(U(3), RH, RK), heads(v, RH, RK), bc(bonus[:], RK), MUL)
                        tt(y, y, U(3), ADD)
                        tt(y, y, fill(), MUL, vector_drained)
                        dve.sem_inc(operand_written, 1)
                        w.take(scalar_result)
                else:
                    done(dve.memset(alT[0:17, :], 1.0))
                    dve.sem_inc(vector_result, 1)
                    w.take(scalar_result)
                    done(dve.memset(gS, 0.0))
                    for t in range(NT):
                        sample = t == SAMPLE
                        ps = fill()
                        ts(la, ps[:, 0:512], 0.0, None, ALU.min)
                        stt(ex, la, -2.0, ps[:, 0:512], MUL, ADD, vector_drained)
                        dve.sem_inc(vector_result, 1)
                        w.take(scalar_result)
                        ts(ex, ex, 1.0, None, ADD)
                        dve.sem_inc(vector_result, 1)
                        w.take(scalar_result)
                        tt(la, la, ex, SUB)
                        dve.sem_inc(operand_written, 1)
                        w.take(scalar_result)
                        q3, k3 = qT[:, :, t * P:(t + 1) * P], kT[:, :, t * P:(t + 1) * P]
                        h4 = lambda ap: heads(ap, GH, P)
                        m4 = lambda m: m.unsqueeze(1).to_broadcast([P, GH, P])
                        tt(h4(at), h4(fill()[:, 0:512]), m4(ident[:]), MUL, vector_drained)
                        for k in (range(2) if sample else range(7)):
                            m = 1 << k
                            b3 = bT.rearrange("p (b m) -> p b m", m=2 * m)
                            tt(df.rearrange("p (b m) -> p b m", m=2 * m), b3,
                               b3[:, :, m - 1:m].to_broadcast([P, 512 // (2 * m), 2 * m]), SUB)
                            dve.sem_inc(vector_result, 1)
                            w.take(scalar_result)
                            tt(h4(qe), q3, h4(ex), MUL)
                            tt(h4(ke), k3, h4(ex), MUL)
                            dve.sem_inc(operand_written, 1)
                            tt(h4(atmp), h4(fill()[:, 0:512]), m4(lev[:, k, :]), MUL, vector_drained)
                            tt(at, at, atmp, ADD)
                        tt(h4(at), h4(at), m4((le4 if sample else le)[:]), MUL)
                        if sample:
                            b4 = bT.rearrange("p (b m) -> p b m", m=DEC_T)
                            tt(df.rearrange("p (b m) -> p b m", m=DEC_T), b4[:, :, 3:4].to_broadcast([P, P, DEC_T]), b4, SUB)
                        else:
                            tt(h4(df), h4(bT)[:, :, P - 1:P].to_broadcast([P, GH, P]), h4(bT), SUB)
                        dve.sem_inc(vector_result, 1)
                        w.take(scalar_result)
                        tt(h4(qe), q3, h4(ex), MUL)
                        tt(h4(ke), k3, h4(df), MUL)
                        dve.sem_inc(operand_written, 1)
                        w.take(scalar_result)
                        if sample:
                            done(dve.memset(qem, 0.0))
                            for h in range(GH):
                                done(dve.tensor_copy(diag_blocks(qem), own_rows(qe[:, h * P:(h + 1) * P])))
                                tt(kdm.rearrange("p (b n) -> p b n", b=DEC_B), kd[:, h * P:(h + 1) * P].unsqueeze(1).to_broadcast([P, DEC_B, P]),
                                   bc(seq_ind[:], P), MUL)
                                dve.sem_inc(operand_written, 1)
                                s0 = gS0[h % 2].rearrange("p (b v) -> p b v", b=DEC_B)
                                w.take(gla_state_loaded[h % 2], 16)
                                done(dve.tensor_copy(go[:, h * GV:(h + 1) * GV], fill()[:, 0:GV]), vector_drained)
                                tt(s0, s0, ebt.rearrange("p (h b) -> p h b", h=GH)[:, h, :].unsqueeze(2).to_broadcast([P, DEC_B, GV]), MUL)
                                for q in range(2):
                                    tt(gS0[h % 2][:, q * D:(q + 1) * D], gS0[h % 2][:, q * D:(q + 1) * D], fill(), ADD, vector_drained)
                                dve.sem_inc(gla_state_new, 1)
                        else:
                            done(dve.tensor_copy(go, fill()), vector_drained)
                            g3 = heads(gS, GH, GV)
                            tt(g3, g3, ebt.rearrange("p (h b) -> p h b", h=GH)[:, :, 0:1].to_broadcast([P, GH, GV]), MUL)
                            tt(gS, gS, fill(), ADD, vector_drained)
                            if t == 1:
                                dve.sem_inc(gla_prompt_new, 1)
                        tt(U(10), go, go, MUL)
                        done(dve.tensor_reduce(rstd[:, 0:4], heads(U(10), GH, GV), AXX, ADD))
                        ts(rstd[:, 0:4], rstd[:, 0:4], 1.0 / GV, EPS, MUL, ADD)
                        dve.sem_inc(vector_result, 1)
                        w.take(scalar_result)
                        done(dve.reciprocal(rstd[:, 0:4], rstd[:, 0:4]))
                        tt(heads(go, GH, GV), heads(go, GH, GV), bc(rstd[:, 0:4], GV), MUL)
                        g = vec()
                        tt(heads(go, GH, GV), heads(go, GH, GV), g[:, 0:GV].unsqueeze(1).to_broadcast([P, GH, GV]), MUL)
                        dve.sem_inc(vec_used, 1)
                        tt(go, go, gr[t], MUL)
                        dve.sem_inc(operand_written, 1)
                        w.take(scalar_result)
                    dve.wait_ge(gla_prompt_stored, 16)
                    dve.wait_ge(gla_state_stored[0], 32)
                    dve.wait_ge(gla_state_stored[1], 32)
                gated_add(U(0))
                dve.sem_inc(arena_free, 1)
                adaln()
                def best_keys(blk, tiles):
                    per_fill = 4 if len(tiles) == 1 else 1
                    for n in range(4):
                        if n % per_fill == 0:
                            ps = fill()
                        for i, t in enumerate(tiles):
                            c = (n % per_fill + i) * P
                            top16(top_s[:, t, 4 * blk + n, :], top_i[:, t, 4 * blk + n, :], ps[:, c:c + P], U(20)[:, 512:512 + P])
                        if n % per_fill == per_fill - 1:
                            dve.sem_inc(vector_drained, 1)
                            steps[vector_drained.name] += 1

                for blk in range(4):
                    best_keys(blk, (0,))

                def choose(t):
                    s4 = top_s[:, t].rearrange("p (h s) e -> p h s e", s=2)
                    tt(cand.rearrange("p (h i j) -> p h i j", h=PH, i=TOPK),
                       s4[:, :, 0, :].unsqueeze(3).to_broadcast([P, PH, TOPK, TOPK]),
                       s4[:, :, 1, :].unsqueeze(2).to_broadcast([P, PH, TOPK, TOPK]), ADD)
                    for h in range(PH):
                        top16(sc[:, h * TOPK:(h + 1) * TOPK], pos[:, h * TOPK:(h + 1) * TOPK], cand[:, h * 256:(h + 1) * 256], rest)
                    done(dve.tensor_copy(iF, top_i[:, t].rearrange("p i e -> p (i e)")))
                    i4 = iF.rearrange("p (h s e) -> p h s e", h=PH, s=2)
                    for side, e_out in ((0, e1), (1, e2)):
                        if side == 0:
                            ts(pi, pos, 4, None, ALU.logical_shift_right)
                        else:
                            ts(pi, pos, 15, None, ALU.bitwise_and)
                        done(dve.tensor_copy(pf, pi))
                        o3 = onehot.rearrange("p (n c) -> p n c", c=TOPK)
                        tt(o3, iota16[:].unsqueeze(1).to_broadcast([P, P, TOPK]), bc(pf, TOPK), ALU.is_equal)
                        o4 = onehot.rearrange("p (h e c) -> p h e c", h=PH, e=TOPK)
                        tt(o4, o4, i4[:, :, side, :].unsqueeze(2).to_broadcast([P, PH, TOPK, TOPK]), MUL)
                        done(dve.tensor_reduce(e_out, o3, AXX, ADD))
                    stt(e1, e1, float(NKEYS), e2, MUL, ADD)
                    if li:
                        ts(e1, e1, float(li * NKEYS * NKEYS), None, ADD)
                    s3 = sc.rearrange("p (h e) -> p h e", h=PH)
                    below = e2 if t == SAMPLE else gate[:, t, :]
                    tt(below.rearrange("p (h e) -> p h e", h=PH), s3, s3[:, :, 0:1].to_broadcast([P, PH, TOPK]), SUB)
                    if t == SAMPLE:
                        for c in range(COPIES):
                            rr = slice(32 * c, 32 * c + 32)
                            done(dve.tensor_copy(gate[rr, t, 0:32], e2[rr, rr]))
                            done(dve.tensor_copy(idx[rr, t * P:t * P + 32], e1[rr, rr]))
                    else:
                        done(dve.tensor_copy(idx[:, t * P:(t + 1) * P], e1))
                    dve.sem_inc(experts_chosen, 1)

                def products(n, t, first, both):
                    groups = groups_of(0, both)
                    per = len(groups) * GRP
                    with dve.Fori(0, n // per) as i:
                        for k, g in enumerate(groups):
                            dve.wait_ge(rows_landed[g], i * (16 * GRP) + (rounds[g] + 1) * 16 * GRP)
                            for s in range(GRP):
                                row = ring[:, g * GRP + s, :]
                                dve.tensor_tensor_reduce(row, row, hc[:, t, :], 1.0, 0.0, MUL, ADD,
                                                         act16[:, k * GRP + s:k * GRP + s + 1]).then_inc(rows_used[g], 1)
                        for g in groups:
                            dve.wait_ge(rows_used[g], i * GRP + (rounds[g] + 1) * GRP + 1)
                        dve.tensor_copy(acts[:, t % 2, bass.ds(i * per + first, per)], act16[:, 0:per]).then_inc(acts_copied, 1)
                        dve.wait_ge(acts_copied, i + (ncopied[0] + 1))
                    ncopied[0] += n // per

                def weigh(t):
                    slots = experts_of(t)
                    nh = slots // TOPK
                    dve.sem_inc(vector_result, 1)
                    w.take(scalar_result)
                    g3 = gate[:, t, 0:slots].rearrange("p (h e) -> p h e", h=nh)
                    done(dve.tensor_reduce(s16[:, 0, 0:nh], g3, AXX, ADD))
                    done(dve.reciprocal(s16[:, 0, 0:nh], s16[:, 0, 0:nh]))
                    tt(g3, g3, bc(s16[:, 0, 0:nh], TOPK), MUL)
                    tt(acts[:, t % 2, 0:slots], acts[:, t % 2, 0:slots], gate[:, t, 0:slots], MUL)
                    dve.sem_inc(vector_result, 1)

                def add_experts(t, gain):
                    tt(peer_tmp, fill(), gain, MUL, vector_drained)
                    tt(x[:, t, :], x[:, t, :], peer_tmp, ADD)

                gain = vec()
                choose(0)
                for turn_, (n, u, v, choice) in enumerate(SEGMENTS):
                    if choice:
                        choose(u[0])
                    both = bool(u and v)
                    if u:
                        products(n, *u, both)
                    if turn_ < 4:
                        best_keys(SCORE_BLOCKS[turn_], (1, SAMPLE))
                    for g in range(NGRP):
                        rounds[g] += n // (len(groups_of(0, both)) * GRP)
                    if u:
                        if u[1] + n == experts_of(u[0]):
                            weigh(u[0])
                            if u[0] == 1:
                                add_experts(0, gain)
                add_experts(1, gain)
                dve.sem_inc(vec_used, 1)
                add_experts(SAMPLE, vec(4))
                dve.sem_inc(vec_used, 1)
            norm()
            dve.sem_inc(y_ready, 1)

        @block.tensor
        def _(pe):
            w = Waits(pe)
            nfv, nfa, nw = [0], [0], [0]
            rounds = [0] * NGRP
            ndiag = [0]

            def for_vector():
                if nfv[0] >= 2:
                    pe.wait_ge(vector_drained, nfv[0] - 1)
                nfv[0] += 1
                return psv[:, (nfv[0] - 1) % 2, :]

            def for_scalar():
                if nfa[0] >= 2:
                    pe.wait_ge(scalar_drained, nfa[0] - 1)
                nfa[0] += 1
                return psa[:, (nfa[0] - 1) % 2, :]

            def scalar_copies():
                pe.wait_ge(scalar_drained, nfa[0])

            def vector_copies():
                pe.wait_ge(vector_drained, nfv[0])

            def weight():
                b = nw[0] % WBUF
                pe.wait_ge(weight_loaded[b], 16 * (nw[0] // WBUF + 1))
                nw[0] += 1
                return wring[:, b]

            def mm(out, lhsT, rhs, start=True, stop=True):
                return nc.tensor.matmul(out, lhsT, rhs, start=start, stop=stop)

            def rows_product(ps, t, wt, cols=512, at_=0):
                for k in range(KD):
                    last = mm(ps[:, at_:at_ + cols], hT[:, k, t * P:(t + 1) * P], wt[:, k, 0:cols], k == 0, k == KD - 1)
                return last

            def turn(src, ps, n=8):
                for k in range(n):
                    last = nc.tensor.transpose(ps[:, k * P:(k + 1) * P], src[:, k * P:(k + 1) * P], ident[:])
                return last

            def h_turned():
                w.take(operand_written)
                for t in range(NT):
                    turn(hc[:, t, :], for_scalar()).then_inc(psum_for_scalar, 1)

            def project_out():
                scalar_copies()
                wts = [weight(), weight()]
                for t in range(NT):
                    ps = for_vector()
                    for j in range(2):
                        last = rows_product(ps, t, wts[j], 512, j * 512)
                    last.then_inc(psum_for_vector, 1)
                pe.wait_ge(psum_for_vector, nfv[0])
                for j in range(2):
                    pe.sem_inc(weight_used, 1)

            pe.wait_ge(consts_built, 1)
            w.take(operand_written)
            ps = for_scalar()
            for k in range(KD):
                last = nc.tensor.transpose(ps[:, k * 9:(k + 1) * 9], crow[0:9, k * P:(k + 1) * P], ident[0:9, 0:9])
            last.then_inc(psum_for_scalar, 1)
            ps = for_scalar()
            for k in range(KD):
                last = nc.tensor.transpose(ps[:, k * DEC_B:(k + 1) * DEC_B], srow[0:DEC_B, k * P:(k + 1) * P], ident[0:8, 0:8])
            last.then_inc(psum_for_scalar, 1)
            nc.tensor.transpose(for_scalar()[:, 0:48], murow[0:48, :], ident[0:48, 0:48]).then_inc(psum_for_scalar, 1)
            scalar_copies()

            def modulation():
                ps = for_vector()
                for j in range(2):
                    wt = weight()
                    for kk in range(KD):
                        last = mm(ps[0:9, j * 512:(j + 1) * 512], cT[:, kk * 9:(kk + 1) * 9], wt[:, kk, :], kk == 0, kk == KD - 1)
                    last.then_inc(weight_used if j == 0 else psum_for_vector, 1)
                pe.wait_ge(psum_for_vector, nfv[0])
                pe.sem_inc(weight_used, 1)

            for k in range(6):
                modulation()
            for li in range(2):
                h_turned()
                if li == 0:
                    pe.wait_ge(lora_loaded, 16 * 8)
                    for n, i in enumerate((0, 3, 1, 2, 4, 5)):
                        w.take(operand_written)
                        mx = mixb[n % 2]
                        if i < 3:
                            for j in range(2):
                                wt = weight()
                                for t in range(NT):
                                    ps = for_scalar()
                                    for k in range(KD):
                                        last = mm(ps[:, 0:512], mx[:, k, t * P:(t + 1) * P], wt[:, k, :], k == 0, k == KD - 1)
                                    last.then_inc(psum_for_scalar, 1)
                                pe.wait_ge(psum_for_scalar, nfa[0])
                                pe.sem_inc(weight_used, 1)
                        else:
                            lo, m = ((0, 64), (64, 64), (128, P))[i - 3]
                            ps = for_scalar()
                            for k in range(KD):
                                last = mm(ps[0:m, 0:TOK], lora1[:, k, lo:lo + m], mx[:, k, :], k == 0, k == KD - 1)
                            last.then_inc(psum_for_scalar, 1)
                            pe.wait_ge(psum_for_scalar, nfa[0])
                        if n < 4:
                            pe.sem_inc(mix_used, 1)
                    scalar_copies()
                    for t in range(NT):
                        sample = t == SAMPLE
                        if t:
                            scalar_copies()
                        for i in range(2):
                            ps = for_scalar()
                            for j in range(2):
                                last = mm(ps[:, j * 512:(j + 1) * 512], loraT[0:65, i, t * P:(t + 1) * P], lora2[0:65, i, j * 512:(j + 1) * 512])
                            last.then_inc(psum_for_scalar, 1)
                        scalar_copies()
                        ps = for_scalar()
                        for j in range(2):
                            last = mm(ps[:, j * 512:(j + 1) * 512], (le4 if sample else cum_mid)[:], U(0)[:, j * 512:(j + 1) * 512])
                        last.then_inc(psum_for_scalar, 1)
                        ps = for_scalar()
                        ind, nn = (seq_ind, DEC_B) if sample else (half_ind, 2)
                        for k in range(KD):
                            last = mm(ps[:, k * nn:(k + 1) * nn], U(0)[:, k * P:(k + 1) * P], ind[:])
                        last.then_inc(psum_for_scalar, 1)
                        for k in range(2):
                            modulation()
                        w.take(operand_written)
                        r, y, v = cur

                        def turn_half(hh):
                            o = hh * 512
                            ps = for_scalar()
                            turn(U(2)[:, o:o + 512], ps[:, 0:512], 4)
                            turn(r[:, o:o + 512], ps[:, 512:1024], 4).then_inc(psum_for_scalar, 1)
                            ps = for_scalar()
                            turn(U(1)[:, o:o + 512], ps[:, 0:512], 4)
                            turn(U(4)[:, o:o + 512], ps[:, 512:1024], 4).then_inc(psum_for_scalar, 1)

                        def hd(ap, h):
                            return ap[:, h * P:(h + 1) * P]

                        def attention(b):
                            bT_ = lambda h: hd(b["turned"], h // 2)
                            kT_ = lambda h: hd(b["turned"], PAIRS + h // 2)
                            az, rz = lambda h: hd(b["atz"], h), lambda h: hd(b["rtz"], h)
                            for lhs, rhs in ((bT_, az), (az, bT_), (kT_, az), (bT_, rz), (kT_, rz)):
                                ps = for_vector()
                                for h in range(HALF_H):
                                    last = mm(ps[:, h * P:(h + 1) * P], lhs(h), rhs(h))
                                last.then_inc(psum_for_vector, 1)

                        def level(b):
                            ps = for_scalar()
                            for h in range(HALF_H):
                                last = mm(ps[:, h * P:(h + 1) * P], hd(b["lt"], h), hd(b["t"], h))
                            last.then_inc(psum_for_scalar, 1)
                            return nfa[0]

                        def solve(b):
                            ps = for_scalar()
                            for h in range(HALF_H):
                                last = mm(ps[:, h * RK:(h + 1) * RK], hd(b["tt"], h), b["rhs"][:, h * RK:(h + 1) * RK])
                            last.then_inc(psum_for_scalar, 1)
                            return nfa[0]

                        if not sample:
                            turn_half(0)
                            first = nfa[0]
                            turn_half(1)
                            second = nfa[0]
                            pe.wait_ge(scalar_drained, first)
                            attention(halves[0])
                            pe.wait_ge(scalar_drained, second)
                            attention(halves[1])
                            for hh, b in enumerate(halves):
                                o = hh * 512
                                w.take(operand_written)
                                ps = for_scalar()
                                for h in range(HALF_H):
                                    out = ps[:, h * RK:(h + 1) * RK]
                                    mm(out, hd(b["atz"], h), st_in[:, hh * PAIRS + h // 2, :], True, False)
                                    last = mm(out, hd(b["ak"], h), v[:, o + h * RK:o + (h + 1) * RK], False, True)
                                last.then_inc(psum_for_scalar, 1)
                            for k in range(1, 7):
                                m = 1 << k
                                marks = []
                                for b in halves:
                                    if k > 1:
                                        w.take(operand_written)
                                    marks.append(level(b))
                                solved = []
                                for b, mark in zip(halves, marks):
                                    pe.wait_ge(scalar_drained, mark)
                                    for lhs, rhs, odd in ([(b["tt"], b["z"], 0)] if k < 6 else []) + [(b["z"], b["tt"], 1)]:
                                        ps = for_vector()
                                        for h in range(HALF_H):
                                            last = mm(compact(ps[:, h * RK:(h + 1) * RK], m), hd(lhs, h), blocks(hd(rhs, h), m, odd))
                                        last.then_inc(psum_for_vector, 1)
                                    solved.append(nfv[0])
                            marks = []
                            for b, mark in zip(halves, solved):
                                pe.wait_ge(vector_drained, mark)
                                marks.append(solve(b))
                            for hh, (b, mark) in enumerate(zip(halves, marks)):
                                o = hh * 512
                                pe.wait_ge(scalar_drained, mark)
                                sa = b["rhs"][:, 512:1024]
                                ps = for_scalar()
                                for h in range(HALF_H):
                                    out = ps[:, h * RK:(h + 1) * RK]
                                    mm(out, hd(b["rtz"], h), st_in[:, hh * PAIRS + h // 2, :], True, False)
                                    mm(out, hd(b["rb"], h), sa[:, h * RK:(h + 1) * RK], False, False)
                                    last = mm(out, hd(b["rk"], h), v[:, o + h * RK:o + (h + 1) * RK], False, True)
                                last.then_inc(psum_for_scalar, 1)
                                ps = for_vector()
                                for h in range(HALF_H):
                                    out = ps[:, h * RK:(h + 1) * RK]
                                    ch = slice(o + (h // 2) * P, o + (h // 2 + 1) * P)
                                    mm(out, U(1)[:, ch], sa[:, h * RK:(h + 1) * RK], True, False)
                                    last = mm(out, U(4)[:, ch], v[:, o + h * RK:o + (h + 1) * RK], False, True)
                                last.then_inc(psum_for_vector, 1)
                            if t == 1:
                                w.take(operand_written)
                                ps = for_scalar()
                                for pr in range(KD):
                                    last = nc.tensor.transpose(ps[0:RK, pr * P:(pr + 1) * P], stateT[:, pr, :], ident[:])
                                last.then_inc(psum_for_scalar, 1)
                        for hh in (range(2) if sample else ()):
                            o = hh * 512
                            b_ = halves[0]
                            turn_half(hh)
                            scalar_copies()
                            attention(b_)
                            w.take(operand_written)
                            level(b_)
                            scalar_copies()
                            ps = for_vector()
                            for h in range(HALF_H):
                                last = mm(ps[:, h * P:(h + 1) * P], hd(b_["z"], h), hd(b_["tt"], h))
                            last.then_inc(psum_for_vector, 1)
                            vector_copies()
                            for q in range(2):
                                w.take(s0_loaded, 64)
                                ps = for_scalar()
                                for b in range(4):
                                    src = hc[0:RK, b // 2, (b % 2) * 512:(b % 2) * 512 + 512]
                                    for pr in range(PAIRS):
                                        last = nc.tensor.transpose(ps[:, b * 256 + pr * RK:b * 256 + (pr + 1) * RK],
                                                                   src[:, pr * P:(pr + 1) * P], ident[0:RK, 0:RK])
                                last.then_inc(psum_for_scalar, 1)
                            scalar_copies()
                            s0 = U(14, 2).rearrange("p (b q v) -> p b q v", b=DEC_B, q=PAIRS)

                            def from_states(z):
                                for q in range(PAIRS):
                                    ps = for_vector()
                                    for e in range(2):
                                        last = mm(ps[:, e * 512:(e + 1) * 512].rearrange("p (b v) -> p b v", b=DEC_B),
                                                  hd(z, 2 * q + e), s0[:, :, q, :])
                                    last.then_inc(psum_for_vector, 1)

                            from_states(b_["atz"])
                            ps = for_vector()
                            for h in range(HALF_H):
                                last = mm(ps[:, h * RK:(h + 1) * RK], hd(b_["ak"], h), v[:, o + h * RK:o + (h + 1) * RK])
                            last.then_inc(psum_for_vector, 1)
                            from_states(b_["rtz"])
                            w.take(operand_written)
                            solve(b_)
                            scalar_copies()
                            sa = b_["rhs"][:, 512:1024]
                            ps = for_vector()
                            for h in range(HALF_H):
                                out = ps[:, h * RK:(h + 1) * RK]
                                mm(out, hd(b_["rb"], h), sa[:, h * RK:(h + 1) * RK], True, False)
                                last = mm(out, hd(b_["rk"], h), v[:, o + h * RK:o + (h + 1) * RK], False, True)
                            last.then_inc(psum_for_vector, 1)
                            for q in range(PAIRS):
                                w.take(operand_written)
                                ps = for_vector()
                                ch = slice(o + q * P, o + (q + 1) * P)
                                for e in range(2):
                                    out = ps[:, e * 512:(e + 1) * 512]
                                    mm(out, U(1)[:, ch], wx[:, 2 * (q % 2), e * 512:(e + 1) * 512], True, False)
                                    last = mm(out, U(4)[:, ch], wx[:, 2 * (q % 2) + 1, e * 512:(e + 1) * 512], False, True)
                                last.then_inc(psum_for_vector, 1)
                            w.take(operand_written)
                            for q in range(4):
                                ps = for_scalar()
                                for b in range(2):
                                    for pr in range(PAIRS):
                                        last = nc.tensor.transpose(ps[0:RK, b * 512 + pr * P:b * 512 + (pr + 1) * P],
                                                                   s0[:, 2 * q + b, pr, :], ident[:])
                                last.then_inc(psum_for_scalar, 1)
                        ps = for_vector()
                        for j in range(2):
                            last = mm(ps[:, j * 512:(j + 1) * 512], loraT[:, 2, t * P:(t + 1) * P], g2[:, j * 512:(j + 1) * 512])
                        last.then_inc(psum_for_vector, 1)
                        w.take(operand_written)
                        turn(y, for_scalar()).then_inc(psum_for_scalar, 1)
                else:
                    scalar_copies()
                    for blk in range(2):
                        wt = weight()
                        for h in range(GH):
                            ps = for_scalar()
                            for k in range(KD):
                                last = mm(ps[:, 0:TOK], wt[:, k, h * P:(h + 1) * P], hT[:, k, :], k == 0, k == KD - 1)
                            last.then_inc(psum_for_scalar, 1)
                        pe.wait_ge(psum_for_scalar, nfa[0])
                        pe.sem_inc(weight_used, 1)
                    for blk in range(4):
                        wt = weight()
                        for t in range(NT):
                            rows_product(for_scalar(), t, wt).then_inc(psum_for_scalar, 1)
                        pe.wait_ge(psum_for_scalar, nfa[0])
                        pe.sem_inc(weight_used, 1)
                    wt = weight()
                    ps = for_scalar()
                    for k in range(KD):
                        last = mm(ps[0:16, 0:TOK], wt[:, k, 0:16], hT[:, k, :], k == 0, k == KD - 1)
                    last.then_inc(psum_for_scalar, 1)
                    pe.wait_ge(psum_for_scalar, nfa[0])
                    pe.sem_inc(weight_used, 1)
                    w.take(gla_small_loaded, 32)
                    for t in range(NT):
                        sample = t == SAMPLE
                        tok = slice(t * P, (t + 1) * P)
                        scalar_copies()
                        mm(for_vector()[:, 0:512], alT[0:17, tok], wa2[0:17, :]).then_inc(psum_for_vector, 1)
                        w.take(operand_written)
                        ps = for_scalar()
                        for h in range(GH):
                            last = mm(ps[:, h * P:(h + 1) * P], la[:, h * P:(h + 1) * P], (le4 if sample else le)[:])
                        last.then_inc(psum_for_scalar, 1)
                        ps = for_vector()
                        for h in range(GH):
                            last = mm(ps[:, h * P:(h + 1) * P], kT[:, h, tok], qT[:, h, tok])
                        last.then_inc(psum_for_vector, 1)
                        for k in (range(2) if sample else range(7)):
                            w.take(operand_written)
                            ps = for_vector()
                            for h in range(GH):
                                last = mm(ps[:, h * P:(h + 1) * P], ke[:, h * P:(h + 1) * P], qe[:, h * P:(h + 1) * P])
                            last.then_inc(psum_for_vector, 1)
                        w.take(operand_written)
                        turn(ke, for_scalar(), 4).then_inc(psum_for_scalar, 1)
                        scalar_copies()
                        if sample:
                            for h in range(GH):
                                w.take(operand_written)
                                pe.wait_ge(gla_state_loaded[h % 2], 16 * (h // 2 + 1))
                                s0 = gS0[h % 2].rearrange("p (b v) -> p b v", b=DEC_B)
                                vv = gv[t][:, h * GV:(h + 1) * GV]
                                out = for_vector()[:, 0:GV]
                                mm(out, at[:, h * P:(h + 1) * P], vv, True, False)
                                for b in range(DEC_B):
                                    last = mm(out, qem[:, b * P:(b + 1) * P], s0[:, b, :], False, b == DEC_B - 1)
                                last.then_inc(psum_for_vector, 1)
                                for q in range(2):
                                    ps = for_vector()
                                    for b in range(4):
                                        bb = 4 * q + b
                                        last = mm(ps[:, b * GV:(b + 1) * GV], kdm[:, bb * P:(bb + 1) * P], vv)
                                    last.then_inc(psum_for_vector, 1)
                        else:
                            ps = for_vector()
                            for h in range(GH):
                                out = ps[:, h * GV:(h + 1) * GV]
                                vv = gv[t][:, h * GV:(h + 1) * GV]
                                mm(out, at[:, h * P:(h + 1) * P], vv, True, False)
                                last = mm(out, qe[:, h * P:(h + 1) * P], gS[:, h * GV:(h + 1) * GV], False, True)
                            last.then_inc(psum_for_vector, 1)
                            ps = for_vector()
                            for h in range(GH):
                                last = mm(ps[:, h * GV:(h + 1) * GV], kd[:, h * P:(h + 1) * P], gv[t][:, h * GV:(h + 1) * GV])
                            last.then_inc(psum_for_vector, 1)
                        w.take(operand_written)
                        turn(go, for_scalar()).then_inc(psum_for_scalar, 1)
                project_out()
                h_turned()
                w.take(keys_loaded, 16)
                for i in range(2):
                    ps = for_scalar()
                    for k in range(8):
                        last = nc.tensor.transpose(ps[:, k * P:(k + 1) * P], sk[:, 8 * i + k, :], ident[:])
                    last.then_inc(psum_for_scalar, 1)
                scalar_copies()
                def query(ps, at_, wt, i, tok):
                    for k in range(KD):
                        last = mm(ps[:, at_:at_ + tok.stop - tok.start], wt[:, k, i * P:(i + 1) * P], hT[:, k, tok], k == 0, k == KD - 1)
                    return last

                for blk in range(5):
                    if blk < 4:
                        wt = weight()
                        ps = for_scalar()
                        for i in range(4):
                            last = query(ps, i * P, wt, i, slice(0, P))
                        last.then_inc(psum_for_scalar, 1)
                    if blk:
                        pe.wait_ge(scalar_drained, nfa[0] - (1 if blk < 4 else 0))
                        ps = for_vector()
                        for i in range(4):
                            last = mm(ps[:, i * P:(i + 1) * P], qa[(blk - 1) % 2][:, i * P:(i + 1) * P], skT[:, 4 * (blk - 1) + i, :])
                        last.then_inc(psum_for_vector, 1)
                    if blk < 2:
                        pe.wait_ge(psum_for_scalar, nfa[0])
                        pe.sem_inc(weight_used, 1)
                held = [wring[:, (nw[0] - 2 + i) % WBUF] for i in range(2)]
                for n in range(HP + 1):
                    if n < HP:
                        if n % 4 == 0:
                            wt = held[n // 4] if n < 8 else weight()
                        ps = for_scalar()
                        query(ps, 0, wt, n % 4, slice(P, TOK)).then_inc(psum_for_scalar, 1)
                    if n:
                        pe.wait_ge(scalar_drained, nfa[0] - (1 if n < HP else 0))
                        hp = 4 * SCORE_BLOCKS[(n - 1) // 4] + (n - 1) % 4
                        ps = for_vector()
                        for i in range(2):
                            last = mm(ps[:, i * P:(i + 1) * P], qb[(n - 1) % 2][:, i * P:(i + 1) * P], skT[:, hp, :])
                        last.then_inc(psum_for_vector, 1)
                    if n < HP and n % 4 == 3:
                        pe.wait_ge(psum_for_scalar, nfa[0])
                        pe.sem_inc(weight_used, 1)
                for n, u, v, choice in SEGMENTS:
                    both = bool(u and v)
                    per = len(groups_of(1, both)) * GRP
                    if v:
                        t, first = v
                        if first == 0:
                            ps = for_vector()
                            for j in range(2):
                                mm(ps[:, j * 512:(j + 1) * 512], zeros[:], hc[:, t, j * 512:(j + 1) * 512], True, False)
                        with pe.Fori(0, n // per) as i:
                            for k, g in enumerate(groups_of(1, both)):
                                pe.wait_ge(diag_ready, i * per + (ndiag[0] + (k + 1) * GRP))
                                pe.wait_ge(rows_landed[g], i * (16 * GRP) + (rounds[g] + 1) * 16 * GRP)
                                for s in range(g * GRP, (g + 1) * GRP):
                                    for j in range(2):
                                        last = mm(ps[:, j * 512:(j + 1) * 512], diag[:, s, :], ring[:, s, j * 512:(j + 1) * 512], False, False)
                                last.then_inc(rows_used[g], GRP)
                        ndiag[0] += n
                        if first + n == experts_of(t):
                            for j in range(2):
                                last = mm(ps[:, j * 512:(j + 1) * 512], zeros[:], hc[:, t, j * 512:(j + 1) * 512], False, True)
                            last.then_inc(psum_for_vector, 1)
                    for g in range(NGRP):
                        rounds[g] += n // per


_INS = ["x_prompt", "x_sample", "state_rwkv_S", "state_rwkv_shift", "state_gla_S", "c_prompt", "c_sample",
        "ada_w", "ada_b", "norm1_g", "norm2_g", "final_g",
        "rw_mu", "rw_w_rkv", "rw_w0", "rw_w1", "rw_w2", "rw_a0", "rw_a1", "rw_a2", "rw_g1", "rw_g2",
        "rw_kk", "rw_ka", "rw_rk", "rw_lnx_w", "rw_lnx_b", "rw_wo",
        "gla_w_in", "gla_wa2", "gla_ba", "gla_gnorm", "gla_wo",
        "peer_wq", "peer_subkeys", "peer_u", "peer_v"]
_OUTS = [(1, 256, 1024), (8, 4, 1024), (1, 1, 16, 64, 64), (1, 1, 1024), (1, 1, 4, 128, 256),
         (1, 8, 16, 64, 64), (1, 8, 1024), (1, 8, 4, 128, 256)]


def kernel(**inputs):
    import numpy as np
    import concourse.bacc as bacc
    from concourse.bass_utils import run_bass_kernel_spmd

    nc = bacc.Bacc("TRN2", target_bir_lowering=False, num_devices=1)
    arrays, aps = {}, {}
    for name in _INS:
        v = np.ascontiguousarray(inputs[name])
        arrays["in_" + name] = v
        aps[name] = nc.dram_tensor("in_" + name, v.shape, mybir.dt.from_np(v.dtype), kind="ExternalInput").ap()
    outs = [nc.dram_tensor(f"out_{i}", s, F32, kind="ExternalOutput").ap() for i, s in enumerate(_OUTS)]
    program(nc, aps, outs)
    r = run_bass_kernel_spmd(nc, [arrays], core_ids=[0])
    return tuple(r.results[0][f"out_{i}"] for i in range(len(_OUTS)))
```

```python
from contextlib import ExitStack

import concourse.bass as bass
from concourse import mybir

F32 = mybir.dt.float32
I32 = mybir.dt.int32
U32 = mybir.dt.uint32
ALU = mybir.AluOpType
ACT = mybir.ActivationFunctionType
AXX = mybir.AxisListType.X

P = 128
D = 1024
KD = D // P
NT = 3
TOK = NT * P
SAMPLE = 2
DEC_B, DEC_T = 8, 4
COPIES = P // (DEC_B * DEC_T)
RH, RK = 16, 64
HALF_H = RH // 2
PAIRS = HALF_H // 2
GH, GK, GV = 4, 128, 256
TAU = 16.0
PH, NKEYS, TOPK = 8, 128, 16
HP = 2 * PH
EPS = 1e-6
LNX_EPS = 64e-5
DECAY_C = 0.6065306597126334
LOWEST = -3.0e38
WBUF = 2
VBUF = 3
GRP, NGRP = 4, 4
RING = GRP * NGRP
SHORT = P // COPIES
SEGMENTS = (
    (P // 4, (0, 0), None, False),
    (P // 4, (0, P // 4), None, False),
    (P // 4, (0, P // 2), None, False),
    (P // 4, (0, 3 * P // 4), None, False),
    (32, None, (0, 0), False),
    (P - 32, (1, 0), (0, 32), True),
    (32, (1, P - 32), None, False),
    (32, None, (1, 0), False),
    (SHORT, (SAMPLE, 0), (1, 32), True),
    (P - 32 - SHORT, None, (1, 32 + SHORT), False),
    (SHORT, None, (SAMPLE, 0), False),
)

SCORE_BLOCKS = (2, 3, 0, 1)


def experts_of(t):
    return SHORT if t == SAMPLE else P


def groups_of(side, both):
    return range(2 * side, 2 * side + 2) if both else range(NGRP)


class Waits:

    def __init__(self, eng):
        self.eng, self.n = eng, {}

    def take(self, sem, k=1):
        self.n[sem.name] = self.n.get(sem.name, 0) + k
        self.eng.wait_ge(sem, self.n[sem.name])


def program(nc, a, outs):
    (y_p, y_s, S_p, sh_p, G_p, S_s, sh_s, G_s) = outs
    with ExitStack() as ctx:
        def sb(name, shape, dt=F32):
            return ctx.enter_context(nc.sbuf_tensor(name, shape, dt))

        def sem(name):
            return ctx.enter_context(nc.semaphore(name))

        mod_d = nc.dram_tensor("mod_d", (2, 6, 9, D), F32, kind="Internal").ap()
        rkv_d = nc.dram_tensor("rkv_d", (3, NT, P, D), F32, kind="Internal").ap()

        x = sb("x", [P, NT, D])
        hc = sb("hc", [P, NT, D])
        hT = sb("hT", [P, KD, TOK])
        wring = sb("wring", [P, WBUF, KD, 512])
        wx = sb("wx", [P, 4, D])
        vring = sb("vring", [P, VBUF, D])
        arena = sb("arena", [P, 23680])
        ident = sb("ident", [P, P])
        zeros = sb("zeros", [P, P])
        le = sb("le", [P, P])
        le4 = sb("le4", [P, P])
        lt = sb("lt", [P, P])
        lt4 = sb("lt4", [P, P])
        cum_mid = sb("cum_mid", [P, P])
        low0 = sb("low0", [P, P])
        rep32 = sb("rep32", [P, P])
        lev = sb("lev", [P, 7, P])
        half_ind = sb("half_ind", [P, 2])
        seq_ind = sb("seq_ind", [P, DEC_B])
        own_seq = sb("own_seq", [P, DEC_B])
        iota16 = sb("iota16", [P, TOPK])
        cT = sb("cT", [P, KD * 9])
        muT = sb("muT", [P, 48])
        shiftT = sb("shiftT", [P, KD * DEC_B])
        rstd = sb("rstd", [P, 2, GH])
        s16 = sb("s16", [P, 2, RH])
        bonus = sb("bonus", [P, RH])
        pcs = sb("pcs", [P, KD, DEC_B])
        stateT = sb("stateT", [P, KD, RK])
        st_in = sb("st_in", [P, KD, RK])
        acts = sb("acts", [P, 2, P])
        act16 = sb("act16", [P, RING])
        idx_grp = sb("idx_grp", [P, RING], U32)

        def U(i, n=1):
            return arena[:, i * D:(i + n) * D]

        def W(off, n):
            return arena[:, off:off + n]

        def heads(ap, h, w):
            return ap.rearrange("p (h w) -> p h w", h=h)

        psv = ctx.enter_context(nc.psum_tensor("psv", [P, 2, D], F32))
        psa = ctx.enter_context(nc.psum_tensor("psa", [P, 2, D], F32))

        pool_consts = sem("pool_consts")
        consts_built = sem("consts_built")
        small_loaded = sem("small_loaded")
        x_loaded = sem("x_loaded")
        psum_for_vector = sem("psum_for_vector")
        psum_for_scalar = sem("psum_for_scalar")
        vector_drained = sem("vector_drained")
        scalar_drained = sem("scalar_drained")
        vector_step = sem("vector_step")
        scalar_step = sem("scalar_step")
        operand_written = sem("operand_written")
        vector_result = sem("vector_result")
        scalar_result = sem("scalar_result")
        weight_loaded = [sem(f"weight_loaded{i}") for i in range(WBUF)]
        weight_used = sem("weight_used")
        vec_loaded = [sem(f"vec_loaded{i}") for i in range(VBUF)]
        vec_used = sem("vec_used")
        mod_ready = sem("mod_ready")
        mod_stored = sem("mod_stored")
        norm_done = sem("norm_done")
        shift_stored = sem("shift_stored")
        mix_used = sem("mix_used")
        lora_loaded = sem("lora_loaded")
        spilled = [sem(f"spilled{i}") for i in range(3)]
        all_spilled = sem("all_spilled")
        cur_loaded = sem("cur_loaded")
        cur_used = sem("cur_used")
        s0_loaded = sem("s0_loaded")
        s0_used = sem("s0_used")
        state_stored = [sem(f"state_stored{i}") for i in range(2)]
        gla_small_loaded = sem("gla_small_loaded")
        gla_state_loaded = [sem(f"gla_state_loaded{i}") for i in range(2)]
        gla_state_new = sem("gla_state_new")
        gla_state_stored = [sem(f"gla_state_stored{i}") for i in range(2)]
        gla_prompt_stored = sem("gla_prompt_stored")
        arena_free = sem("arena_free")
        keys_loaded = sem("keys_loaded")
        experts_chosen = sem("experts_chosen")
        idx_copied = sem("idx_copied")
        pool_passed = sem("pool_passed")
        rows_landed = [sem(f"rows_landed{i}") for i in range(NGRP)]
        rows_used = [sem(f"rows_used{i}") for i in range(NGRP)]
        acts_copied = sem("acts_copied")
        diag_ready = sem("diag_ready")
        y_ready = sem("y_ready")
        y_stored = sem("y_stored")
        gla_prompt_new = sem("gla_prompt_new")

        block = ctx.enter_context(nc.Block())

        xx, lora1 = W(0, 3 * D).rearrange("p (k t) -> p k t", k=KD), W(9 * D, 2 * D).rearrange("p (k t) -> p k t", k=KD)
        mixb = [W((3 + 3 * i) * D, 3 * D).rearrange("p (k t) -> p k t", k=KD) for i in range(2)]
        spill_buf = [W(11 * D + 512 * i, 512) for i in range(3)]
        cur = [U(16 + i) for i in range(3)]
        lora2 = U(19, 2).rearrange("p (i n) -> p i n", i=2)
        g2 = U(21)
        loraT = W(22 * D, 3 * TOK).rearrange("p (i t) -> p i t", i=3)
        halves = [dict(atz=U(5), rtz=U(6), turned=U(7), nt=U(8), ak=U(9), rb=U(10), rk=U(11),
                       t=U(12), tt=U(13), lt=U(14), z=U(3), rhs=U(0)),
                  dict(atz=wx[:, 0, :], rtz=wx[:, 1, :], turned=U(16), nt=wx[:, 2, :], ak=wx[:, 3, :], rb=hc[:, 0, :], rk=hc[:, 1, :],
                       t=hc[:, 2, :], tt=U(15), lt=U(7), z=U(2), rhs=U(16))]
        crow, srow, murow = U(2), U(3), W(4 * D, P)
        qT = W(0, 4 * TOK).rearrange("p (h t) -> p h t", h=GH)
        kT = W(4 * TOK, 4 * TOK).rearrange("p (h t) -> p h t", h=GH)
        gv = [U(3 + t) for t in range(NT)]
        gr = [U(6 + t) for t in range(NT)]
        def gla_set(units, kd, go, ebt):
            names = ("la", "bT", "ex", "df", "qe", "ke", "at", "atmp")
            own = {name: units[i // 2][:, 512 * (i % 2):512 * (i % 2) + 512] for i, name in enumerate(names)}
            return dict(own, kd=kd, go=go, ebt=ebt, square=units[1])

        gla_sets = [gla_set([U(9 + i) for i in range(4)], W(13 * D, 512), U(14), W(13 * D + 512, GH * DEC_B)),
                    gla_set([wx[:, i, :] for i in range(4)], hc[:, 0, 0:512], hc[:, 1, :], hc[:, 0, 512:512 + GH * DEC_B])]
        GLA_TURNS = ((0, 1), (SAMPLE,))
        gS = U(15)
        gS0 = [U(16, 2), U(18, 2)]
        qem, kdm = U(20), U(21)
        alT, wa2 = W(22 * D, TOK), W(22 * D + TOK, 512)
        ring = U(0, 16).rearrange("p (s n) -> p s n", s=RING)
        skT = U(16, 2).rearrange("p (i n) -> p i n", i=HP)
        qa = [U(0)[:, 0:512], U(0)[:, 512:1024]]
        qb = [wx[:, 3, 0:256], wx[:, 3, 256:512]]
        sk = U(19, 2).rearrange("p (i k) -> p i k", i=HP)
        diag = U(19, 2).rearrange("p (s k) -> p s k", s=RING)
        top_s = W(21 * D, NT * 256).rearrange("p (t i e) -> p t i e", t=NT, i=HP)
        top_i = W(21 * D + NT * 256, NT * 256).bitcast(U32).rearrange("p (t i e) -> p t i e", t=NT, i=HP)
        peer_tmp = U(16)
        cand = wx[:, 0:2, :].rearrange("p u n -> p (u n)")
        onehot = cand
        small = [U(18)[:, P * i:P * (i + 1)] for i in range(8)]
        scratch, sc, pf, e1, e2 = small[0:5]
        pos, pi = small[5].bitcast(U32), small[6].bitcast(U32)
        rest, iF = wx[:, 2, 0:256], wx[:, 2, 256:512]
        gate = W(22 * D + 512, NT * P).rearrange("p (t e) -> p t e", t=NT)
        idx = wx[:, 3, 512:512 + NT * P + 16].bitcast(U32)

        def diag_blocks(dst):
            return bass.AP(tensor=dst.tensor, offset=dst.offset,
                           ap=[list(dst.ap[0]), [P + DEC_T, DEC_B], [DEC_B * DEC_T, COPIES], [1, DEC_T]])

        def blocks(ap, m, odd):
            return ap.rearrange("p (b two m) -> p b two m", two=2, m=m)[:, :, odd, :]

        def compact(ap, m):
            return ap.rearrange("p (b m) -> p b m", m=m)

        def own_rows(src):
            return src.rearrange("p (c b i) -> p b c i", c=COPIES, b=DEC_B)

        @block.sync
        def _(sp):
            w = Waits(sp)
            n = [0]

            def weight(src):
                b = n[0] % WBUF
                if n[0] >= WBUF:
                    w.take(weight_used)
                cols = src.shape[1]
                sp.dma_start(wring[:, b, :, 0:cols], src.rearrange("(k p) n -> p k n", p=P)).then_inc(weight_loaded[b], 16)
                n[0] += 1

            sp.dma_start(crow[0:1, :], a["c_prompt"]).then_inc(small_loaded, 16)
            sp.dma_start(crow[1:9, :], a["c_sample"]).then_inc(small_loaded, 16)
            sp.dma_start(srow[0:8, :], a["state_rwkv_shift"][0]).then_inc(small_loaded, 16)
            sp.dma_start(murow[0:48, :], a["rw_mu"][0].rearrange("i (k p) -> (i k) p", p=P)).then_inc(small_loaded, 16)
            xs = a["x_sample"].rearrange("b t d -> (b t) d")
            for t in range(2):
                sp.dma_start(x[:, t, :], a["x_prompt"][0, t * P:(t + 1) * P, :]).then_inc(x_loaded, 16)
            for c in range(COPIES):
                sp.dma_start(x[32 * c:32 * c + 32, SAMPLE, :], xs).then_inc(x_loaded, 16)
            def ada(li, blocks):
                for j in blocks:
                    weight(a["ada_w"][li][:, j * 512:(j + 1) * 512])

            ada(0, range(8))
            for li in range(2):
                if li == 0:
                    w.take(arena_free)
                    for src, lo in ((a["rw_w1"], 0), (a["rw_a1"], 64), (a["rw_g1"], 128)):
                        cols = src.shape[2]
                        sp.dma_start(lora1[:, :, lo:lo + cols], src[0].rearrange("(k p) n -> p k n", p=P)).then_inc(lora_loaded, 16)
                    for i, (m, b) in enumerate((("rw_w2", "rw_w0"), ("rw_a2", "rw_a0"))):
                        sp.dma_start(lora2[0:64, i, :], a[m][0]).then_inc(lora_loaded, 16)
                        sp.dma_start(lora2[64:65, i, :], a[b]).then_inc(lora_loaded, 16)
                    sp.dma_start(g2, a["rw_g2"][0]).then_inc(lora_loaded, 16)
                    w.take(norm_done)
                    sp.dma_start(sh_p[0], hc[P - 1:P, 1, :]).then_inc(shift_stored, 16)
                    sp.dma_start(sh_s[0], hc[DEC_T - 1:DEC_B * DEC_T:DEC_T, SAMPLE, :]).then_inc(shift_stored, 16)
                    for i in (0, 1, 2):
                        for j in range(2):
                            weight(a["rw_w_rkv"][0, i][:, j * 512:(j + 1) * 512])
                    ada(1, (0, 1))
                    w.take(all_spilled)
                    for t in range(NT):
                        if t:
                            w.take(cur_used)
                        for i in range(3):
                            sp.dma_start(cur[i], rkv_d[i, t]).then_inc(cur_loaded, 16)
                        if t < SAMPLE:
                            ada(1, (4 * t + 2, 4 * t + 3))
                            ada(0, (8 + 2 * t, 9 + 2 * t))
                            ada(1, (4 * t + 4, 4 * t + 5))
                        if t == SAMPLE:
                            w.take(shift_stored, 32)
                            for hh in range(2):
                                for q in range(2):
                                    if hh or q:
                                        w.take(s0_used)
                                    for b in range(4):
                                        sp.dma_start(
                                            hc[0:RK, 0:2, :].rearrange("v u (c n) -> v (u c) n", c=2)[:, b, :].rearrange("v (h k) -> v h k", k=RK),
                                            a["state_rwkv_S"][0, 4 * q + b, hh * HALF_H:(hh + 1) * HALF_H].rearrange("h v k -> v h k"),
                                        ).then_inc(s0_loaded, 16)
                                    if hh == 0 and q == 0:
                                        ada(1, (10, 11))
                                        for j in range(2):
                                            weight(a["rw_wo"][0][:, j * 512:(j + 1) * 512])
                else:
                    for j in range(6):
                        if j == 2:
                            w.take(norm_done)
                            sp.dma_start(wa2[0:16, :], a["gla_wa2"][0]).then_inc(gla_small_loaded, 16)
                            sp.dma_start(wa2[16:17, :], a["gla_ba"]).then_inc(gla_small_loaded, 16)
                        weight(a["gla_w_in"][0][:, j * 512:(j + 1) * 512])
                    weight(a["gla_w_in"][0][:, 3072:3088])
                    for j in range(2):
                        weight(a["gla_wo"][0][:, j * 512:(j + 1) * 512])
                    def gla_state(b):
                        return gS0[b].rearrange("p (b v) -> p b v", b=DEC_B)

                    for h in range(GH + 2):
                        if h == 2:
                            w.take(gla_prompt_new)
                            sp.dma_start(G_p[0, 0].rearrange("h k v -> k h v"), gS.rearrange("p (h v) -> p h v", h=GH)).then_inc(gla_prompt_stored, 16)
                        if h >= 2:
                            w.take(gla_state_new)
                            sp.dma_start(G_s[0, :, h - 2].rearrange("b k v -> k b v"), gla_state(h % 2)).then_inc(gla_state_stored[h % 2], 16)
                        if h < GH:
                            if h >= 2:
                                w.take(gla_state_stored[h % 2], 16)
                            sp.dma_start(gla_state(h % 2), a["state_gla_S"][0, :, h].rearrange("b k v -> k b v")).then_inc(gla_state_loaded[h % 2], 16)
                w.take(arena_free)
                sp.dma_start(sk[:, :, :], a["peer_subkeys"][li].rearrange("h s n k -> n (h s) k")).then_inc(keys_loaded, 16)
                for j in (*range(4), *SCORE_BLOCKS[2:]):
                    weight(a["peer_wq"][li][:, j * 512:(j + 1) * 512])
            w.take(y_ready)
            sp.dma_start(y_p[0].rearrange("(t p) d -> p t d", p=P), hc[:, 0:2, :]).then_inc(y_stored, 16)
            w.take(y_ready)
            sp.dma_start(y_s.rearrange("b t d -> (b t) d"), hc[0:32, SAMPLE, :]).then_inc(y_stored, 16)
            sp.wait_ge(y_stored, 32)
            sp.wait_ge(shift_stored, 32)
            sp.wait_ge(gla_prompt_stored, 16)
            sp.wait_ge(gla_state_stored[0], 32)
            sp.wait_ge(gla_state_stored[1], 32)

        @block.gpsimd
        def _(pool):
            w = Waits(pool)
            nv = [0]
            rounds = [0] * NGRP
            ncopy = [0]

            def vec(src, sample=False):
                b = nv[0] % VBUF
                if nv[0] >= VBUF:
                    w.take(vec_used)
                nv[0] += 1
                if sample:
                    for c in range(COPIES):
                        pool.dma_start(vring[32 * c:32 * c + 32, b, :],
                                       src[1:9, :].unsqueeze(1).to_broadcast([DEC_B, DEC_T, D])).then_inc(vec_loaded[b], 16)
                else:
                    nn = src.shape[1]
                    pool.dma_start(vring[:, b, 0:nn], src.to_broadcast([P, nn])).then_inc(vec_loaded[b], 16)

            def row(name, i=0):
                return a[name][i:i + 1, :]

            pool.memset(zeros[:], 0.0).then_inc(pool_consts, 1)
            pool.memset(ident[:], 0.0).then_inc(pool_consts, 1)
            pool.wait_ge(pool_consts, 2)
            pool.affine_select(out=ident[:], in_=ident[:], compare_op=ALU.not_equal, fill=1.0, base=0,
                               pattern=[[-1, P]], channel_multiplier=1).then_inc(pool_consts, 1)
            pool.iota(U(5)[:, 0:P].bitcast(I32), [[1, P]], base=0, channel_multiplier=0).then_inc(pool_consts, 1)
            pool.iota(U(5)[:, P:2 * P].bitcast(I32), [[0, P]], base=0, channel_multiplier=1).then_inc(pool_consts, 1)

            def norm_vecs(name, li, k, kinds=(False, True)):
                vec(row(name, li))
                for s in kinds:
                    vec(mod_d[li, k + 1] if s else mod_d[li, k + 1, 0:1], s)
                    vec(mod_d[li, k] if s else mod_d[li, k, 0:1], s)

            u_rows = a["peer_u"].rearrange("l n d -> (l n) d")
            v_rows = a["peer_v"].rearrange("l n d -> (l n) d")

            def gather(n, u, v):
                both = bool(u and v)
                sides = [(side, tab, *which) for side, tab, which in ((0, u_rows, u), (1, v_rows, v)) if which]
                turns = sorted((k, side, g, tab, t, first) for side, tab, t, first in sides
                               for k, g in enumerate(groups_of(side, both)))
                per = len(turns) // len(sides) * GRP
                with pool.Fori(0, n // per) as i:
                    for m, (k, side, g, tab, t, first) in enumerate(turns):
                        pool.wait_ge(rows_used[g], i * GRP + (rounds[g] * GRP + 1))
                        pool.sem_inc(pool_passed, 1)
                        pool.tensor_copy(idx_grp[:, g * GRP:(g + 1) * GRP],
                                         idx[:, bass.ds(i * per + (t * P + first + k * GRP), GRP)]).then_inc(idx_copied, 1)
                        pool.wait_ge(idx_copied, i * NGRP + (ncopy[0] + m + 1))
                        pool.sem_inc(pool_passed, 1)
                        for s in range(g * GRP, (g + 1) * GRP):
                            pool.indirect_dma_start(ring[:, s, :], None, tab,
                                                    bass.IndirectOffsetOnAxis(idx_grp[:, s:s + 1], 0)).then_inc(rows_landed[g], 16)
                for g in range(NGRP):
                    rounds[g] += n // per
                ncopy[0] += NGRP * (n // per)

            def bias(li, k):
                vec(a["ada_b"][li:li + 1, k * D:(k + 1) * D])

            for k in range(2):
                bias(0, k)
            for li in range(2):
                if li == 0:
                    w.take(mod_stored, 2 * 16)
                    norm_vecs("norm1_g", li, 0)
                    for k in (2, 3):
                        bias(0, k)
                for t in range(NT):
                    if li == 0:
                        for name in ("rw_kk", "rw_ka", "rw_rk", "rw_lnx_w", "rw_lnx_b"):
                            if name == "rw_lnx_w":
                                for k in (2 * t, 2 * t + 1):
                                    bias(1, k)
                            vec(a["rw_rk"].rearrange("r h k -> r (h k)") if name == "rw_rk" else row(name))
                        if t < SAMPLE:
                            bias(0, 4 + t)
                    else:
                        vec(row("gla_gnorm"))
                if li == 0:
                    w.take(mod_stored, 10 * 16)
                vec(mod_d[li, 2, 0:1])
                norm_vecs("norm2_g", li, 3, (False,))
                vec(mod_d[li, 2, 0:1])
                vec(mod_d[li, 2], True)
                norm_vecs("norm2_g", li, 3)
                vec(mod_d[li, 5, 0:1])
                w.take(experts_chosen)
                for n, u, v, choice in SEGMENTS:
                    if choice:
                        w.take(experts_chosen)
                    gather(n, u, v)
                for kinds in ((False,), (True,)):
                    if kinds[0]:
                        vec(mod_d[li, 5], True)
                    if li == 0:
                        norm_vecs("norm1_g", 1, 0, kinds)
                    else:
                        vec(a["final_g"].rearrange("(o n) -> o n", o=1))

        @block.scalar
        def _(act):
            w = Waits(act)
            steps = {}
            nf = [0]
            nsp = [0]
            rounds = [0] * NGRP
            nst = [0, 0]
            tile_vecs = [9, 17, 25]

            def done(ins, s=None):
                s = s or scalar_step
                steps[s.name] = steps.get(s.name, 0) + 1
                ins.then_inc(s, 1)
                act.wait_ge(s, steps[s.name])

            def fill():
                w.take(psum_for_scalar)
                nf[0] += 1
                return psa[:, (nf[0] - 1) % 2, :]

            def copy_out(dst, cols, rows=P, func=ACT.Copy, scale=1.0):
                ps = fill()
                src = ps[0:rows, 0:cols]
                if len(dst.shape) == 3:
                    src = src.rearrange("p (x y) -> p x y", y=dst.shape[2])
                done(act.activation(dst, src, func, scale=scale), scalar_drained)

            def root(dst, src):
                w.take(vector_result)
                done(act.activation(dst, src, ACT.Sqrt))
                act.sem_inc(scalar_result, 1)

            w.take(small_loaded, 64)
            done(act.activation(crow[0:9, :], crow[0:9, :], ACT.Silu))
            act.sem_inc(operand_written, 1)
            copy_out(cT[:, :], KD * 9)
            copy_out(shiftT[:, :], KD * DEC_B)
            copy_out(muT[:, :], 48)
            act.sem_inc(arena_free, 1)

            def store_mod(li, k, n):
                w.take(mod_ready)
                act.dma_start(mod_d[li, k], vring[0:9, n % VBUF, :]).then_inc(mod_stored, 16)

            def to_hT(t):
                copy_out(hT[:, :, t * P:(t + 1) * P], D)

            for k in range(2):
                store_mod(0, k, k)
            def rows_in(*tiles):
                root(rstd[:, 0, tiles[0]:tiles[-1] + 1], rstd[:, 0, tiles[0]:tiles[-1] + 1])
                for t in tiles:
                    to_hT(t)

            for li in range(2):
                if li == 0:
                    rows_in(0, 1, 2)
                    act.sem_inc(scalar_result, 1)
                    for k in (2, 3):
                        store_mod(0, k, 5 + k)

                    def spill(i):
                        for j in range(2):
                            for t in range(NT):
                                b = nsp[0] % 3
                                if nsp[0] >= 3:
                                    act.wait_ge(spilled[b], 16 * (nsp[0] // 3))
                                copy_out(spill_buf[b], 512)
                                act.dma_start(rkv_d[i, t][:, j * 512:(j + 1) * 512], spill_buf[b]).then_inc(spilled[b], 16)
                                nsp[0] += 1

                    spill(0)
                    copy_out(loraT[0:64, 0, :], TOK, 64, ACT.Tanh)
                    spill(1)
                    spill(2)
                    copy_out(loraT[0:64, 1, :], TOK, 64)
                    copy_out(loraT[:, 2, :], TOK, P, ACT.Sigmoid)
                    for b in range(3):
                        act.wait_ge(spilled[b], 16 * 6)
                    act.sem_inc(all_spilled, 1)
                    act.sem_inc(scalar_result, 1)
                    for t in range(NT):
                        sample = t == SAMPLE
                        copy_out(U(0), D, func=ACT.Sigmoid)
                        copy_out(U(1), D, func=ACT.Sigmoid)
                        ps = fill()
                        done(act.activation(U(5), ps, ACT.Exp, scale=-DECAY_C))
                        done(act.activation(U(6), ps, ACT.Exp, scale=DECAY_C), scalar_drained)
                        nn = DEC_B if sample else 2
                        copy_out(pcs[:, :, 0:nn], KD * nn, func=ACT.Exp, scale=-DECAY_C)
                        done(act.activation(U(7), U(0), ACT.Exp, scale=DECAY_C))
                        act.sem_inc(scalar_result, 1)
                        root(s16[:, 0, :], s16[:, 0, :])
                        w.take(vector_result)
                        def turned(b):
                            ps = fill()
                            for i, name in enumerate(("atz", "rtz")):
                                z = b[name].rearrange("p (q e t) -> p q e t", q=PAIRS, e=2)
                                for e in range(2):
                                    r0 = 64 * e
                                    ins = act.activation(z[r0:r0 + 64, :, e, :],
                                                         ps[r0:r0 + 64, i * 512:(i + 1) * 512].rearrange("p (q t) -> p q t", q=PAIRS), ACT.Copy)
                                    done(ins, scalar_drained if i and e else None)
                            copy_out(b["turned"], D)

                        def store_next_mod():
                            for i in range(2):
                                store_mod(1, 2 * t + i, tile_vecs[t] + 3 + i)

                        if not sample:
                            for b in halves:
                                turned(b)
                            store_next_mod()
                            for b in halves:
                                copy_out(b["rhs"][:, 0:512], 512)
                            for k in range(1, 7):
                                for b in halves:
                                    copy_out(b["z"], D)
                            for b in halves:
                                copy_out(b["rhs"][:, 512:1024], 512)
                            for hh in range(2):
                                copy_out(cur[1][:, hh * 512:(hh + 1) * 512], 512)
                            if t == 1:
                                copy_out(U(8)[0:RK, :], D, RK)
                                act.dma_start(S_p[0, 0].rearrange("h v k -> v h k"),
                                              U(8)[0:RK, :].rearrange("v (h k) -> v h k", k=RK)).then_inc(state_stored[0], 16)
                                nst[0] += 16
                                act.wait_ge(state_stored[0], nst[0])
                            act.sem_inc(scalar_result, 1)
                        for hh in (range(2) if sample else ()):
                            turned(halves[0])
                            if hh == 0:
                                store_next_mod()
                            copy_out(U(3), D)
                            for q in range(2):
                                copy_out(U(14, 2).rearrange("p (q n) -> p q n", q=2)[:, q, :], D)
                                act.sem_inc(s0_used, 1)
                            act.sem_inc(scalar_result, 1)
                            copy_out(U(0)[:, 512:1024], 512)
                            act.sem_inc(scalar_result, 1)
                            for q in range(4):
                                i = q % 2
                                if nst[i]:
                                    act.wait_ge(state_stored[i], nst[i])
                                copy_out(U(8 + i)[0:RK, :], D, RK)
                                for b in range(2):
                                    act.dma_start(S_s[0, 2 * q + b, hh * HALF_H:(hh + 1) * HALF_H].rearrange("h v k -> v h k"),
                                                  U(8 + i)[0:RK, b * 512:(b + 1) * 512].rearrange("v (h k) -> v h k", k=RK)).then_inc(state_stored[i], 16)
                                    nst[i] += 16
                            for i in range(2):
                                if nst[i]:
                                    act.wait_ge(state_stored[i], nst[i])
                            act.sem_inc(scalar_result, 1)
                        root(s16[:, 1, :], s16[:, 1, :])
                        to_hT(t)
                        act.sem_inc(cur_used, 1)
                        act.sem_inc(scalar_result, 1)
                        if not sample:
                            store_mod(0, 4 + t, tile_vecs[t] + 7)
                else:
                    for h in range(GH):
                        copy_out(qT[:, h, :], TOK, scale=GK ** -0.5)
                    for h in range(GH):
                        copy_out(kT[:, h, :], TOK)
                    for j in range(2):
                        for t in range(NT):
                            copy_out(gv[t][:, j * 512:(j + 1) * 512], 512)
                    for j in range(2):
                        for t in range(NT):
                            copy_out(gr[t][:, j * 512:(j + 1) * 512], 512, func=ACT.Silu)
                    w.take(vector_result)
                    copy_out(alT[0:16, :], TOK, 16)
                    act.sem_inc(scalar_result, 1)
                    for turn_ in GLA_TURNS:
                        sample = turn_[0] == SAMPLE
                        sets = [gla_sets[t % 2] for t in turn_]
                        for b in sets:
                            w.take(vector_result)
                            done(act.activation(b["ex"], b["ex"], ACT.Exp, scale=-1.0))
                            act.sem_inc(scalar_result, 1)
                        for b in sets:
                            w.take(vector_result)
                            done(act.activation(b["ex"], b["ex"], ACT.Ln))
                            act.sem_inc(scalar_result, 1)
                        for b in sets:
                            copy_out(b["bT"], 512, scale=1.0 / TAU)
                            act.sem_inc(scalar_result, 1)
                        for k in (range(2) if sample else range(7)):
                            m = 1 << k
                            for b in sets:
                                w.take(vector_result)
                                d3 = b["df"].rearrange("p (b m) -> p b m", m=2 * m)
                                e3 = b["ex"].rearrange("p (b m) -> p b m", m=2 * m)
                                done(act.activation(e3[:, :, m:2 * m], d3[:, :, m:2 * m], ACT.Exp))
                                done(act.activation(e3[:, :, 0:m], d3[:, :, 0:m], ACT.Exp, scale=-1.0))
                                act.sem_inc(scalar_result, 1)
                        nb = DEC_B if sample else 1
                        for b in sets:
                            w.take(vector_result)
                            done(act.activation(b["ex"], b["bT"], ACT.Exp))
                            done(act.activation(b["df"], b["df"], ACT.Exp))
                            src = b["bT"].rearrange("p (h s i) -> p h s i", h=GH, i=DEC_T)[:, :, 0:DEC_B, DEC_T - 1] if sample else \
                                b["bT"].rearrange("p (h s) -> p h s", h=GH)[:, :, P - 1:P]
                            done(act.activation(b["ebt"].rearrange("p (h b) -> p h b", h=GH)[:, :, 0:nb], src, ACT.Exp))
                            act.sem_inc(scalar_result, 1)
                        for b in sets:
                            copy_out(b["kd"], 512)
                            act.sem_inc(scalar_result, 1)
                        for t in turn_:
                            root(rstd[:, t % 2, :], rstd[:, t % 2, :])
                        for t in turn_:
                            to_hT(t)
                            act.sem_inc(scalar_result, 1)
                rows_in(0)
                for i in range(2):
                    copy_out(skT[:, 8 * i:8 * i + 8, :], D)
                root(rstd[:, 0, 1:3], rstd[:, 0, 1:3])
                for blk in range(4):
                    copy_out(qa[blk % 2], 512)
                for t in (1, 2):
                    to_hT(t)
                for hp in range(HP):
                    copy_out(qb[hp % 2], 2 * P)
                def diagonals(n, t, first, both):
                    groups = groups_of(1, both)
                    per = len(groups) * GRP
                    with act.Fori(0, n // per) as i:
                        for k, g in enumerate(groups):
                            act.wait_ge(rows_used[g], i * GRP + (rounds[g] * GRP + 1))
                            for s in range(GRP):
                                act.activation(diag[:, g * GRP + s, :], rep32[:, :] if t == SAMPLE else ident[:, :], ACT.Copy,
                                               scale=acts[:, t % 2, bass.ds(i * per + (first + k * GRP + s), 1)]).then_inc(diag_ready, 1)

                for n, u, v, choice in SEGMENTS:
                    both = bool(u and v)
                    if v:
                        diagonals(n, *v, both)
                    for g in range(NGRP):
                        rounds[g] += n // (len(groups_of(0, both)) * GRP)
                    if u and u[1] + n == experts_of(u[0]):
                        t, slots = u[0], experts_of(u[0])
                        w.take(vector_result)
                        done(act.activation(gate[:, t, 0:slots], gate[:, t, 0:slots], ACT.Exp))
                        done(act.activation(acts[:, t % 2, 0:slots], acts[:, t % 2, 0:slots], ACT.Gelu))
                        act.sem_inc(scalar_result, 1)
                        w.take(vector_result)
                if li == 0:
                    rows_in(0, 1)
                    rows_in(SAMPLE)
                else:
                    for tiles in (slice(0, 2), slice(2, 3)):
                        root(rstd[:, 0, tiles], rstd[:, 0, tiles])

        @block.vector
        def _(dve):
            w = Waits(dve)
            steps = {}
            nf = [0]
            nv = [0]
            vd = [0] * VBUF
            rounds = [0] * NGRP
            ncopied = [0]
            am_made = [0]

            def done(ins, s=None):
                s = s or vector_step
                steps[s.name] = steps.get(s.name, 0) + 1
                ins.then_inc(s, 1)
                dve.wait_ge(s, steps[s.name])

            def tt(out, i0, i1, op, s=None):
                done(dve.tensor_tensor(out, i0, i1, op), s)

            def ts(out, i0, a1, a2, o0, o1=None, s=None):
                done(dve.tensor_scalar(out, i0, a1, a2, o0, o1) if o1 is not None else dve.tensor_scalar(out, i0, a1, None, o0), s)

            def stt(out, i0, sc, i1, o0, o1, s=None):
                done(dve.scalar_tensor_tensor(out=out, in0=i0, scalar=sc, in1=i1, op0=o0, op1=o1), s)

            def fill():
                w.take(psum_for_vector)
                nf[0] += 1
                return psv[:, (nf[0] - 1) % 2, :]

            def vec(k=1):
                b = nv[0] % VBUF
                vd[b] += 16 * k
                dve.wait_ge(vec_loaded[b], vd[b])
                nv[0] += 1
                return vring[:, b, :]

            MUL, ADD, SUB = ALU.mult, ALU.add, ALU.subtract

            w.take(pool_consts, 5)
            ci, ri = U(5)[:, 0:P].bitcast(I32), U(5)[:, P:2 * P].bitcast(I32)
            c2, r2 = U(6)[:, 0:P].bitcast(I32), U(6)[:, P:2 * P].bitcast(I32)
            cf, rf = U(7)[:, 0:P], U(7)[:, P:2 * P]
            eq = U(8).rearrange("p (k n) -> p k n", k=8)
            done(dve.tensor_copy(cf, ci))
            done(dve.tensor_copy(rf, ri))
            tt(le[:], rf, cf, ALU.is_le)
            tt(lt[:], rf, cf, ALU.is_lt)
            for k in range(7):
                ts(c2, ci, k, None, ALU.arith_shift_right)
                ts(r2, ri, k, None, ALU.arith_shift_right)
                tt(eq[:, k, :], c2, r2, ALU.is_equal)
                if k == 2:
                    tt(seq_ind[:], ci[:, 0:DEC_B], r2[:, 0:DEC_B], ALU.is_equal)
            done(dve.memset(eq[:, 7, :], 1.0))
            for k in range(7):
                tt(lev[:, k, :], eq[:, k + 1, :], eq[:, k, :], SUB)
            tt(le4[:], le[:], eq[:, 2, :], MUL)
            tt(lt4[:], lt[:], eq[:, 2, :], MUL)
            tt(low0[:], rf, cf, ALU.is_gt)
            tt(low0[:], low0[:], lev[:, 0, :], MUL)
            ts(half_ind[:, 0:1], rf[:, 0:1], 63.5, None, ALU.is_le)
            ts(half_ind[:, 1:2], rf[:, 0:1], 63.5, None, ALU.is_gt)
            tt(cum_mid[:], le[:], half_ind[:, 0:1].to_broadcast([P, P]), SUB)
            ts(c2, ci, 31, None, ALU.bitwise_and)
            ts(r2, ri, 31, None, ALU.bitwise_and)
            tt(rep32[:], c2, r2, ALU.is_equal)
            done(dve.tensor_reduce(own_seq[:], rep32[:, 0:DEC_B * DEC_T].rearrange("p (b i) -> p b i", i=DEC_T), AXX, ADD))
            done(dve.tensor_copy(iota16[:], cf[:, 0:TOPK]))
            done(dve.memset(stateT[:], 0.0))
            for g in range(NGRP):
                dve.sem_inc(rows_used[g], 1)
            dve.sem_inc(consts_built, 1)

            def norm(tiles):
                var = rstd[:, 0, tiles[0]:tiles[-1] + 1]
                for t in tiles:
                    done(dve.tensor_tensor_reduce(hc[:, t, :], x[:, t, :], x[:, t, :], 1.0, 0.0, MUL, ADD, rstd[:, 0, t:t + 1]))
                ts(var, var, 1.0 / D, EPS, MUL, ADD)
                dve.sem_inc(vector_result, 1)
                w.take(scalar_result)
                done(dve.reciprocal(var, var))
                g = vec()
                for t in tiles:
                    stt(hc[:, t, :], x[:, t, :], rstd[:, 0, t:t + 1], g, MUL, MUL)
                dve.sem_inc(vec_used, 1)

            def adaln(tiles):
                norm(tiles)
                for same in ([t for t in tiles if t != SAMPLE], [t for t in tiles if t == SAMPLE]):
                    if same:
                        k = 4 if same == [SAMPLE] else 1
                        sc = vec(k)
                        for t in same:
                            stt(hc[:, t, :], sc, 1.0, hc[:, t, :], ADD, MUL)
                        dve.sem_inc(vec_used, 1)
                        sh = vec(k)
                        for t in same:
                            tt(hc[:, t, :], hc[:, t, :], sh, ADD)
                        dve.sem_inc(vec_used, 1)
                dve.sem_inc(operand_written, 1)

            def gated_add(t, tmp):
                g = vec(4 if t == SAMPLE else 1)
                tt(tmp, fill(), g, MUL, vector_drained)
                dve.sem_inc(vec_used, 1)
                tt(x[:, t, :], x[:, t, :], tmp, ADD)

            def top16(vals, idxs, src, scratch):
                done(dve.max(vals[:, 0:8], src))
                done(dve.max_index(idxs[:, 0:8], vals[:, 0:8], src))
                done(dve.match_replace(scratch, vals[:, 0:8], src, LOWEST))
                done(dve.max(vals[:, 8:16], scratch))
                done(dve.max_index(idxs[:, 8:16], vals[:, 8:16], scratch))

            def bc(ap, n):
                return ap.unsqueeze(2).to_broadcast([P, ap.shape[1], n])

            def modulation():
                b = vec()
                tt(b[0:9, :], fill()[0:9, :], b[0:9, :], ADD, vector_drained)
                dve.sem_inc(mod_ready, 1)

            def modulation_stored(n):
                w.take(mod_stored, 16 * n)
                dve.sem_inc(vec_used, n)

            for k in range(2):
                modulation()
            modulation_stored(2)
            w.take(x_loaded, 6 * 16)
            for li in range(2):
                if li == 0:
                    adaln((0, 1, 2))
                dve.sem_inc(norm_done, 1)
                if li == 0:
                    w.take(scalar_result)
                    n = 2 * P
                    tt(xx[:, :, 1:n], hT[:, :, 0:n - 1], hT[:, :, 1:n], SUB)
                    ts(xx[:, :, 0:1], hT[:, :, 0:1], -1.0, None, MUL)
                    xs4 = xx[:, :, n:].rearrange("p k (s i) -> p k s i", i=DEC_T)
                    hs4 = hT[:, :, n:].rearrange("p k (s i) -> p k s i", i=DEC_T)
                    for k in range(KD):
                        tt(xs4[:, k, :, 1:DEC_T], hs4[:, k, :, 0:DEC_T - 1], hs4[:, k, :, 1:DEC_T], SUB)
                    sT = shiftT[:, :].rearrange("p (k b) -> p k b", k=KD)
                    for c in range(COPIES):
                        tt(xs4[:, :, c * DEC_B:(c + 1) * DEC_B, 0], sT, hs4[:, :, c * DEC_B:(c + 1) * DEC_B, 0], SUB)
                    done(dve.memset(loraT[64:65, 0:2, :], 1.0))
                    for n, i in enumerate((0, 3, 1, 2, 4, 5)):
                        if n >= 2:
                            w.take(mix_used)
                        for k in range(KD):
                            stt(mixb[n % 2][:, k, :], xx[:, k, :], muT[:, i * KD + k:i * KD + k + 1], hT[:, k, :], MUL, ADD)
                        dve.sem_inc(operand_written, 1)
                        if n == 0:
                            modulation()
                            modulation()
                    modulation_stored(2)
                    w.take(scalar_result)
                    w.take(shift_stored, 32)
                    for name in ("atz", "rtz"):
                        done(dve.memset(halves[1][name], 0.0))
                    for t in range(NT):
                        sample = t == SAMPLE
                        r, k_, v = cur
                        w.take(cur_loaded, 48)
                        g = vec()
                        tt(U(2), k_, g, MUL)
                        dve.sem_inc(vec_used, 1)
                        tt(U(3), U(2), U(2), MUL)
                        done(dve.tensor_reduce(s16[:, 0, :], heads(U(3), RH, RK), AXX, ADD))
                        w.take(scalar_result)
                        dve.sem_inc(vector_result, 1)
                        w.take(scalar_result)
                        ts(s16[:, 0, :], s16[:, 0, :], 1e-12, None, ALU.max)
                        done(dve.reciprocal(s16[:, 0, :], s16[:, 0, :]))
                        tt(heads(U(2), RH, RK), heads(U(2), RH, RK), bc(s16[:, 0, :], RK), MUL)
                        g = vec()
                        stt(U(3), U(1), -1.0, g, ADD, MUL)
                        dve.sem_inc(vec_used, 1)
                        stt(U(4), U(3), 1.0, k_, ADD, MUL)
                        g = vec()
                        tt(U(3), U(4), r, MUL)
                        tt(U(3), U(3), g, MUL)
                        dve.sem_inc(vec_used, 1)
                        done(dve.tensor_reduce(bonus[:], heads(U(3), RH, RK), AXX, ADD))
                        tt(U(1), U(1), U(2), MUL)
                        tt(U(1), U(1), U(6), MUL)
                        stt(U(2), U(2), -1.0, U(7), MUL, MUL)
                        tt(U(2), U(2), U(5), MUL)
                        tt(r, r, U(5), MUL)
                        tt(U(4), U(4), U(6), MUL)
                        done(dve.memset(U(5), 0.0))
                        done(dve.memset(U(6), 0.0))
                        dve.sem_inc(vector_result, 1)
                        dve.sem_inc(operand_written, 1)
                        for k in range(2):
                            modulation()
                        strict, incl = (lt4, le4) if sample else (lt, le)

                        def m8(m):
                            return m.unsqueeze(1).to_broadcast([P, HALF_H, P])

                        h8 = lambda ap: heads(ap, HALF_H, P)

                        def attention(b):
                            tt(h8(b["nt"]), h8(fill()), m8(strict[:]), MUL, vector_drained)
                            tt(h8(b["t"]), h8(fill()), m8(low0[:]), MUL, vector_drained)
                            tt(h8(b["ak"]), h8(fill()), m8(strict[:]), MUL, vector_drained)
                            tt(h8(b["rb"]), h8(fill()), m8(incl[:]), MUL, vector_drained)
                            tt(h8(b["rk"]), h8(fill()), m8(incl[:]), MUL, vector_drained)
                            tt(h8(b["t"]), h8(b["t"]), m8(ident[:]), ADD)
                            tt(h8(b["tt"]), h8(b["nt"]), m8(lev[:, 0, :]), MUL)
                            tt(h8(b["tt"]), h8(b["tt"]), m8(ident[:]), ADD)

                        def level_part(b, k):
                            tt(h8(b["lt"]), h8(b["nt"]), m8(lev[:, k, :]), MUL)

                        if not sample:
                            tt(st_in[:], stateT[:], pcs[:, :, 0:1].to_broadcast([P, KD, RK]), MUL)
                            for b in halves:
                                attention(b)
                                level_part(b, 1)
                                dve.sem_inc(operand_written, 1)
                            for k in range(1, 7):
                                m = 1 << k
                                for b in halves:
                                    if k < 6:
                                        t_even = blocks(b["t"], m, 0)
                                        tt(t_even, t_even, compact(fill()[:, 0:512], m), ADD, vector_drained)
                                        level_part(b, k + 1)
                                    tt_odd = blocks(b["tt"], m, 1)
                                    tt(tt_odd, tt_odd, compact(fill()[:, 0:512], m), ADD, vector_drained)
                                    if k < 6:
                                        dve.sem_inc(operand_written, 1)
                            for hh in range(2):
                                sl = slice(hh * PAIRS, (hh + 1) * PAIRS)
                                ps = fill().rearrange("p (q e v) -> p q e v", q=PAIRS * 2, e=2)[:, 0:PAIRS]
                                for e in range(2):
                                    rr = slice(64 * e, 64 * e + 64)
                                    tt(st_in[rr, sl], st_in[rr, sl], ps[rr, :, e, :], ADD, vector_drained if e else None)
                            tt(stateT[:], st_in[:], pcs[:, :, 1:2].to_broadcast([P, KD, RK]), MUL)
                            if t == 1:
                                dve.sem_inc(operand_written, 1)
                            w.take(scalar_result)
                        for hh in (range(2) if sample else ()):
                            b = halves[0]
                            attention(b)
                            level_part(b, 1)
                            dve.sem_inc(operand_written, 1)
                            tt(b["tt"], b["tt"], fill(), ADD, vector_drained)
                            w.take(scalar_result)
                            kept = U(3)
                            for part in range(2):
                                for g2_ in range(PAIRS):
                                    prod = U(12).rearrange("p (e b v) -> p e b v", e=2, b=DEC_B)
                                    tt(prod, fill().rearrange("p (e b v) -> p e b v", e=2, b=DEC_B),
                                       own_seq[:].unsqueeze(1).unsqueeze(3).to_broadcast([P, 2, DEC_B, RK]), MUL, vector_drained)
                                    to = part * 512 + g2_ * P
                                    done(dve.tensor_reduce(heads(kept[:, to:to + P], 2, RK), prod.rearrange("p e b v -> p e v b"), AXX, ADD))
                                if part == 0:
                                    tt(b["rhs"][:, 0:512], kept[:, 0:512], fill()[:, 0:512], ADD, vector_drained)
                                    dve.sem_inc(operand_written, 1)
                            w.take(scalar_result)
                            s0 = U(14, 2).rearrange("p (b q v) -> p b q v", b=DEC_B, q=PAIRS)

                            def spread(q):
                                for src, dst in ((b["rhs"][:, 512 + P * q:512 + P * (q + 1)], wx[:, 2 * (q % 2), :]),
                                                 (v[:, hh * 512 + P * q:hh * 512 + P * (q + 1)], wx[:, 2 * (q % 2) + 1, :])):
                                    tt(dst.rearrange("p (e b v) -> p e b v", e=2, b=DEC_B),
                                       heads(src, 2, RK).unsqueeze(2).to_broadcast([P, 2, DEC_B, RK]),
                                       seq_ind[:].unsqueeze(1).unsqueeze(3).to_broadcast([P, 2, DEC_B, RK]), MUL)
                                dve.sem_inc(operand_written, 1)

                            spread(0)
                            spread(1)
                            tt(k_[:, hh * 512:(hh + 1) * 512], kept[:, 512:1024], fill()[:, 0:512], ADD, vector_drained)
                            for q in range(PAIRS):
                                ps = fill()
                                for e in range(2):
                                    rr = slice(64 * e, 64 * e + 64)
                                    tt(s0[rr, :, q, :], s0[rr, :, q, :], ps[rr, e * 512:(e + 1) * 512].rearrange("p (b v) -> p b v", b=DEC_B),
                                       ADD, vector_drained if e else None)
                                tt(s0[:, :, q, :], s0[:, :, q, :], bc(pcs[:, hh * PAIRS + q, :], RK), MUL)
                                if q + 2 < PAIRS:
                                    spread(q + 2)
                            dve.sem_inc(operand_written, 1)
                            w.take(scalar_result)
                        modulation_stored(2)
                        y = k_
                        mean, var = s16[:, 0, :], s16[:, 1, :]
                        done(dve.tensor_reduce(mean, heads(y, RH, RK), AXX, ADD))
                        ts(mean, mean, 1.0 / RK, None, MUL)
                        tt(heads(y, RH, RK), heads(y, RH, RK), bc(mean, RK), SUB)
                        tt(U(3), y, y, MUL)
                        done(dve.tensor_reduce(var, heads(U(3), RH, RK), AXX, ADD))
                        ts(var, var, 1.0 / RK, LNX_EPS, MUL, ADD)
                        dve.sem_inc(vector_result, 1)
                        w.take(scalar_result)
                        done(dve.reciprocal(var, var))
                        tt(heads(y, RH, RK), heads(y, RH, RK), bc(var, RK), MUL)
                        g = vec()
                        tt(y, y, g, MUL)
                        dve.sem_inc(vec_used, 1)
                        g = vec()
                        tt(y, y, g, ADD)
                        dve.sem_inc(vec_used, 1)
                        tt(heads(U(3), RH, RK), heads(v, RH, RK), bc(bonus[:], RK), MUL)
                        tt(y, y, U(3), ADD)
                        tt(y, y, fill(), MUL, vector_drained)
                        dve.sem_inc(operand_written, 1)
                        if not sample:
                            modulation()
                        w.take(scalar_result)
                        if not sample:
                            modulation_stored(1)
                else:
                    done(dve.memset(alT[0:17, :], 1.0))
                    dve.sem_inc(vector_result, 1)
                    w.take(scalar_result)
                    done(dve.memset(gS, 0.0))
                    for b in gla_sets:
                        for name in ("qe", "ke"):
                            done(dve.memset(b[name], 0.0))
                    h4 = lambda ap: heads(ap, GH, P)
                    m4 = lambda m: m.unsqueeze(1).to_broadcast([P, GH, P])

                    def level_blocks(ap, m, odd):
                        return ap.rearrange("p h (b two m) -> p h b two m", two=2, m=m)[:, :, :, odd, :]

                    def difference(b, k):
                        m = 1 << k
                        b3 = b["bT"].rearrange("p (b m) -> p b m", m=2 * m)
                        tt(b["df"].rearrange("p (b m) -> p b m", m=2 * m), b3,
                           b3[:, :, m - 1:m].to_broadcast([P, 512 // (2 * m), 2 * m]), SUB)
                        dve.sem_inc(vector_result, 1)

                    for turn_ in GLA_TURNS:
                        sample = turn_[0] == SAMPLE
                        tiles = [(t, gla_sets[t % 2], qT[:, :, t * P:(t + 1) * P], kT[:, :, t * P:(t + 1) * P]) for t in turn_]
                        for t, b, q3, k3 in tiles:
                            ps = fill()
                            ts(b["la"], ps[:, 0:512], 0.0, None, ALU.min)
                            stt(b["ex"], b["la"], -2.0, ps[:, 0:512], MUL, ADD, vector_drained)
                            dve.sem_inc(vector_result, 1)
                        for t, b, q3, k3 in tiles:
                            w.take(scalar_result)
                            ts(b["ex"], b["ex"], 1.0, None, ADD)
                            dve.sem_inc(vector_result, 1)
                        for t, b, q3, k3 in tiles:
                            w.take(scalar_result)
                            tt(b["la"], b["la"], b["ex"], SUB)
                            dve.sem_inc(operand_written, 1)
                        for t, b, q3, k3 in tiles:
                            w.take(scalar_result)
                            difference(b, 0)
                        for t, b, q3, k3 in tiles:
                            tt(h4(b["at"]), h4(fill()[:, 0:512]), m4(ident[:]), MUL, vector_drained)
                        last_level = 1 if sample else 6
                        for k in range(last_level + 1):
                            m = 1 << k
                            for t, b, q3, k3 in tiles:
                                w.take(scalar_result)
                                tt(level_blocks(h4(b["qe"]), m, 1), level_blocks(q3, m, 1), level_blocks(h4(b["ex"]), m, 1), MUL)
                                tt(level_blocks(h4(b["ke"]), m, 0), level_blocks(k3, m, 0), level_blocks(h4(b["ex"]), m, 0), MUL)
                                dve.sem_inc(operand_written, 1)
                            for t, b, q3, k3 in tiles:
                                if k < last_level:
                                    difference(b, k + 1)
                                elif sample:
                                    b4 = b["bT"].rearrange("p (b m) -> p b m", m=DEC_T)
                                    tt(b["df"].rearrange("p (b m) -> p b m", m=DEC_T), b4[:, :, 3:4].to_broadcast([P, P, DEC_T]), b4, SUB)
                                    dve.sem_inc(vector_result, 1)
                                else:
                                    tt(h4(b["df"]), h4(b["bT"])[:, :, P - 1:P].to_broadcast([P, GH, P]), h4(b["bT"]), SUB)
                                    dve.sem_inc(vector_result, 1)
                                tt(h4(b["atmp"]), h4(fill()[:, 0:512]), m4(lev[:, k, :]), MUL, vector_drained)
                                tt(b["at"], b["at"], b["atmp"], ADD)
                        for t, b, q3, k3 in tiles:
                            w.take(scalar_result)
                            tt(h4(b["ke"]), k3, h4(b["df"]), MUL)
                            tt(h4(b["qe"]), q3, h4(b["ex"]), MUL)
                            tt(h4(b["at"]), h4(b["at"]), m4((le4 if sample else le)[:]), MUL)
                            dve.sem_inc(operand_written, 1)
                        for t, b, q3, k3 in tiles:
                            w.take(scalar_result)
                        for t, b, q3, k3 in tiles:
                            go, ebt, kd, qe = b["go"], b["ebt"].rearrange("p (h b) -> p h b", h=GH), b["kd"], b["qe"]
                            if sample:
                                done(dve.memset(qem, 0.0))
                                for h in range(GH):
                                    done(dve.tensor_copy(diag_blocks(qem), own_rows(qe[:, h * P:(h + 1) * P])))
                                    tt(kdm.rearrange("p (b n) -> p b n", b=DEC_B), kd[:, h * P:(h + 1) * P].unsqueeze(1).to_broadcast([P, DEC_B, P]),
                                       bc(seq_ind[:], P), MUL)
                                    dve.sem_inc(operand_written, 1)
                                    s0 = gS0[h % 2].rearrange("p (b v) -> p b v", b=DEC_B)
                                    w.take(gla_state_loaded[h % 2], 16)
                                    done(dve.tensor_copy(go[:, h * GV:(h + 1) * GV], fill()[:, 0:GV]), vector_drained)
                                    tt(s0, s0, ebt[:, h, :].unsqueeze(2).to_broadcast([P, DEC_B, GV]), MUL)
                                    for q in range(2):
                                        tt(gS0[h % 2][:, q * D:(q + 1) * D], gS0[h % 2][:, q * D:(q + 1) * D], fill(), ADD, vector_drained)
                                    dve.sem_inc(gla_state_new, 1)
                            else:
                                dve.sem_inc(operand_written, 1)
                                done(dve.tensor_copy(go, fill()), vector_drained)
                                g3 = heads(gS, GH, GV)
                                tt(g3, g3, ebt[:, :, 0:1].to_broadcast([P, GH, GV]), MUL)
                                tt(gS, gS, fill(), ADD, vector_drained)
                                if t == 1:
                                    dve.sem_inc(gla_prompt_new, 1)
                        for t, b, q3, k3 in tiles:
                            var = rstd[:, t % 2, :]
                            tt(b["square"], b["go"], b["go"], MUL)
                            done(dve.tensor_reduce(var, heads(b["square"], GH, GV), AXX, ADD))
                            ts(var, var, 1.0 / GV, EPS, MUL, ADD)
                            dve.sem_inc(vector_result, 1)
                        for t, b, q3, k3 in tiles:
                            var, go = rstd[:, t % 2, :], b["go"]
                            w.take(scalar_result)
                            done(dve.reciprocal(var, var))
                            tt(heads(go, GH, GV), heads(go, GH, GV), bc(var, GV), MUL)
                            g = vec()
                            tt(heads(go, GH, GV), heads(go, GH, GV), g[:, 0:GV].unsqueeze(1).to_broadcast([P, GH, GV]), MUL)
                            dve.sem_inc(vec_used, 1)
                            tt(go, go, gr[t], MUL)
                            dve.sem_inc(operand_written, 1)
                        for t in turn_:
                            w.take(scalar_result)
                    dve.wait_ge(gla_prompt_stored, 16)
                    dve.wait_ge(gla_state_stored[0], 32)
                    dve.wait_ge(gla_state_stored[1], 32)
                dve.sem_inc(arena_free, 1)
                gated_add(0, U(2))
                adaln((0,))
                for t in (1, 2):
                    gated_add(t, U(2))
                adaln((1, 2))
                def best_keys(blk, tiles):
                    per_fill = 4 if len(tiles) == 1 else 1
                    for n in range(4):
                        if n % per_fill == 0:
                            ps = fill()
                        for i, t in enumerate(tiles):
                            c = (n % per_fill + i) * P
                            top16(top_s[:, t, 4 * blk + n, :], top_i[:, t, 4 * blk + n, :], ps[:, c:c + P], U(20)[:, 512:512 + P])
                        if n % per_fill == per_fill - 1:
                            dve.sem_inc(vector_drained, 1)
                            steps[vector_drained.name] += 1

                for blk in range(4):
                    best_keys(blk, (0,))

                def choose(t):
                    s4 = top_s[:, t].rearrange("p (h s) e -> p h s e", s=2)
                    tt(cand.rearrange("p (h i j) -> p h i j", h=PH, i=TOPK),
                       s4[:, :, 0, :].unsqueeze(3).to_broadcast([P, PH, TOPK, TOPK]),
                       s4[:, :, 1, :].unsqueeze(2).to_broadcast([P, PH, TOPK, TOPK]), ADD)
                    for h in range(PH):
                        top16(sc[:, h * TOPK:(h + 1) * TOPK], pos[:, h * TOPK:(h + 1) * TOPK], cand[:, h * 256:(h + 1) * 256], rest)
                    done(dve.tensor_copy(iF, top_i[:, t].rearrange("p i e -> p (i e)")))
                    i4 = iF.rearrange("p (h s e) -> p h s e", h=PH, s=2)
                    for side, e_out in ((0, e1), (1, e2)):
                        if side == 0:
                            ts(pi, pos, 4, None, ALU.logical_shift_right)
                        else:
                            ts(pi, pos, 15, None, ALU.bitwise_and)
                        done(dve.tensor_copy(pf, pi))
                        o3 = onehot.rearrange("p (n c) -> p n c", c=TOPK)
                        tt(o3, iota16[:].unsqueeze(1).to_broadcast([P, P, TOPK]), bc(pf, TOPK), ALU.is_equal)
                        o4 = onehot.rearrange("p (h e c) -> p h e c", h=PH, e=TOPK)
                        tt(o4, o4, i4[:, :, side, :].unsqueeze(2).to_broadcast([P, PH, TOPK, TOPK]), MUL)
                        done(dve.tensor_reduce(e_out, o3, AXX, ADD))
                    stt(e1, e1, float(NKEYS), e2, MUL, ADD)
                    if li:
                        ts(e1, e1, float(li * NKEYS * NKEYS), None, ADD)
                    s3 = sc.rearrange("p (h e) -> p h e", h=PH)
                    below = e2 if t == SAMPLE else gate[:, t, :]
                    tt(below.rearrange("p (h e) -> p h e", h=PH), s3, s3[:, :, 0:1].to_broadcast([P, PH, TOPK]), SUB)
                    if t == SAMPLE:
                        for c in range(COPIES):
                            rr = slice(32 * c, 32 * c + 32)
                            done(dve.tensor_copy(gate[rr, t, 0:32], e2[rr, rr]))
                            done(dve.tensor_copy(idx[rr, t * P:t * P + 32], e1[rr, rr]))
                    else:
                        done(dve.tensor_copy(idx[:, t * P:(t + 1) * P], e1))
                    dve.sem_inc(experts_chosen, 1)

                def products(n, t, first, both):
                    groups = groups_of(0, both)
                    per = len(groups) * GRP
                    with dve.Fori(0, n // per) as i:
                        for k, g in enumerate(groups):
                            dve.wait_ge(rows_landed[g], i * (16 * GRP) + (rounds[g] + 1) * 16 * GRP)
                            for s in range(GRP):
                                row = ring[:, g * GRP + s, :]
                                dve.tensor_tensor_reduce(row, row, hc[:, t, :], 1.0, 0.0, MUL, ADD,
                                                         act16[:, k * GRP + s:k * GRP + s + 1]).then_inc(rows_used[g], 1)
                        for g in groups:
                            dve.wait_ge(rows_used[g], i * GRP + (rounds[g] + 1) * GRP + 1)
                        dve.tensor_copy(acts[:, t % 2, bass.ds(i * per + first, per)], act16[:, 0:per]).then_inc(acts_copied, 1)
                        dve.wait_ge(acts_copied, i + (ncopied[0] + 1))
                    ncopied[0] += n // per

                def weigh(t):
                    slots = experts_of(t)
                    nh = slots // TOPK
                    dve.sem_inc(vector_result, 1)
                    w.take(scalar_result)
                    g3 = gate[:, t, 0:slots].rearrange("p (h e) -> p h e", h=nh)
                    done(dve.tensor_reduce(s16[:, 0, 0:nh], g3, AXX, ADD))
                    done(dve.reciprocal(s16[:, 0, 0:nh], s16[:, 0, 0:nh]))
                    tt(g3, g3, bc(s16[:, 0, 0:nh], TOPK), MUL)
                    tt(acts[:, t % 2, 0:slots], acts[:, t % 2, 0:slots], gate[:, t, 0:slots], MUL)
                    dve.sem_inc(vector_result, 1)

                def add_experts(t, gain):
                    tt(peer_tmp, fill(), gain, MUL, vector_drained)
                    tt(x[:, t, :], x[:, t, :], peer_tmp, ADD)

                gain = vec()
                choose(0)
                for turn_, (n, u, v, choice) in enumerate(SEGMENTS):
                    if choice:
                        choose(u[0])
                    both = bool(u and v)
                    if u:
                        products(n, *u, both)
                    if turn_ < 4:
                        best_keys(SCORE_BLOCKS[turn_], (1, SAMPLE))
                    for g in range(NGRP):
                        rounds[g] += n // (len(groups_of(0, both)) * GRP)
                    if u:
                        if u[1] + n == experts_of(u[0]):
                            weigh(u[0])
                            if u[0] == 1:
                                add_experts(0, gain)
                enter = adaln if li == 0 else norm
                add_experts(1, gain)
                dve.sem_inc(vec_used, 1)
                enter((0, 1))
                if li:
                    dve.sem_inc(y_ready, 1)
                add_experts(SAMPLE, vec(4))
                dve.sem_inc(vec_used, 1)
                enter((SAMPLE,))
            dve.sem_inc(y_ready, 1)

        @block.tensor
        def _(pe):
            w = Waits(pe)
            nfv, nfa, nw = [0], [0], [0]
            rounds = [0] * NGRP
            ndiag = [0]

            def for_vector():
                if nfv[0] >= 2:
                    pe.wait_ge(vector_drained, nfv[0] - 1)
                nfv[0] += 1
                return psv[:, (nfv[0] - 1) % 2, :]

            def for_scalar():
                if nfa[0] >= 2:
                    pe.wait_ge(scalar_drained, nfa[0] - 1)
                nfa[0] += 1
                return psa[:, (nfa[0] - 1) % 2, :]

            def scalar_copies():
                pe.wait_ge(scalar_drained, nfa[0])

            def vector_copies():
                pe.wait_ge(vector_drained, nfv[0])

            def weight():
                b = nw[0] % WBUF
                pe.wait_ge(weight_loaded[b], 16 * (nw[0] // WBUF + 1))
                nw[0] += 1
                return wring[:, b]

            def mm(out, lhsT, rhs, start=True, stop=True):
                return nc.tensor.matmul(out, lhsT, rhs, start=start, stop=stop)

            def rows_product(ps, t, wt, cols=512, at_=0):
                for k in range(KD):
                    last = mm(ps[:, at_:at_ + cols], hT[:, k, t * P:(t + 1) * P], wt[:, k, 0:cols], k == 0, k == KD - 1)
                return last

            def turn(src, ps, n=8):
                for k in range(n):
                    last = nc.tensor.transpose(ps[:, k * P:(k + 1) * P], src[:, k * P:(k + 1) * P], ident[:])
                return last

            def h_turned(*tiles):
                w.take(operand_written)
                for t in tiles:
                    turn(hc[:, t, :], for_scalar()).then_inc(psum_for_scalar, 1)

            def project_out():
                scalar_copies()
                wts = [weight(), weight()]
                for t in range(NT):
                    ps = for_vector()
                    for j in range(2):
                        last = rows_product(ps, t, wts[j], 512, j * 512)
                    last.then_inc(psum_for_vector, 1)
                pe.wait_ge(psum_for_vector, nfv[0])
                for j in range(2):
                    pe.sem_inc(weight_used, 1)

            pe.wait_ge(consts_built, 1)
            w.take(operand_written)
            ps = for_scalar()
            for k in range(KD):
                last = nc.tensor.transpose(ps[:, k * 9:(k + 1) * 9], crow[0:9, k * P:(k + 1) * P], ident[0:9, 0:9])
            last.then_inc(psum_for_scalar, 1)
            ps = for_scalar()
            for k in range(KD):
                last = nc.tensor.transpose(ps[:, k * DEC_B:(k + 1) * DEC_B], srow[0:DEC_B, k * P:(k + 1) * P], ident[0:8, 0:8])
            last.then_inc(psum_for_scalar, 1)
            nc.tensor.transpose(for_scalar()[:, 0:48], murow[0:48, :], ident[0:48, 0:48]).then_inc(psum_for_scalar, 1)
            scalar_copies()

            def modulation():
                ps = for_vector()
                for j in range(2):
                    wt = weight()
                    for kk in range(KD):
                        last = mm(ps[0:9, j * 512:(j + 1) * 512], cT[:, kk * 9:(kk + 1) * 9], wt[:, kk, :], kk == 0, kk == KD - 1)
                    last.then_inc(weight_used if j == 0 else psum_for_vector, 1)
                pe.wait_ge(psum_for_vector, nfv[0])
                pe.sem_inc(weight_used, 1)

            for k in range(2):
                modulation()
            for li in range(2):
                if li == 0:
                    h_turned(0, 1, 2)
                    for k in range(2):
                        modulation()
                    pe.wait_ge(lora_loaded, 16 * 8)
                    for n, i in enumerate((0, 3, 1, 2, 4, 5)):
                        w.take(operand_written)
                        mx = mixb[n % 2]
                        if i < 3:
                            for j in range(2):
                                wt = weight()
                                for t in range(NT):
                                    ps = for_scalar()
                                    for k in range(KD):
                                        last = mm(ps[:, 0:512], mx[:, k, t * P:(t + 1) * P], wt[:, k, :], k == 0, k == KD - 1)
                                    last.then_inc(psum_for_scalar, 1)
                                pe.wait_ge(psum_for_scalar, nfa[0])
                                pe.sem_inc(weight_used, 1)
                        else:
                            lo, m = ((0, 64), (64, 64), (128, P))[i - 3]
                            ps = for_scalar()
                            for k in range(KD):
                                last = mm(ps[0:m, 0:TOK], lora1[:, k, lo:lo + m], mx[:, k, :], k == 0, k == KD - 1)
                            last.then_inc(psum_for_scalar, 1)
                            pe.wait_ge(psum_for_scalar, nfa[0])
                        if n < 4:
                            pe.sem_inc(mix_used, 1)
                    scalar_copies()
                    for t in range(NT):
                        sample = t == SAMPLE
                        if t:
                            scalar_copies()
                        for i in range(2):
                            ps = for_scalar()
                            for j in range(2):
                                last = mm(ps[:, j * 512:(j + 1) * 512], loraT[0:65, i, t * P:(t + 1) * P], lora2[0:65, i, j * 512:(j + 1) * 512])
                            last.then_inc(psum_for_scalar, 1)
                        scalar_copies()
                        ps = for_scalar()
                        for j in range(2):
                            last = mm(ps[:, j * 512:(j + 1) * 512], (le4 if sample else cum_mid)[:], U(0)[:, j * 512:(j + 1) * 512])
                        last.then_inc(psum_for_scalar, 1)
                        ps = for_scalar()
                        ind, nn = (seq_ind, DEC_B) if sample else (half_ind, 2)
                        for k in range(KD):
                            last = mm(ps[:, k * nn:(k + 1) * nn], U(0)[:, k * P:(k + 1) * P], ind[:])
                        last.then_inc(psum_for_scalar, 1)
                        for k in range(2):
                            modulation()
                        w.take(operand_written)
                        r, y, v = cur

                        def turn_half(hh):
                            o = hh * 512
                            ps = for_scalar()
                            turn(U(2)[:, o:o + 512], ps[:, 0:512], 4)
                            turn(r[:, o:o + 512], ps[:, 512:1024], 4).then_inc(psum_for_scalar, 1)
                            ps = for_scalar()
                            turn(U(1)[:, o:o + 512], ps[:, 0:512], 4)
                            turn(U(4)[:, o:o + 512], ps[:, 512:1024], 4).then_inc(psum_for_scalar, 1)

                        def hd(ap, h):
                            return ap[:, h * P:(h + 1) * P]

                        def attention(b):
                            bT_ = lambda h: hd(b["turned"], h // 2)
                            kT_ = lambda h: hd(b["turned"], PAIRS + h // 2)
                            az, rz = lambda h: hd(b["atz"], h), lambda h: hd(b["rtz"], h)
                            for lhs, rhs in ((bT_, az), (az, bT_), (kT_, az), (bT_, rz), (kT_, rz)):
                                ps = for_vector()
                                for h in range(HALF_H):
                                    last = mm(ps[:, h * P:(h + 1) * P], lhs(h), rhs(h))
                                last.then_inc(psum_for_vector, 1)

                        def level(b):
                            ps = for_scalar()
                            for h in range(HALF_H):
                                last = mm(ps[:, h * P:(h + 1) * P], hd(b["lt"], h), hd(b["t"], h))
                            last.then_inc(psum_for_scalar, 1)
                            return nfa[0]

                        def solve(b):
                            ps = for_scalar()
                            for h in range(HALF_H):
                                last = mm(ps[:, h * RK:(h + 1) * RK], hd(b["tt"], h), b["rhs"][:, h * RK:(h + 1) * RK])
                            last.then_inc(psum_for_scalar, 1)
                            return nfa[0]

                        if not sample:
                            turn_half(0)
                            first = nfa[0]
                            turn_half(1)
                            second = nfa[0]
                            pe.wait_ge(scalar_drained, first)
                            attention(halves[0])
                            pe.wait_ge(scalar_drained, second)
                            attention(halves[1])
                            for hh, b in enumerate(halves):
                                o = hh * 512
                                w.take(operand_written)
                                ps = for_scalar()
                                for h in range(HALF_H):
                                    out = ps[:, h * RK:(h + 1) * RK]
                                    mm(out, hd(b["atz"], h), st_in[:, hh * PAIRS + h // 2, :], True, False)
                                    last = mm(out, hd(b["ak"], h), v[:, o + h * RK:o + (h + 1) * RK], False, True)
                                last.then_inc(psum_for_scalar, 1)
                            for k in range(1, 7):
                                m = 1 << k
                                marks = []
                                for b in halves:
                                    if k > 1:
                                        w.take(operand_written)
                                    marks.append(level(b))
                                solved = []
                                for b, mark in zip(halves, marks):
                                    pe.wait_ge(scalar_drained, mark)
                                    for lhs, rhs, odd in ([(b["tt"], b["z"], 0)] if k < 6 else []) + [(b["z"], b["tt"], 1)]:
                                        ps = for_vector()
                                        for h in range(HALF_H):
                                            last = mm(compact(ps[:, h * RK:(h + 1) * RK], m), hd(lhs, h), blocks(hd(rhs, h), m, odd))
                                        last.then_inc(psum_for_vector, 1)
                                    solved.append(nfv[0])
                            marks = []
                            for b, mark in zip(halves, solved):
                                pe.wait_ge(vector_drained, mark)
                                marks.append(solve(b))
                            for hh, (b, mark) in enumerate(zip(halves, marks)):
                                o = hh * 512
                                pe.wait_ge(scalar_drained, mark)
                                sa = b["rhs"][:, 512:1024]
                                ps = for_scalar()
                                for h in range(HALF_H):
                                    out = ps[:, h * RK:(h + 1) * RK]
                                    mm(out, hd(b["rtz"], h), st_in[:, hh * PAIRS + h // 2, :], True, False)
                                    mm(out, hd(b["rb"], h), sa[:, h * RK:(h + 1) * RK], False, False)
                                    last = mm(out, hd(b["rk"], h), v[:, o + h * RK:o + (h + 1) * RK], False, True)
                                last.then_inc(psum_for_scalar, 1)
                                ps = for_vector()
                                for h in range(HALF_H):
                                    out = ps[:, h * RK:(h + 1) * RK]
                                    ch = slice(o + (h // 2) * P, o + (h // 2 + 1) * P)
                                    mm(out, U(1)[:, ch], sa[:, h * RK:(h + 1) * RK], True, False)
                                    last = mm(out, U(4)[:, ch], v[:, o + h * RK:o + (h + 1) * RK], False, True)
                                last.then_inc(psum_for_vector, 1)
                            if t == 1:
                                w.take(operand_written)
                                ps = for_scalar()
                                for pr in range(KD):
                                    last = nc.tensor.transpose(ps[0:RK, pr * P:(pr + 1) * P], stateT[:, pr, :], ident[:])
                                last.then_inc(psum_for_scalar, 1)
                        for hh in (range(2) if sample else ()):
                            o = hh * 512
                            b_ = halves[0]
                            turn_half(hh)
                            scalar_copies()
                            attention(b_)
                            w.take(operand_written)
                            level(b_)
                            scalar_copies()
                            ps = for_vector()
                            for h in range(HALF_H):
                                last = mm(ps[:, h * P:(h + 1) * P], hd(b_["z"], h), hd(b_["tt"], h))
                            last.then_inc(psum_for_vector, 1)
                            vector_copies()
                            for q in range(2):
                                w.take(s0_loaded, 64)
                                ps = for_scalar()
                                for b in range(4):
                                    src = hc[0:RK, b // 2, (b % 2) * 512:(b % 2) * 512 + 512]
                                    for pr in range(PAIRS):
                                        last = nc.tensor.transpose(ps[:, b * 256 + pr * RK:b * 256 + (pr + 1) * RK],
                                                                   src[:, pr * P:(pr + 1) * P], ident[0:RK, 0:RK])
                                last.then_inc(psum_for_scalar, 1)
                            scalar_copies()
                            s0 = U(14, 2).rearrange("p (b q v) -> p b q v", b=DEC_B, q=PAIRS)

                            def from_states(z):
                                for q in range(PAIRS):
                                    ps = for_vector()
                                    for e in range(2):
                                        last = mm(ps[:, e * 512:(e + 1) * 512].rearrange("p (b v) -> p b v", b=DEC_B),
                                                  hd(z, 2 * q + e), s0[:, :, q, :])
                                    last.then_inc(psum_for_vector, 1)

                            from_states(b_["atz"])
                            ps = for_vector()
                            for h in range(HALF_H):
                                last = mm(ps[:, h * RK:(h + 1) * RK], hd(b_["ak"], h), v[:, o + h * RK:o + (h + 1) * RK])
                            last.then_inc(psum_for_vector, 1)
                            from_states(b_["rtz"])
                            w.take(operand_written)
                            solve(b_)
                            scalar_copies()
                            sa = b_["rhs"][:, 512:1024]
                            ps = for_vector()
                            for h in range(HALF_H):
                                out = ps[:, h * RK:(h + 1) * RK]
                                mm(out, hd(b_["rb"], h), sa[:, h * RK:(h + 1) * RK], True, False)
                                last = mm(out, hd(b_["rk"], h), v[:, o + h * RK:o + (h + 1) * RK], False, True)
                            last.then_inc(psum_for_vector, 1)
                            for q in range(PAIRS):
                                w.take(operand_written)
                                ps = for_vector()
                                ch = slice(o + q * P, o + (q + 1) * P)
                                for e in range(2):
                                    out = ps[:, e * 512:(e + 1) * 512]
                                    mm(out, U(1)[:, ch], wx[:, 2 * (q % 2), e * 512:(e + 1) * 512], True, False)
                                    last = mm(out, U(4)[:, ch], wx[:, 2 * (q % 2) + 1, e * 512:(e + 1) * 512], False, True)
                                last.then_inc(psum_for_vector, 1)
                            w.take(operand_written)
                            for q in range(4):
                                ps = for_scalar()
                                for b in range(2):
                                    for pr in range(PAIRS):
                                        last = nc.tensor.transpose(ps[0:RK, b * 512 + pr * P:b * 512 + (pr + 1) * P],
                                                                   s0[:, 2 * q + b, pr, :], ident[:])
                                last.then_inc(psum_for_scalar, 1)
                        ps = for_vector()
                        for j in range(2):
                            last = mm(ps[:, j * 512:(j + 1) * 512], loraT[:, 2, t * P:(t + 1) * P], g2[:, j * 512:(j + 1) * 512])
                        last.then_inc(psum_for_vector, 1)
                        if not sample:
                            modulation()
                        w.take(operand_written)
                        turn(y, for_scalar()).then_inc(psum_for_scalar, 1)
                else:
                    scalar_copies()
                    for blk in range(2):
                        wt = weight()
                        for h in range(GH):
                            ps = for_scalar()
                            for k in range(KD):
                                last = mm(ps[:, 0:TOK], wt[:, k, h * P:(h + 1) * P], hT[:, k, :], k == 0, k == KD - 1)
                            last.then_inc(psum_for_scalar, 1)
                        pe.wait_ge(psum_for_scalar, nfa[0])
                        pe.sem_inc(weight_used, 1)
                    for blk in range(4):
                        wt = weight()
                        for t in range(NT):
                            rows_product(for_scalar(), t, wt).then_inc(psum_for_scalar, 1)
                        pe.wait_ge(psum_for_scalar, nfa[0])
                        pe.sem_inc(weight_used, 1)
                    wt = weight()
                    ps = for_scalar()
                    for k in range(KD):
                        last = mm(ps[0:16, 0:TOK], wt[:, k, 0:16], hT[:, k, :], k == 0, k == KD - 1)
                    last.then_inc(psum_for_scalar, 1)
                    pe.wait_ge(psum_for_scalar, nfa[0])
                    pe.sem_inc(weight_used, 1)
                    w.take(gla_small_loaded, 32)
                    scalar_copies()
                    for turn_ in GLA_TURNS:
                        sample = turn_[0] == SAMPLE
                        tiles = [(t, gla_sets[t % 2], slice(t * P, (t + 1) * P)) for t in turn_]
                        for t, b, tok in tiles:
                            mm(for_vector()[:, 0:512], alT[0:17, tok], wa2[0:17, :]).then_inc(psum_for_vector, 1)
                        for t, b, tok in tiles:
                            w.take(operand_written)
                            ps = for_scalar()
                            for h in range(GH):
                                last = mm(ps[:, h * P:(h + 1) * P], b["la"][:, h * P:(h + 1) * P], (le4 if sample else le)[:])
                            last.then_inc(psum_for_scalar, 1)
                        for t, b, tok in tiles:
                            ps = for_vector()
                            for h in range(GH):
                                last = mm(ps[:, h * P:(h + 1) * P], kT[:, h, tok], qT[:, h, tok])
                            last.then_inc(psum_for_vector, 1)
                        for k in (range(2) if sample else range(7)):
                            for t, b, tok in tiles:
                                w.take(operand_written)
                                ps = for_vector()
                                for h in range(GH):
                                    last = mm(ps[:, h * P:(h + 1) * P], b["ke"][:, h * P:(h + 1) * P], b["qe"][:, h * P:(h + 1) * P])
                                last.then_inc(psum_for_vector, 1)
                        for t, b, tok in tiles:
                            w.take(operand_written)
                            turn(b["ke"], for_scalar(), 4).then_inc(psum_for_scalar, 1)
                        scalar_copies()
                        for t, b, tok in tiles:
                            at, qe, kd = b["at"], b["qe"], b["kd"]
                            if sample:
                                for h in range(GH):
                                    w.take(operand_written)
                                    pe.wait_ge(gla_state_loaded[h % 2], 16 * (h // 2 + 1))
                                    s0 = gS0[h % 2].rearrange("p (b v) -> p b v", b=DEC_B)
                                    vv = gv[t][:, h * GV:(h + 1) * GV]
                                    out = for_vector()[:, 0:GV]
                                    mm(out, at[:, h * P:(h + 1) * P], vv, True, False)
                                    for i in range(DEC_B):
                                        last = mm(out, qem[:, i * P:(i + 1) * P], s0[:, i, :], False, i == DEC_B - 1)
                                    last.then_inc(psum_for_vector, 1)
                                    for q in range(2):
                                        ps = for_vector()
                                        for i in range(4):
                                            last = mm(ps[:, i * GV:(i + 1) * GV], kdm[:, (4 * q + i) * P:(4 * q + i + 1) * P], vv)
                                        last.then_inc(psum_for_vector, 1)
                            else:
                                w.take(operand_written)
                                ps = for_vector()
                                for h in range(GH):
                                    out = ps[:, h * GV:(h + 1) * GV]
                                    vv = gv[t][:, h * GV:(h + 1) * GV]
                                    mm(out, at[:, h * P:(h + 1) * P], vv, True, False)
                                    last = mm(out, qe[:, h * P:(h + 1) * P], gS[:, h * GV:(h + 1) * GV], False, True)
                                last.then_inc(psum_for_vector, 1)
                                ps = for_vector()
                                for h in range(GH):
                                    last = mm(ps[:, h * GV:(h + 1) * GV], kd[:, h * P:(h + 1) * P], gv[t][:, h * GV:(h + 1) * GV])
                                last.then_inc(psum_for_vector, 1)
                        for t, b, tok in tiles:
                            w.take(operand_written)
                            turn(b["go"], for_scalar()).then_inc(psum_for_scalar, 1)
                project_out()
                h_turned(0)
                w.take(keys_loaded, 16)
                for i in range(2):
                    ps = for_scalar()
                    for k in range(8):
                        last = nc.tensor.transpose(ps[:, k * P:(k + 1) * P], sk[:, 8 * i + k, :], ident[:])
                    last.then_inc(psum_for_scalar, 1)
                scalar_copies()
                def query(ps, at_, wt, i, tok):
                    for k in range(KD):
                        last = mm(ps[:, at_:at_ + tok.stop - tok.start], wt[:, k, i * P:(i + 1) * P], hT[:, k, tok], k == 0, k == KD - 1)
                    return last

                for blk in range(5):
                    if blk < 4:
                        wt = weight()
                        ps = for_scalar()
                        for i in range(4):
                            last = query(ps, i * P, wt, i, slice(0, P))
                        last.then_inc(psum_for_scalar, 1)
                    if blk:
                        pe.wait_ge(scalar_drained, nfa[0] - (1 if blk < 4 else 0))
                        ps = for_vector()
                        for i in range(4):
                            last = mm(ps[:, i * P:(i + 1) * P], qa[(blk - 1) % 2][:, i * P:(i + 1) * P], skT[:, 4 * (blk - 1) + i, :])
                        last.then_inc(psum_for_vector, 1)
                    if blk < 2:
                        pe.wait_ge(psum_for_scalar, nfa[0])
                        pe.sem_inc(weight_used, 1)
                h_turned(1, 2)
                scalar_copies()
                held = [wring[:, (nw[0] - 2 + i) % WBUF] for i in range(2)]
                for n in range(HP + 1):
                    if n < HP:
                        if n % 4 == 0:
                            wt = held[n // 4] if n < 8 else weight()
                        ps = for_scalar()
                        query(ps, 0, wt, n % 4, slice(P, TOK)).then_inc(psum_for_scalar, 1)
                    if n:
                        pe.wait_ge(scalar_drained, nfa[0] - (1 if n < HP else 0))
                        hp = 4 * SCORE_BLOCKS[(n - 1) // 4] + (n - 1) % 4
                        ps = for_vector()
                        for i in range(2):
                            last = mm(ps[:, i * P:(i + 1) * P], qb[(n - 1) % 2][:, i * P:(i + 1) * P], skT[:, hp, :])
                        last.then_inc(psum_for_vector, 1)
                    if n < HP and n % 4 == 3:
                        pe.wait_ge(psum_for_scalar, nfa[0])
                        pe.sem_inc(weight_used, 1)
                for n, u, v, choice in SEGMENTS:
                    both = bool(u and v)
                    per = len(groups_of(1, both)) * GRP
                    if v:
                        t, first = v
                        if first == 0:
                            ps = for_vector()
                            for j in range(2):
                                mm(ps[:, j * 512:(j + 1) * 512], zeros[:], hc[:, t, j * 512:(j + 1) * 512], True, False)
                        with pe.Fori(0, n // per) as i:
                            for k, g in enumerate(groups_of(1, both)):
                                pe.wait_ge(diag_ready, i * per + (ndiag[0] + (k + 1) * GRP))
                                pe.wait_ge(rows_landed[g], i * (16 * GRP) + (rounds[g] + 1) * 16 * GRP)
                                for s in range(g * GRP, (g + 1) * GRP):
                                    for j in range(2):
                                        last = mm(ps[:, j * 512:(j + 1) * 512], diag[:, s, :], ring[:, s, j * 512:(j + 1) * 512], False, False)
                                last.then_inc(rows_used[g], GRP)
                        ndiag[0] += n
                        if first + n == experts_of(t):
                            for j in range(2):
                                last = mm(ps[:, j * 512:(j + 1) * 512], zeros[:], hc[:, t, j * 512:(j + 1) * 512], False, True)
                            last.then_inc(psum_for_vector, 1)
                    for g in range(NGRP):
                        rounds[g] += n // per
                if li == 0:
                    h_turned(0, 1)
                    h_turned(SAMPLE)


_INS = ["x_prompt", "x_sample", "state_rwkv_S", "state_rwkv_shift", "state_gla_S", "c_prompt", "c_sample",
        "ada_w", "ada_b", "norm1_g", "norm2_g", "final_g",
        "rw_mu", "rw_w_rkv", "rw_w0", "rw_w1", "rw_w2", "rw_a0", "rw_a1", "rw_a2", "rw_g1", "rw_g2",
        "rw_kk", "rw_ka", "rw_rk", "rw_lnx_w", "rw_lnx_b", "rw_wo",
        "gla_w_in", "gla_wa2", "gla_ba", "gla_gnorm", "gla_wo",
        "peer_wq", "peer_subkeys", "peer_u", "peer_v"]
_OUTS = [(1, 256, 1024), (8, 4, 1024), (1, 1, 16, 64, 64), (1, 1, 1024), (1, 1, 4, 128, 256),
         (1, 8, 16, 64, 64), (1, 8, 1024), (1, 8, 4, 128, 256)]


def kernel(**inputs):
    import numpy as np
    import concourse.bacc as bacc
    from concourse.bass_utils import run_bass_kernel_spmd

    nc = bacc.Bacc("TRN2", target_bir_lowering=False, num_devices=1)
    arrays, aps = {}, {}
    for name in _INS:
        v = np.ascontiguousarray(inputs[name])
        arrays["in_" + name] = v
        aps[name] = nc.dram_tensor("in_" + name, v.shape, mybir.dt.from_np(v.dtype), kind="ExternalInput").ap()
    outs = [nc.dram_tensor(f"out_{i}", s, F32, kind="ExternalOutput").ap() for i, s in enumerate(_OUTS)]
    program(nc, aps, outs)
    r = run_bass_kernel_spmd(nc, [arrays], core_ids=[0])
    return tuple(r.results[0][f"out_{i}"] for i in range(len(_OUTS)))
```
